# Optimizing a Trainium2 kernel written in Bass

```python
import jax
import jax.numpy as jnp
from jax import lax
import numpy as np

D_MODEL = 1024
BATCH = 1
SEQ = 512
DEPTH = 2
DEC_BATCH = 8
DEC_SEQ = 4
PAST_LEN = 1024
PAGE_SIZE = 128

HEAD_DIM = 64
A_HEADS = D_MODEL // 128
A_WIDTH = A_HEADS * HEAD_DIM
A_LORA_W = 64
A_LORA_A = 64
A_SHIFT = 3 * A_WIDTH + A_LORA_W + A_LORA_A
A_GN_EPS = 64e-5
B_HEADS = D_MODEL // 128
B_WIDTH = B_HEADS * HEAD_DIM
B_BIAS_INIT = -6.0
C_WINDOWS = (128, 512, 2048)
C_DILATIONS = (1, 4, 16)
C_GROUPS = 3
C_HEADS = (3 * D_MODEL) // 512
C_WIDTH = C_HEADS * HEAD_DIM
C_QKV = C_GROUPS * C_WIDTH
ROPE_THETA = 10000.0
NORM_EPS = 1e-6
Q_BLOCK = 128
IN_SIZES = (A_SHIFT, A_WIDTH, 3 * B_WIDTH, B_WIDTH, 3 * C_QKV, C_WIDTH, 3 * D_MODEL)
D_IN = A_SHIFT + A_WIDTH + 3 * B_WIDTH + B_WIDTH + 3 * C_QKV + C_WIDTH + 3 * D_MODEL

kernel_name = 'hybrid_rwkv7_stickbreak_dilated_step'

def _split(x, sizes):
    cuts = [int(c) for c in np.cumsum(sizes)[:-1]]
    return jnp.split(x, cuts, axis=-1)

def rms_norm(x, w):
    xf = x.astype(jnp.float32)
    return xf * lax.rsqrt(jnp.mean(xf * xf, axis=-1, keepdims=True) + NORM_EPS) * w.astype(jnp.float32)

def rope(x, pos):
    half = HEAD_DIM // 2
    inv = 1.0 / (ROPE_THETA ** (jnp.arange(0, HEAD_DIM, 2, dtype=jnp.float32) / HEAD_DIM))
    ang = pos.astype(jnp.float32)[:, None] * inv[None, :]
    cos = jnp.cos(ang)[None, :, None, None, :]
    sin = jnp.sin(ang)[None, :, None, None, :]
    x1, x2 = x[..., :half], x[..., half:]
    return jnp.concatenate([x1 * cos - x2 * sin, x2 * cos + x1 * sin], axis=-1)

def rwkv7_mix(pa, prev, s0, mu, w0, w2, a0, a2, k_k, k_a, r_k, gn_w, gn_b):
    b, t_len, _ = pa.shape
    shifted = jnp.concatenate([prev[:, None, :].astype(pa.dtype), pa[:, :-1]], axis=1)
    xs = pa + (shifted - pa) * mu
    r, k, v, wd, ad = _split(xs, (A_WIDTH, A_WIDTH, A_WIDTH, A_LORA_W, A_LORA_A))
    w_log = -jax.nn.softplus(-(w0 + jnp.tanh(wd) @ w2)) - 0.5
    decay = jnp.exp(-jnp.exp(w_log))
    a = jax.nn.sigmoid(a0 + ad @ a2)
    heads = lambda u: u.reshape(b, t_len, A_HEADS, HEAD_DIM).astype(jnp.float32)
    kk = heads(k * k_k)
    kk = kk / jnp.maximum(jnp.sqrt(jnp.sum(kk * kk, axis=-1, keepdims=True)), 1e-12)
    k = k * (1.0 + (a - 1.0) * k_a)
    r, k, v, decay, a = heads(r), heads(k), heads(v), heads(decay), heads(a)

    def step(s, inp):
        r_t, k_t, v_t, w_t, kk_t, a_t = inp
        s = (s * w_t[:, :, None, :]
             - jnp.einsum('bhij,bhj->bhi', s, kk_t)[..., None] * (kk_t * a_t)[:, :, None, :]
             + v_t[..., None] * k_t[:, :, None, :])
        return s, jnp.einsum('bhij,bhj->bhi', s, r_t)

    seq_first = lambda u: jnp.moveaxis(u, 1, 0)
    s_last, y = lax.scan(step, s0.astype(jnp.float32),
                         (seq_first(r), seq_first(k), seq_first(v), seq_first(decay), seq_first(kk), seq_first(a)))
    y = jnp.moveaxis(y, 0, 1)
    mean = jnp.mean(y, axis=-1, keepdims=True)
    var = jnp.mean(jnp.square(y - mean), axis=-1, keepdims=True)
    yn = (y - mean) * lax.rsqrt(var + A_GN_EPS)
    yn = yn * gn_w.reshape(A_HEADS, HEAD_DIM) + gn_b.reshape(A_HEADS, HEAD_DIM)
    bonus = jnp.sum(r * k * r_k, axis=-1, keepdims=True) * v
    return (yn + bonus).reshape(b, t_len, A_WIDTH), s_last, pa[:, -1]

def sweep_queries(block_fn, q):
    b, nq = q.shape[:2]
    blk = min(Q_BLOCK, nq)
    nb = nq // blk
    qb = jnp.moveaxis(q.reshape((b, nb, blk) + q.shape[2:]), 1, 0)
    starts = blk * jnp.arange(nb)
    out = lax.map(lambda a: block_fn(a[0], a[1] + jnp.arange(blk)), (qb, starts))
    return jnp.moveaxis(out, 0, 1).reshape((b, nq) + out.shape[3:])

def _sb_block(q, k_all, v_all, q_idx, bias):
    z = (jnp.einsum('bqhd,bkhd->bhqk', q, k_all).astype(jnp.float32) * (HEAD_DIM ** -0.5)
         + bias.astype(jnp.float32)[None, :, None, None])
    k_idx = jnp.arange(k_all.shape[1])
    before = k_idx[None, :] < q_idx[:, None]
    log_beta = jax.nn.log_sigmoid(z)
    log_rest = jnp.where(before, log_beta - z, 0.0)
    later = lax.cumsum(log_rest, axis=3, reverse=True) - log_rest
    w = jnp.where(before, jnp.exp(log_beta + later), 0.0)
    return jnp.einsum('bhqk,bkhd->bqhd', w, v_all.astype(jnp.float32))

def _dilated_block(q, kvs, local_idx, n_new):
    outs, lses = [], []
    for g in range(C_GROUPS):
        k_g, v_g = kvs[g]
        d = C_DILATIONS[g]
        q_idx = (k_g.shape[1] - n_new) + local_idx
        idx = q_idx[:, None] - d * jnp.arange(C_WINDOWS[g] // d + 1)[None, :]
        valid = idx >= 0
        idx = jnp.maximum(idx, 0)
        kg = jnp.take(k_g, idx, axis=1)
        vg = jnp.take(v_g, idx, axis=1)
        s = jnp.einsum('bqhd,bqjhd->bhqj', q[:, :, g], kg).astype(jnp.float32) * (HEAD_DIM ** -0.5)
        s = jnp.where(valid[None, None], s, -jnp.inf)
        lse = jax.nn.logsumexp(s, axis=-1, keepdims=True)
        outs.append(jnp.einsum('bhqj,bqjhd->bqhd', jnp.exp(s - lse), vg.astype(jnp.float32)))
        lses.append(lse[..., 0])
    mix = jax.nn.softmax(jnp.stack(lses, axis=0), axis=0)
    mix = jnp.swapaxes(mix, 2, 3)[..., None]
    return jnp.sum(jnp.stack(outs, axis=0) * mix, axis=0)

def trunk_layer(x, pos, a_s0, a_prev, b_past_k, b_past_v, c_bufs, lp):
    b, t_len, _ = x.shape
    xn = rms_norm(x, lp['norm_w'])
    pa, za, b_qkv, zb, c_qkv, zc, m = _split(xn @ lp['w_in'], IN_SIZES)

    ya, a_s, a_last = rwkv7_mix(pa, a_prev, a_s0, lp['a_mu'], lp['a_w0'], lp['a_w2'], lp['a_a0'], lp['a_a2'],
                                lp['a_kk'], lp['a_ka'], lp['a_rk'], lp['a_gn_w'], lp['a_gn_b'])
    ya = ya * jax.nn.silu(za)

    bq, bk, bv = [u.reshape(b, t_len, B_HEADS, HEAD_DIM) for u in jnp.split(b_qkv, 3, axis=-1)]
    if b_past_k is None:
        bk_all, bv_all = bk, bv
    else:
        bk_all = jnp.concatenate([b_past_k.astype(bk.dtype), bk], axis=1)
        bv_all = jnp.concatenate([b_past_v.astype(bv.dtype), bv], axis=1)
    off_b = bk_all.shape[1] - t_len
    b_bias = lp['b_bias']
    yb = sweep_queries(lambda qb, li: _sb_block(qb, bk_all, bv_all, off_b + li, b_bias), bq)
    yb = yb.reshape(b, t_len, B_WIDTH) * jax.nn.silu(zb)

    cq, ck, cv = [u.reshape(b, t_len, C_GROUPS, C_HEADS, HEAD_DIM) for u in jnp.split(c_qkv, 3, axis=-1)]
    cq = rope(rms_norm(cq, lp['c_qnorm']), pos)
    ck = rope(rms_norm(ck, lp['c_knorm']), pos)
    kvs, new_c = [], []
    for g in range(C_GROUPS):
        k_g, v_g = ck[:, :, g], cv[:, :, g]
        if c_bufs is not None:
            buf = c_bufs[g].astype(k_g.dtype)
            k_g = jnp.concatenate([buf[:, :, 0], k_g], axis=1)
            v_g = jnp.concatenate([buf[:, :, 1], v_g], axis=1)
        kvs.append((k_g, v_g))
        keep = min(C_WINDOWS[g], k_g.shape[1])
        new_c.append(jnp.stack([k_g[:, -keep:], v_g[:, -keep:]], axis=2))
    yc = sweep_queries(lambda qb, li: _dilated_block(qb, kvs, li, t_len), cq)
    yc = yc.reshape(b, t_len, C_WIDTH) * jax.nn.silu(zc)

    gm = jax.nn.sigmoid(m).reshape(b, t_len, 3, D_MODEL)
    merged = (gm[:, :, 0] * (ya @ lp['w_br_a']) + gm[:, :, 1] * (yb @ lp['w_br_b'])
              + gm[:, :, 2] * (yc @ lp['w_br_c']))
    x = x + (merged @ lp['w_out']).astype(x.dtype)
    return x, a_s, a_last, bk, bv, new_c

def setup_inputs(seed: int = 0) -> dict:
    key = jax.random.key(seed)
    ks = jax.random.split(key, 40)
    nrm = lambda k, shape, scale: scale * jax.random.normal(k, shape, jnp.float32)
    n_pages = PAST_LEN // PAGE_SIZE
    n_pool = (DEC_BATCH * n_pages * 5) // 4
    perm = jax.random.permutation(ks[0], n_pool)[:DEC_BATCH * n_pages]
    wb = [min(w, PAST_LEN) for w in C_WINDOWS]
    return {
        'x_prompt': nrm(ks[1], (BATCH, SEQ, D_MODEL), 1.0),
        'x_sample': nrm(ks[2], (DEC_BATCH, DEC_SEQ, D_MODEL), 1.0),
        'state_a_wkv': nrm(ks[3], (DEPTH, DEC_BATCH, A_HEADS, HEAD_DIM, HEAD_DIM), 0.5),
        'state_a_shift': nrm(ks[4], (DEPTH, DEC_BATCH, A_SHIFT), 1.0),
        'cache_b_k': nrm(ks[5], (DEPTH, n_pool, PAGE_SIZE, B_HEADS, HEAD_DIM), 1.0),
        'cache_b_v': nrm(ks[6], (DEPTH, n_pool, PAGE_SIZE, B_HEADS, HEAD_DIM), 1.0),
        'cache_c1_kv': nrm(ks[7], (DEPTH, DEC_BATCH, wb[0], 2, C_HEADS, HEAD_DIM), 1.0),
        'cache_c2_kv': nrm(ks[8], (DEPTH, DEC_BATCH, wb[1], 2, C_HEADS, HEAD_DIM), 1.0),
        'cache_c3_kv': nrm(ks[9], (DEPTH, DEC_BATCH, wb[2], 2, C_HEADS, HEAD_DIM), 1.0),
        'page_table': perm.reshape(DEC_BATCH, n_pages).astype(jnp.int32),
        'norm_w': 1.0 + nrm(ks[10], (DEPTH, D_MODEL), 0.02),
        'w_in': nrm(ks[11], (DEPTH, D_MODEL, D_IN), D_MODEL ** -0.5),
        'a_mu': jax.random.uniform(ks[12], (DEPTH, A_SHIFT), jnp.float32),
        'a_w0': -0.5 + nrm(ks[13], (DEPTH, A_WIDTH), 0.3),
        'a_w2': nrm(ks[14], (DEPTH, A_LORA_W, A_WIDTH), 0.5 * A_LORA_W ** -0.5),
        'a_a0': nrm(ks[15], (DEPTH, A_WIDTH), 0.1),
        'a_a2': nrm(ks[16], (DEPTH, A_LORA_A, A_WIDTH), A_LORA_A ** -0.5),
        'a_kk': 0.85 + nrm(ks[17], (DEPTH, A_WIDTH), 0.05),
        'a_ka': 1.0 + nrm(ks[18], (DEPTH, A_WIDTH), 0.05),
        'a_rk': nrm(ks[19], (DEPTH, A_HEADS, HEAD_DIM), 0.1),
        'a_gn_w': 1.0 + nrm(ks[20], (DEPTH, A_WIDTH), 0.02),
        'a_gn_b': nrm(ks[21], (DEPTH, A_WIDTH), 0.02),
        'b_bias': B_BIAS_INIT + nrm(ks[28], (DEPTH, B_HEADS), 0.1),
        'c_qnorm': 1.0 + nrm(ks[22], (DEPTH, HEAD_DIM), 0.02),
        'c_knorm': 1.0 + nrm(ks[23], (DEPTH, HEAD_DIM), 0.02),
        'w_br_a': nrm(ks[24], (DEPTH, A_WIDTH, D_MODEL), A_WIDTH ** -0.5),
        'w_br_b': nrm(ks[25], (DEPTH, B_WIDTH, D_MODEL), B_WIDTH ** -0.5),
        'w_br_c': nrm(ks[26], (DEPTH, C_WIDTH, D_MODEL), C_WIDTH ** -0.5),
        'w_out': nrm(ks[27], (DEPTH, D_MODEL, D_MODEL), D_MODEL ** -0.5),
    }

def reference(x_prompt, x_sample, state_a_wkv, state_a_shift, cache_b_k, cache_b_v, cache_c1_kv, cache_c2_kv,
              cache_c3_kv, page_table, norm_w, w_in, a_mu, a_w0, a_w2, a_a0, a_a2, a_kk, a_ka, a_rk, a_gn_w,
              a_gn_b, b_bias, c_qnorm, c_knorm, w_br_a, w_br_b, w_br_c, w_out):
    bp, tp = x_prompt.shape[:2]
    bs, ts = x_sample.shape[:2]
    past = page_table.shape[1] * PAGE_SIZE
    pos_p = jnp.arange(tp)
    pos_s = past + jnp.arange(ts)
    c_caches = (cache_c1_kv, cache_c2_kv, cache_c3_kv)
    yp, ys = x_prompt, x_sample
    wkv_p, wkv_s, sh_p, sh_s, bk_p, bv_p, bk_s, bv_s, c_p, c_s = [], [], [], [], [], [], [], [], [], []
    for l in range(DEPTH):
        lp = {'norm_w': norm_w[l], 'w_in': w_in[l], 'a_mu': a_mu[l], 'a_w0': a_w0[l], 'a_w2': a_w2[l],
              'a_a0': a_a0[l], 'a_a2': a_a2[l], 'a_kk': a_kk[l], 'a_ka': a_ka[l], 'a_rk': a_rk[l],
              'a_gn_w': a_gn_w[l], 'a_gn_b': a_gn_b[l], 'b_bias': b_bias[l], 'c_qnorm': c_qnorm[l],
              'c_knorm': c_knorm[l], 'w_br_a': w_br_a[l], 'w_br_b': w_br_b[l], 'w_br_c': w_br_c[l],
              'w_out': w_out[l]}
        yp, s1, s2, s3, s4, s5 = trunk_layer(
            yp, pos_p, jnp.zeros((bp, A_HEADS, HEAD_DIM, HEAD_DIM), jnp.float32),
            jnp.zeros((bp, A_SHIFT), jnp.float32), None, None, None, lp)
        wkv_p.append(s1); sh_p.append(s2); bk_p.append(s3); bv_p.append(s4); c_p.append(s5)
        past_k = cache_b_k[l][page_table].reshape(bs, past, B_HEADS, HEAD_DIM)
        past_v = cache_b_v[l][page_table].reshape(bs, past, B_HEADS, HEAD_DIM)
        ys, s1, s2, s3, s4, s5 = trunk_layer(
            ys, pos_s, state_a_wkv[l], state_a_shift[l], past_k, past_v, [c[l] for c in c_caches], lp)
        wkv_s.append(s1); sh_s.append(s2); bk_s.append(s3); bv_s.append(s4); c_s.append(s5)
    stk = lambda u: jnp.stack(u, axis=0)
    return (yp, ys, stk(wkv_p), stk(wkv_s), stk(sh_p), stk(sh_s), stk(bk_p), stk(bv_p), stk(bk_s), stk(bv_s),
            stk([c[0] for c in c_p]), stk([c[0] for c in c_s]), stk([c[1] for c in c_p]), stk([c[1] for c in c_s]),
            stk([c[2] for c in c_p]), stk([c[2] for c in c_s]))


_drawn_inputs = setup_inputs


def setup_inputs(seed=0):
    import zlib

    import numpy as np

    out = dict(_drawn_inputs(seed))
    spreads = {}
    factors = {'a_kk': 4.555,
     'a_gn_w': 6.288,
     'a_gn_b': 5.95,
     'b_bias': 8.0,
     'c_qnorm': 8.0,
     'c_knorm': 3.661}
    for name, (base, spread) in spreads.items():
        noise = np.random.default_rng([zlib.crc32(name.encode()), seed]).standard_normal(out[name].shape)
        drawn = base * np.exp(spread * noise) if base else spread * noise
        out[name] = jnp.asarray(drawn.astype(out[name].dtype))
    for name, factor in factors.items():
        out[name] = (out[name] * factor).astype(out[name].dtype)
    return out
```

```python
from contextlib import ExitStack

import numpy as np

import concourse.bass as bass
from concourse import mybir

F32 = mybir.dt.float32
I32 = mybir.dt.int32
ALU = mybir.AluOpType
ACT = mybir.ActivationFunctionType
AX_X = mybir.AxisListType.X

P = 128
D_MODEL, SEQ, DEPTH = 1024, 512, 2
DEC_BATCH, DEC_SEQ, PAST_LEN, PAGE = 8, 4, 1024, 128
HD = 64
A_HEADS, B_HEADS, C_HEADS, C_GROUPS = 8, 8, 6, 3
A_WIDTH, B_WIDTH, C_WIDTH = 512, 512, 384
C_QKV = C_GROUPS * C_WIDTH
A_SHIFT = 3 * A_WIDTH + 128
WINDOWS, DILATIONS = (128, 512, 2048), (1, 4, 16)
NORM_EPS, A_GN_EPS = 1e-6, 64e-5
QK_SCALE = HD ** -0.5
NDEC = DEC_BATCH * DEC_SEQ
NT = SEQ + NDEC
HALF = NT // 2
KT = D_MODEL // P
TT = SEQ // P
TOK_TILES = [(i * P, P) for i in range(TT)] + [(SEQ, NDEC)]
N_PAGES = PAST_LEN // PAGE
CHUNK = 64
NCHUNK = SEQ // CHUNK
DECAY_RATE = float(np.exp(-0.5))
NEG = -1.0e30

_SIZES = (A_SHIFT, A_WIDTH, 3 * B_WIDTH, B_WIDTH, 3 * C_QKV, C_WIDTH, 3 * D_MODEL)
PA0, ZA0, BQ0, ZB0, CQ0, ZC0, M0 = [sum(_SIZES[:i]) for i in range(7)]
BK0, BV0 = BQ0 + B_WIDTH, BQ0 + 2 * B_WIDTH
CK0, CV0 = CQ0 + C_QKV, CQ0 + 2 * C_QKV

PRM = {}
_row = 0
for _name, _n in (("norm_w", 8), ("a_mu", 13), ("a_w0", 4), ("a_a0", 4), ("a_kk", 4), ("a_ka", 4), ("a_rk", 4),
                  ("a_gn_w", 4), ("a_gn_b", 4)):
    PRM[_name] = (_row, _row + _n)
    _row += _n
N_PRM = _row

CW = 256
RING = 4


def cut(source, col0, width, ktiles=KT):
    return [(source, col0 + c, min(CW, width - c), ktiles) for c in range(0, width, CW)]


PLAN = {}
CHUNKS = []


def plan(stage, chunks):
    PLAN[stage] = (len(CHUNKS), len(CHUNKS) + len(chunks))
    CHUNKS.extend(chunks)


plan("norm", [])
plan("proj_a", cut("w_in", PA0, A_SHIFT))
plan("proj_b", cut("w_in", BQ0, 3 * B_WIDTH))
for _g in range(C_GROUPS):
    plan(f"proj_c{_g}", cut("w_in", CQ0 + _g * C_WIDTH, C_WIDTH) + cut("w_in", CK0 + _g * C_WIDTH, C_WIDTH)
         + cut("w_in", CV0 + _g * C_WIDTH, C_WIDTH))
plan("gate", cut("w_in", ZA0, A_WIDTH) + cut("w_in", ZB0, B_WIDTH) + cut("w_in", ZC0, C_WIDTH))
_out = []
for _j in range(D_MODEL // CW):
    for _i, (_w, _k) in enumerate((("w_br_a", 4), ("w_br_b", 4), ("w_br_c", 3))):
        _out += [("w_in", M0 + _i * D_MODEL + _j * CW, CW, KT), (_w, _j * CW, CW, _k)]
plan("merge", _out)
plan("out", cut("w_out", 0, D_MODEL))


def chunk_units(source, c0, width):
    token_major = source == "w_out" or (source == "w_in" and (BV0 <= c0 < ZB0 or CQ0 <= c0 < ZC0))
    return len(TOK_TILES) if token_major else width // P


UNITS_AFTER = [int(x) for x in np.cumsum([chunk_units(s, c0, w) for s, c0, w, _ in CHUNKS])]


def host_constants():
    t = np.arange(P)
    same = (t[:, None] // CHUNK) == (t[None, :] // CHUNK)
    c = {}
    c["ident"] = np.eye(P)
    c["bones"] = (t[:, None] // HD == t[None, :] // HD)
    c["before"] = same & (t[:, None] < t[None, :])
    c["upto"] = same & (t[:, None] <= t[None, :])
    lv = []
    for b in (1, 2, 4, 8, 16, 32):
        lv.append((t[:, None] // (2 * b) == t[None, :] // (2 * b)) & (t[:, None] // b % 2 == 0) & (t[None, :] // b % 2 == 1))
    c["levels"] = np.stack(lv, 1).reshape(P, -1)
    c["level1"] = lv[0].T
    q = np.arange(NDEC)
    sameb = (q[:, None] // DEC_SEQ) == (q[None, :] // DEC_SEQ)
    pad = lambda m: np.concatenate([m, np.zeros((P - m.shape[0],) + m.shape[1:])])
    c["before4"] = pad(sameb & (q[:, None] < q[None, :]))
    c["upto4"] = pad(sameb & (q[:, None] <= q[None, :]))
    c["rowb"] = pad(q[:, None] // DEC_SEQ == np.arange(DEC_BATCH)[None, :])
    reset = np.ones(NT)
    reset[0:SEQ:CHUNK] = 0
    reset[SEQ::DEC_SEQ] = 0
    c["reset"] = np.broadcast_to(reset, (P, NT))
    colb = np.zeros((DEC_BATCH, NDEC))
    for b in range(DEC_BATCH):
        colb[b, b * DEC_SEQ:(b + 1) * DEC_SEQ] = 1
    c["colb"] = np.broadcast_to(colb.reshape(-1), (P, DEC_BATCH * NDEC))
    c["tri"] = -(t[:, None] >= t[None, :]).astype(np.float32)
    c["allneg"] = -np.ones((P, P))
    r = np.arange(P)
    c["rowhead"] = (r[:, None] % 32) // DEC_SEQ == np.arange(8)[None, :]
    c["rowtoken"] = (r[:, None] // 32 * DEC_SEQ + r[:, None] % DEC_SEQ) == np.arange(4 * DEC_SEQ)[None, :]
    seen = [(r[:, None] // 32 + 4 * half == q[None, :] // DEC_SEQ) & (q[None, :] % DEC_SEQ < r[:, None] % DEC_SEQ) for half in range(2)]
    c["bnew"] = np.concatenate(seen, 1)
    c["bnewneg"] = np.where(c["bnew"], 0.0, NEG)
    dist = t[:, None] - t[None, :]
    neg = lambda ok: np.where(ok, 0.0, NEG)
    g = [[neg(dist % d == 0)] * 3 + [neg((dist % d == 0) & (dist >= 0))] for d in (4, 16)]
    c["cmask"] = np.concatenate(g[0] + g[1] + [neg(dist <= 0), neg(dist >= 0)], 1)
    r = np.arange(P) % 32
    qt = r % DEC_SEQ
    m1 = neg(np.arange(P)[None, :] >= qt[:, None])
    m2 = neg(np.repeat(np.arange(4), 128)[None, :] == qt[:, None])
    m3 = neg(np.repeat(np.arange(4), 64)[None, :] == qt[:, None])
    c["dmask"] = np.concatenate([m1, m3], 1)
    c["dmask2"] = m2
    new = []
    for half in range(2):
        b = half * 4 + np.arange(P) // 32
        for g_ in range(3):
            own = b[:, None] == q[None, :] // DEC_SEQ
            s = q[None, :] % DEC_SEQ
            new.append(neg(own & ((s <= qt[:, None]) if g_ == 0 else (s == qt[:, None]))))
    c["dnew"] = np.concatenate(new, 1)
    inv = (1.0 / (np.float32(10000.0) ** (np.arange(0, HD, 2, dtype=np.float32) / np.float32(HD)))).astype(np.float32)
    pos = np.zeros((5, P), np.float32)
    pos[:4] = np.arange(SEQ).reshape(4, P)
    pos[4, :NDEC] = PAST_LEN + np.arange(NDEC) % DEC_SEQ
    ang = (pos[:, :, None] * inv).astype(np.float32).transpose(1, 0, 2)
    cos, sin = np.cos(ang.astype(np.float64)), np.sin(ang.astype(np.float64))
    c["rot_same"] = np.concatenate([cos, cos], -1).reshape(P, -1)
    c["rot_swap"] = np.concatenate([-sin, sin], -1).reshape(P, -1)
    return {k: np.ascontiguousarray(v, dtype=np.float32) for k, v in c.items()}


CONST_W = {k: v.shape[1] for k, v in host_constants().items()}


class Chain:

    def __init__(self, sem):
        self.sem, self.n = sem, 0

    def __call__(self, eng, ins):
        self.n += 1
        ins.then_inc(self.sem, 1)
        eng.wait_ge(self.sem, self.n)


class Shared:
    pass


def build(nc, I, O):
    ctx = ExitStack()
    with ctx:
        uid = [0]

        def sb(name, shape, dt=F32, c=ctx):
            uid[0] += 1
            return c.enter_context(nc.sbuf_tensor(f"{name}_{uid[0]}", shape, dt))

        scopes = [(ctx, [])]

        def sem(name):
            scope, sems = scopes[-1]
            s = scope.enter_context(nc.semaphore(name))
            sems.append(s)
            return s

        def clear(sems):
            nc.all_engine_barrier()
            nums = sorted(s.num for s in sems)
            while nums:
                n = 1
                while n < len(nums) and nums[n] == nums[0] + n:
                    n += 1
                nc.sync.sem_clear(range(nums[0], nums[0] + n))
                nums = nums[n:]
            nc.all_engine_barrier()

        K = {k: sb(k, [P, w]) for k, w in CONST_W.items()}
        epsn = sb("epsn", [P, 2])
        xnT = sb("xnT", [P, KT, NT])
        ring = sb("ring", [P, RING, KT, CW])
        ya = sb("ya", [P, 4, NT])
        prm = sb("prm", [P, N_PRM])
        bias_b = sb("bias_b", [P, B_HEADS])
        ps = ctx.enter_context(nc.psum_tensor("ps", [P, 8, 512], F32))
        ident = K["ident"]

        const_in = ctx.enter_context(nc.semaphore("const_in"))
        weights_in = [sem(f"weights_in{i}") for i in range(RING)]
        products_done = sem("products_done")
        products_taken = [sem(f"products_taken{i}") for i in range(2)]
        out_stored = sem("out_stored")
        cD, cA, cG = Chain(sem("vector_step")), Chain(sem("scalar_step")), Chain(sem("gpsimd_step"))
        stores = [0]

        def store(eng, dst, src, stored=None):
            stores[0] += stored is None
            eng.dma_start(dst, src).then_inc(out_stored if stored is None else stored, 16)

        def stores_done(eng):
            eng.wait_ge(out_stored, 16 * stores[0])

        with nc.Block() as block:
            @block.sync
            def _(sp):
                for k in CONST_W:
                    sp.dma_start(K[k][:, :], I[k]).then_inc(const_in, 16)
                sp.dma_start(O["y_prompt"][0], I["x_prompt"][0]).then_inc(const_in, 16)
                sp.dma_start(O["y_sample"].rearrange("b t d -> (b t) d"),
                             I["x_sample"].rearrange("b t d -> (b t) d")).then_inc(const_in, 16)
                sp.wait_ge(const_in, 16 * (len(CONST_W) + 2))

        y_rows = [O["y_prompt"][0][i * P:(i + 1) * P, :] for i in range(TT)] + [O["y_sample"].rearrange("b t d -> (b t) d")]

        loop = ctx.enter_context(nc.Fori(0, DEPTH))
        l = loop
        L = {k: v[l] for k, v in I.items() if len(v.shape) > 1 and v.shape[0] == DEPTH and k not in CONST_W}
        W = {n: L[n].rearrange("(k p) n -> p k n", p=P) for n in ("w_in", "w_br_a", "w_br_b", "w_br_c", "w_out")}

        def load_chunks(sp, first, last):
            for n in range(first, min(last, len(CHUNKS))):
                source, c0, w, kts = CHUNKS[n]
                if n >= RING:
                    sp.wait_ge(products_done, UNITS_AFTER[n - RING])
                sp.dma_start(ring[:, n % RING, 0:kts, 0:w], W[source][:, :, c0:c0 + w]).then_inc(weights_in[n % RING], 16)

        def prefetch(sp, stage):
            a, b = PLAN[stage]
            load_chunks(sp, a + RING, b + RING)

        def weights(pe, n):
            pe.wait_ge(weights_in[n % RING], 16 * (n // RING + 1))
            return ring[:, n % RING]

        unit = {"pe": 0, "take": 0}

        def pair(u):
            return ps[:, 2 * (u % 2):2 * (u % 2) + 2]

        def unit_begin(pe):
            u = unit["pe"]
            unit["pe"] += 1
            if u >= 2:
                pe.wait_ge(products_taken[u % 2], u // 2)
            return pair(u)

        def unit_wait(eng):
            u = unit["take"]
            unit["take"] += 1
            eng.wait_ge(products_done, u + 1)
            return pair(u)

        def taken():
            return products_taken[(unit["take"] - 1) % 2]

        def wait_taken(eng, u):
            for v in (u - 1, u):
                eng.wait_ge(products_taken[v % 2], v // 2 + 1)

        def channel_products(pe, slot, w, kts, rhs):
            for c in range(w // P):
                o = unit_begin(pe)
                for half in range(2):
                    for k in range(kts):
                        last = pe.matmul(o[:, half, 0:HALF], slot[:, k, c * P:(c + 1) * P],
                                         rhs[:, k, half * HALF:(half + 1) * HALF], start=(k == 0), stop=(k == kts - 1))
                last.then_inc(products_done, 1)

        def token_products(pe, slot, w, lhs):
            for t0, m in TOK_TILES:
                o = unit_begin(pe)
                for k in range(KT):
                    last = pe.matmul(o[0:m, 0, 0:w], lhs[:, k, t0:t0 + m], slot[:, k, 0:w], start=(k == 0), stop=(k == KT - 1))
                last.then_inc(products_done, 1)

        copies_done = sem("copies_done")
        e = Shared()
        e.I, e.O, e.L, e.l, e.K = I, O, L, l, K
        e.sb, e.sem, e.ps, e.ident, e.xnT = sb, sem, ps, ident, xnT
        e.ya, e.prm, e.bias_b, e.y_rows, e.cD = ya, prm, bias_b, y_rows, cD
        e.cA, e.cG, e.store, e.stores, e.stores_done = cA, cG, store, stores, stores_done
        e.out_stored, e.copies_done, e.load_chunks, e.prefetch, e.weights = out_stored, copies_done, load_chunks, prefetch, weights
        e.unit, e.pair, e.unit_wait, e.taken, e.wait_taken = unit, pair, unit_wait, taken, wait_taken
        e.products_done, e.products_taken, e.channel_products, e.token_products = products_done, products_taken, channel_products, token_products
        for f in STAGES:
            with ExitStack() as c2:
                scopes.append((c2, []))
                f(nc, c2, e)
                clear(scopes.pop()[1])
        nc.sync.wait_ge(out_stored, 16 * stores[0])
        nc.sync.wait_ge(copies_done, 16 * 3 * DEC_BATCH)
        clear(scopes[0][1])


def stage_norm(nc, c, e):
    x = e.sb("x", [P, 5, D_MODEL], c=c)
    sq = e.sb("sq", [P, D_MODEL], c=c)
    ss = e.sb("ss", [P, 5], c=c)
    rows = e.sb("prm_rows", [N_PRM, P], c=c)
    x_in, prm_in, rstd_in, normed, turned, evacd, prm_t, cleared = [e.sem("n_" + s) for s in
        ("x_in", "prm_in", "sqrt", "normed", "turned", "evacd", "prm_t", "cleared")]
    with nc.Block() as block:
        @block.sync
        def _(sp):
            for i, (t0, m) in enumerate(TOK_TILES):
                if m < P:
                    sp.wait_ge(cleared, 1)
                sp.dma_start(x[0:m, i, :], e.y_rows[i]).then_inc(x_in, 16)
            for name, (a, b) in PRM.items():
                src = e.L[name]
                src = src.rearrange("h d -> (h d)") if len(src.shape) == 2 else src
                sp.dma_start(rows[a:b, :], src.rearrange("(r c) -> r c", c=P)).then_inc(prm_in, 16)
            sp.dma_start(e.bias_b[:, :], e.L["b_bias"].partition_broadcast(P)).then_inc(prm_in, 16)
            e.load_chunks(sp, 0, RING)

        @block.vector
        def _(v):
            v.memset(x[:, 4, :], 0.0).then_inc(cleared, 1)
            v.wait_ge(x_in, 16 * 5)
            for i in range(5):
                e.cD(v, v.tensor_tensor_reduce(sq[:, :], x[:, i, :], x[:, i, :], 1.0, 0.0, ALU.mult, ALU.add, ss[:, i:i + 1]))
            v.tensor_scalar(ss[:, :], ss[:, :], 1.0 / D_MODEL, NORM_EPS, ALU.mult, ALU.add).then_inc(normed, 1)
            v.wait_ge(rstd_in, 1)
            e.cD(v, v.reciprocal(ss[:, :], ss[:, :]))
            for i in range(5):
                v.tensor_scalar(x[:, i, :], x[:, i, :], ss[:, i:i + 1], None, ALU.mult).then_inc(normed, 1)
            v.wait_ge(prm_t, 1)
            e.cD(v, v.tensor_copy(e.prm[:, :], e.ps[:, 4, 0:N_PRM]))
            for i, (t0, m) in enumerate(TOK_TILES):
                v.wait_ge(turned, i + 1)
                pp = e.ps[:, 2 * (i % 2):2 * (i % 2) + 2].rearrange("p a (k t) -> p (a k) t", t=P)
                nw = e.prm[:, 0:KT].unsqueeze(2).to_broadcast([P, KT, m])
                v.tensor_tensor(e.xnT[:, :, t0:t0 + m], pp[:, :, 0:m], nw, ALU.mult).then_inc(evacd, 1)

        @block.scalar
        def _(a):
            a.wait_ge(normed, 1)
            a.activation(ss[:, :], ss[:, :], ACT.Sqrt).then_inc(rstd_in, 1)

        @block.tensor
        def _(pe):
            pe.wait_ge(prm_in, 16 * (len(PRM) + 1))
            pe.transpose(e.ps[:, 4, 0:N_PRM], rows[:, :], e.ident[0:N_PRM, 0:N_PRM]).then_inc(prm_t, 1)
            for i, (t0, m) in enumerate(TOK_TILES):
                pe.wait_ge(normed, 2 + i)
                if i >= 2:
                    pe.wait_ge(evacd, i - 1)
                for k in range(KT):
                    last = pe.transpose(e.ps[:, 2 * (i % 2) + k // 4, k % 4 * P:k % 4 * P + m], x[0:m, i, k * P:(k + 1) * P],
                                        e.ident[0:m, 0:m])
                last.then_inc(turned, 1)


def stage_rwkv(nc, c, e):
    ps, K, prm = e.ps, e.K, e.prm
    pa = e.sb("pa", [P, 13, NT], c=c)
    b2 = e.sb("b2", [P, 4, NT], c=c)
    b3 = e.sb("b3", [P, 4, NT], c=c)
    T = [e.sb(f"t{i}", [P, 5, A_WIDTH], c=c) for i in range(5)]
    B0, B1, B4, B5 = [T[i][:, :, :].rearrange("p a b -> p (a b)")[:, 0:4 * NT].rearrange("p (j t) -> p j t", j=4)
                      for i in range(4)]
    pc = e.sb("chunk_decay", [P, 4, 16], c=c)
    r_, k_, v_ = pa[:, 0:4], pa[:, 4:8], pa[:, 8:12]

    def param(name, j0, n, w=NT):
        a = PRM[name][0] + j0
        return prm[:, a:a + n].unsqueeze(2).to_broadcast([P, n, w])

    with nc.Block() as block:
        @block.sync
        def _(sp):
            e.prefetch(sp, "proj_a")

        @block.tensor
        def _(pe):
            for n in range(*PLAN["proj_a"]):
                slot = e.weights(pe, n)
                e.channel_products(pe, slot, CHUNKS[n][2], KT, e.xnT)

        @block.scalar
        def _(a):
            for j in range(13):
                o = e.unit_wait(a)
                a.copy(pa[:, j].rearrange("p (h t) -> p h t", h=2), o[:, :, 0:HALF]).then_inc(e.taken(), 1)

    c2 = ExitStack()
    w2 = e.sb("w2", [P, A_WIDTH], c=c2)
    last_rows = e.sb("last_rows", [9, 13, P], c=c2)
    prev_rows = e.sb("prev_rows", [DEC_BATCH, 13 * P], c=c2)
    prev = e.sb("prev", [P, 13, DEC_BATCH], c=c2)
    last = e.sb("last", [P, 13, 9], c=c2)
    omka = e.sb("one_minus_ka", [P, 4], c=c2)
    (prev_in, lora_in, prev_t, last_copied, last_t, last_rows_copied, mixed, th_done, lora_mm, sig_done, kk_sq, kk_mm,
     kk_rt, rk_done, rk_mm, vt_mm, vt_done, bonus_done, cum_done, e1, e2, e3, al_done, be_done, tr_mm, tr_taken) = [
        e.sem("a_" + s) for s in (
            "prev_in", "lora_in", "prev_t", "last_copied", "last_t", "last_rows_copied", "mixed", "tanh", "lora_mm", "sig",
            "kk_sq", "kk_mm", "kk_root", "rk", "rk_mm", "vt_mm", "vt_done", "bonus", "cum", "exp1", "exp2", "exp3",
            "alpha", "beta", "tr_mm", "tr_taken")]
    alT, beT, kaT, vT = T[1], T[2], T[3], T[4]

    def bank_pairs_544(j):
        return ps[:, 2 * j:2 * j + 2, 0:HALF]

    def halves(x):
        return x.rearrange("p (h t) -> p h t", h=2)

    with nc.Block() as block:
        @block.sync
        def _(sp):
            sp.dma_start(prev_rows[:, :], e.L["state_a_shift"]).then_inc(prev_in, 16)
            sp.dma_start(w2[0:64, :], e.L["a_w2"]).then_inc(lora_in, 16)
            sp.dma_start(w2[64:P, :], e.L["a_a2"]).then_inc(lora_in, 16)
            sp.wait_ge(last_rows_copied, 1)
            rows = last_rows[:, :, :].rearrange("r j c -> r (j c)")
            e.store(sp, e.O["a_shift_prompt"][e.l], rows[0:1, :])
            e.store(sp, e.O["a_shift_sample"][e.l], rows[1:9, :])
            e.stores_done(sp)

        @block.tensor
        def _(pe):
            pe.wait_ge(prev_in, 16)
            for j in range(13):
                i = pe.transpose(ps[:, 0, j * 8:(j + 1) * 8], prev_rows[:, j * P:(j + 1) * P], e.ident[0:8, 0:8])
            i.then_inc(prev_t, 1)
            pe.wait_ge(last_copied, 1)
            for j in range(13):
                i = pe.transpose(ps[0:9, 4 + j // 4, j % 4 * P:(j % 4 + 1) * P], last[:, j, :], e.ident[:, :])
            i.then_inc(last_t, 1)
            pe.wait_ge(lora_in, 32)
            pe.wait_ge(th_done, 1)
            pe.wait_ge(mixed, 2)
            for j in range(4):
                for which in range(2):
                    u = 2 * j + which
                    if u >= 2:
                        pe.wait_ge(sig_done, u - 1)
                    else:
                        pe.wait_ge(last_rows_copied, 1)
                    s = slice(0, 64) if which == 0 else slice(64, P)
                    for h in range(2):
                        i = pe.matmul(ps[:, 2 * (u % 2) + h, 0:HALF], w2[s, j * P:(j + 1) * P],
                                      pa[s, 12, h * HALF:(h + 1) * HALF], start=True, stop=True)
                    i.then_inc(lora_mm, 1)
            pe.wait_ge(kk_sq, 1)
            pe.wait_ge(sig_done, 8)
            for j in range(4):
                for h in range(2):
                    i = pe.matmul(ps[:, 2 * j + h, 0:HALF], K["bones"][:, :], B0[:, j, h * HALF:(h + 1) * HALF], start=True, stop=True)
            i.then_inc(kk_mm, 1)
            pe.wait_ge(kk_rt, 1)
            for i5, (t0, m) in enumerate(TOK_TILES):
                if i5 >= 2:
                    pe.wait_ge(vt_done, i5 - 1)
                for j in range(4):
                    i = pe.transpose(ps[0:m, i5 % 2, j * P:(j + 1) * P], v_[:, j, t0:t0 + m], e.ident[:, :])
                i.then_inc(vt_mm, 1)
            pe.wait_ge(rk_done, 1)
            pe.wait_ge(vt_done, 5)
            for j in range(4):
                for h in range(2):
                    i = pe.matmul(ps[:, 2 * j + h, 0:HALF], K["bones"][:, :], B0[:, j, h * HALF:(h + 1) * HALF], start=True, stop=True)
            i.then_inc(rk_mm, 1)
            for n, (src, sig) in enumerate(((b3, al_done), (b2, be_done), (k_, be_done))):
                pe.wait_ge(sig, 1)
                if n == 0:
                    pe.wait_ge(bonus_done, 1)
                    pe.wait_ge(al_done, 3)
                for i5, (t0, m) in enumerate(TOK_TILES):
                    u = n * 5 + i5
                    if u >= 2:
                        pe.wait_ge(tr_taken, u - 1)
                    for j in range(4):
                        i = pe.transpose(ps[0:m, u % 2, j * P:(j + 1) * P], src[:, j, t0:t0 + m], e.ident[:, :])
                    i.then_inc(tr_mm, 1)

        @block.scalar
        def _(a):
            e.cA(a, a.copy(last[:, :, 0], pa[:, :, SEQ - 1]))
            a.copy(last[:, :, 1:9], pa[:, :, SEQ:NT].rearrange("p j (b t) -> p j b t", t=4)[:, :, :, 3]).then_inc(last_copied, 1)
            a.wait_ge(last_t, 1)
            for g in range(4):
                n = 4 if g < 3 else 1
                e.cA(a, a.copy(last_rows[:, 4 * g:4 * g + n, :], ps[0:9, 4 + g, 0:n * P].rearrange("r (j c) -> r j c", c=P)))
            a.sem_inc(last_rows_copied, 1)
            a.wait_ge(mixed, 1)
            a.activation(pa[0:64, 12, :], pa[0:64, 12, :], ACT.Tanh).then_inc(th_done, 1)
            for j in range(4):
                for which, (dst, pn) in enumerate(((B1, "a_w0"), (b2, "a_a0"))):
                    u = 2 * j + which
                    a.wait_ge(lora_mm, u + 1)
                    a.activation(halves(dst[:, j]), ps[:, 2 * (u % 2):2 * (u % 2) + 2, 0:HALF], ACT.Sigmoid,
                                 bias=prm[:, PRM[pn][0] + j:PRM[pn][0] + j + 1]).then_inc(sig_done, 1)
            a.wait_ge(kk_mm, 1)
            for j in range(4):
                e.cA(a, a.activation(halves(B0[:, j]), bank_pairs_544(j), ACT.Sqrt))
            a.sem_inc(kk_rt, 1)
            a.wait_ge(cum_done, 1)
            a.activation(B5, B1, ACT.Exp, scale=-DECAY_RATE).then_inc(e1, 1)
            a.wait_ge(al_done, 1)
            a.activation(B5, B4, ACT.Exp, scale=DECAY_RATE).then_inc(e2, 1)
            a.wait_ge(be_done, 1)
            a.activation(B5, B4, ACT.Exp, scale=-DECAY_RATE).then_inc(e3, 1)
            for n, dst in enumerate((alT, beT, kaT)):
                for i5, (t0, m) in enumerate(TOK_TILES):
                    u = n * 5 + i5
                    a.wait_ge(tr_mm, u + 1)
                    a.copy(dst[0:m, i5, :], ps[0:m, u % 2, :]).then_inc(tr_taken, 1)

        @block.vector
        def _(v):
            D = e.cD
            v.wait_ge(prev_t, 1)
            D(v, v.tensor_copy(prev[:, :, :], ps[:, 0, 0:104].rearrange("p (j b) -> p j b", b=8)))
            D(v, v.tensor_scalar(omka[:, :], prm[:, PRM["a_ka"][0]:PRM["a_ka"][1]], -1.0, 1.0, ALU.mult, ALU.add))
            v.wait_ge(last_copied, 1)
            v.wait_ge(last_t, 1)
            for j0 in (12, 0, 4, 8):
                n = 1 if j0 == 12 else 4
                x, d = pa[:, j0:j0 + n], B0[:, 0:n]
                xs, ds = [y[:, :, SEQ:NT].rearrange("p j (b t) -> p j b t", t=4) for y in (x, d)]
                v.tensor_tensor(d[:, :, 1:SEQ], x[:, :, 0:SEQ - 1], x[:, :, 1:SEQ], ALU.subtract)
                v.tensor_scalar(d[:, :, 0:1], x[:, :, 0:1], -1.0, None, ALU.mult)
                v.tensor_tensor(ds[:, :, :, 1:4], xs[:, :, :, 0:3], xs[:, :, :, 1:4], ALU.subtract)
                D(v, v.tensor_tensor(ds[:, :, :, 0], prev[:, j0:j0 + n, :], xs[:, :, :, 0], ALU.subtract))
                D(v, v.tensor_tensor(d, d, param("a_mu", j0, n), ALU.mult))
                if j0 == 12:
                    v.tensor_tensor(x, x, d, ALU.add).then_inc(mixed, 1)
                    v.wait_ge(mixed, 1)
                    v.sem_inc(mixed, 1)
                else:
                    D(v, v.tensor_tensor(x, x, d, ALU.add))
            D(v, v.tensor_tensor(b3[:, :, :], k_, param("a_kk", 0, 4), ALU.mult))
            v.tensor_tensor(B0, b3[:, :, :], b3[:, :, :], ALU.mult).then_inc(kk_sq, 1)
            v.wait_ge(sig_done, 8)
            for j in range(4):
                v.tensor_tensor_scan(B4[:, j], K["reset"][:, :], B1[:, j], 0.0, ALU.mult, ALU.add)
            v.wait_ge(kk_rt, 1)
            D(v, v.tensor_scalar(B0, B0, 1e-12, None, ALU.max))
            D(v, v.reciprocal(B0, B0))
            D(v, v.tensor_tensor(b3[:, :, :], b3[:, :, :], B0, ALU.mult))
            v.tensor_tensor(B1, B4, B1, ALU.subtract).then_inc(cum_done, 1)
            D(v, v.tensor_tensor(B0, b2[:, :, :], param("a_ka", 0, 4), ALU.mult))
            D(v, v.tensor_tensor(B0, B0, omka[:, :].unsqueeze(2).to_broadcast([P, 4, NT]), ALU.add))
            D(v, v.tensor_tensor(k_, k_, B0, ALU.mult))
            D(v, v.tensor_tensor(b2[:, :, :], b2[:, :, :], b3[:, :, :], ALU.mult))
            D(v, v.tensor_tensor(B0, r_, k_, ALU.mult))
            v.tensor_tensor(B0, B0, param("a_rk", 0, 4), ALU.mult).then_inc(rk_done, 1)
            for i5, (t0, m) in enumerate(TOK_TILES):
                v.wait_ge(vt_mm, i5 + 1)
                v.tensor_copy(vT[0:m, i5, :], ps[0:m, i5 % 2, :]).then_inc(vt_done, 1)
            v.wait_ge(rk_mm, 1)
            for j in range(4):
                D(v, v.tensor_tensor(halves(v_[:, j]), bank_pairs_544(j), halves(v_[:, j]), ALU.mult))
            v.sem_inc(bonus_done, 1)
            v.wait_ge(e1, 1)
            v.tensor_tensor(b3[:, :, :], b3[:, :, :], B5, ALU.mult).then_inc(al_done, 1)
            v.wait_ge(e2, 1)
            D(v, v.tensor_tensor(b2[:, :, :], b2[:, :, :], B5, ALU.mult))
            v.tensor_tensor(k_, k_, B5, ALU.mult).then_inc(be_done, 1)
            v.wait_ge(e3, 1)
            v.tensor_tensor(r_, r_, B5, ALU.mult).then_inc(al_done, 1)
            v.tensor_copy(pc[:, :, 0:8], B5[:, :, 0:SEQ].rearrange("p j (c t) -> p j c t", t=CHUNK)[:, :, :, CHUNK - 1])
            D(v, v.tensor_copy(pc[:, :, 8:16], B5[:, :, SEQ:NT].rearrange("p j (c t) -> p j c t", t=4)[:, :, :, 3]))
            v.sem_inc(al_done, 1)
    c2.close()
    _rwkv_inverse(nc, c, e, pa, b2, b3, T, pc)


def _rwkv_inverse(nc, c, e, pa, b2, b3, T, pc):
    ps, K = e.ps, e.K
    alT, beT, kaT, vT = T[1], T[2], T[3], T[4]
    kap, rho = pa[:, 4:8], pa[:, 0:4]
    c2 = ExitStack()
    S = [[e.sb(f"inv{par}_{n}", [P, 512], c=c2) for n in ("x", "xt", "lt", "mt", "y", "lm")] for par in range(2)]
    pe_s, dve_s, act_s, pool_s = [[e.sem(f"inv_{n}{par}") for par in range(2)] for n in ("pe", "dve", "act", "pool")]
    NLEV = 5

    def levels(u):
        return NLEV if u < 8 else 1

    def base(u, per_head):
        return per_head * (u // 2)

    PEN, DVN, ACN, PON = 3 + 2 * NLEV, 2 + NLEV, NLEV + 3, NLEV

    def blocks(u):
        if u < 8:
            j, R = u // 2, slice(64 * (u % 2), 64 * (u % 2) + 64)
            return [(i, P, slice(i * P, (i + 1) * P), (R, j, slice(i * P, (i + 1) * P))) for i in range(4)]
        return [(h, NDEC, slice(h * NDEC, (h + 1) * NDEC),
                 (slice(64 * (h % 2), 64 * (h % 2) + 64), h // 2, slice(SEQ, NT))) for h in range(8)]

    with nc.Block() as block:
        @block.sync
        def _(sp):
            for b in range(DEC_BATCH):
                for i in range(C_GROUPS):
                    src, dst = e.L[f"cache_c{i + 1}_kv"][b], e.O[f"c{i + 1}_kv_sample"][e.l][b]
                    stay = dst.shape[0] - DEC_SEQ
                    flat = lambda x: x.rearrange("r k h d -> (r k h d)").rearrange("(s x) -> s x", s=16)
                    sp.dma_start(flat(dst[0:stay]), flat(src[src.shape[0] - stay:])).then_inc(e.copies_done, 16)

        @block.tensor
        def _(pe):
            def unit_steps(u):
                par, bk = u % 2, 4 * (u % 2)
                x, xt, lt, mt, y, lm = S[par]
                b = base(u, PEN)
                m = P if u < 8 else NDEC
                if u >= 2:
                    pe.wait_ge(act_s[par], base(u, ACN))
                    pe.wait_ge(dve_s[par], base(u, DVN))
                if u == 8:
                    pe.wait_ge(act_s[1], base(9, ACN))
                    pe.wait_ge(dve_s[1], base(9, DVN))
                for bank, (L_, R_) in enumerate(((b3, b2), (b2, b3), (kap, b3))):
                    for i, _, f, (R, j, t) in blocks(u):
                        o = ps[0:m, bk + bank, f] if u < 8 else ps[0:m, bank + 4 * (i % 2), j * NDEC:(j + 1) * NDEC]
                        last = pe.matmul(o, L_[R, j, t], R_[R, j, t], start=True, stop=True)
                last.then_inc(pe_s[par], 1)
                yield
                for lev in range(levels(u)):
                    pe.wait_ge(pool_s[par], base(u, PON) + lev + 1)
                    pe.wait_ge(dve_s[par], base(u, DVN) + 2 + lev)
                    for i, _, f, _x in blocks(u):
                        last = pe.matmul(ps[0:m, bk, f], lm[0:m, f], x[0:m, f], start=True, stop=True)
                    last.then_inc(pe_s[par], 1)
                    yield
                    pe.wait_ge(act_s[par], base(u, ACN) + lev + 1)
                    for i, _, f, _x in blocks(u):
                        last = pe.matmul(ps[0:m, bk + 2, f], y[0:m, f], xt[0:m, f], start=True, stop=True)
                    for i, _, f, _x in blocks(u):
                        last = pe.matmul(ps[0:m, bk + 1, f], xt[0:m, f], y[0:m, f], start=True, stop=True)
                    last.then_inc(pe_s[par], 1)
                    yield
                nl = levels(u)
                pe.wait_ge(dve_s[par], base(u, DVN) + 2 + nl)
                for i, _, f, (R, j, t) in blocks(u):
                    h, tile = (u, i) if u < 8 else (i, 4)
                    pe.matmul(ps[0:m, bk + 3, i * HD:(i + 1) * HD],
                              mt[0:m, f], vT[0:m, tile, h * HD:(h + 1) * HD], start=True, stop=True)
                for i, _, f, (R, j, t) in blocks(u):
                    h, tile = (u, i) if u < 8 else (i, 4)
                    o = ps[R, bk, f] if u < 8 else ps[R, bk + h % 2, j * NDEC:(j + 1) * NDEC]
                    last = pe.matmul(o, alT[0:m, tile, h * HD:(h + 1) * HD], xt[0:m, f], start=True, stop=True)
                last.then_inc(pe_s[par], 1)
                yield
                pe.wait_ge(act_s[par], base(u, ACN) + nl + 1)
                for i, _, f, (R, j, t) in blocks(u):
                    last = pe.matmul(ps[0:m, bk + 2, i * HD:(i + 1) * HD], xt[0:m, f], y[0:m, i * HD:(i + 1) * HD],
                                     start=True, stop=True)
                last.then_inc(pe_s[par], 1)
                yield

            for u0 in range(0, 8, 2):
                for _ in zip(unit_steps(u0), unit_steps(u0 + 1)):
                    pass
            for _ in unit_steps(8):
                pass

        @block.gpsimd
        def _(g):
            def unit_steps(u):
                par = u % 2
                x, xt, lt, mt, y, lm = S[par]
                m = P if u < 8 else NDEC
                w = 512 if u < 8 else 8 * NDEC
                g.wait_ge(dve_s[par], base(u, DVN) + 1)
                for lev in range(levels(u)):
                    if lev:
                        g.wait_ge(pe_s[par], base(u, PEN) + 2 * lev)
                    mk = K["levels"][0:m, (lev + 1) * P:(lev + 1) * P + m].unsqueeze(1).to_broadcast([m, w // m, m])
                    g.tensor_tensor(lm[0:m, 0:w].rearrange("p (i t) -> p i t", t=m), lt[0:m, 0:w].rearrange("p (i t) -> p i t", t=m),
                                    mk, ALU.mult).then_inc(pool_s[par], 1)
                    yield

            for u0 in range(0, 8, 2):
                for _ in zip(unit_steps(u0), unit_steps(u0 + 1)):
                    pass
            for _ in unit_steps(8):
                pass

        @block.scalar
        def _(a):
            def unit_steps(u):
                par, bk = u % 2, 4 * (u % 2)
                x, xt, lt, mt, y, lm = S[par]
                b, m = base(u, PEN), (P if u < 8 else NDEC)
                w = 512 if u < 8 else 8 * NDEC
                for lev in range(levels(u)):
                    a.wait_ge(pe_s[par], b + 2 + 2 * lev)
                    a.copy(y[0:m, 0:w], ps[0:m, bk, 0:w]).then_inc(act_s[par], 1)
                    yield
                nl = levels(u)
                a.wait_ge(pe_s[par], b + 2 + 2 * nl)
                vw = 256 if u < 8 else 512
                a.copy(y[0:m, 0:vw], ps[0:m, bk + 3, 0:vw]).then_inc(act_s[par], 1)
                if u < 8:
                    R, j = slice(64 * (u % 2), 64 * (u % 2) + 64), u // 2
                    a.mul(b3[R, j, 0:SEQ], ps[R, bk, :], -1.0).then_inc(act_s[par], 1)
                else:
                    for hh in range(2):
                        R = slice(64 * hh, 64 * hh + 64)
                        i = a.mul(b3[R, :, SEQ:NT], ps[R, bk + hh, 0:4 * NDEC].rearrange("p (j t) -> p j t", t=NDEC), -1.0)
                        e.cA(a, i)
                    a.sem_inc(act_s[par], 1)
                yield
                a.wait_ge(pe_s[par], b + 3 + 2 * nl)
                if u < 8:
                    a.mul(alT[:, 0:4, u * HD:(u + 1) * HD], ps[:, bk + 2, 0:256].rearrange("p (i d) -> p i d", d=HD),
                          -1.0).then_inc(act_s[par], 1)
                else:
                    a.mul(alT[0:m, 4, :], ps[0:m, bk + 2, :], -1.0).then_inc(act_s[par], 1)
                yield

            for u0 in range(0, 8, 2):
                for _ in zip(unit_steps(u0), unit_steps(u0 + 1)):
                    pass
            for _ in unit_steps(8):
                pass

        @block.vector
        def _(v):
            D = e.cD

            def unit_steps(u):
                par, bk = u % 2, 4 * (u % 2)
                x, xt, lt, mt, y, lm = S[par]
                b, m = base(u, PEN), (P if u < 8 else NDEC)
                w = 512 if u < 8 else 8 * NDEC
                tl = lambda ap: ap.rearrange("p (i t) -> p i t", t=m)
                bc = lambda mk: mk.unsqueeze(1).to_broadcast([m, w // m, m])
                before = K["before"][0:m, 0:m] if u < 8 else K["before4"][0:m, 0:m]

                def masked(dst, bank, mask):
                    if u < 8:
                        return v.tensor_tensor(tl(dst[0:m, 0:w]), tl(ps[0:m, bk + bank, 0:w]), bc(mask), ALU.mult)
                    return v.tensor_tensor(dst[0:m, 0:w].rearrange("p (a z t) -> p z a t", z=2, t=m),
                                           ps[0:m, bank:bank + 5:4, 0:w // 2].rearrange("p z (a t) -> p z a t", t=m),
                                           mask.unsqueeze(1).unsqueeze(1).to_broadcast([m, 2, w // (2 * m), m]), ALU.mult)

                v.wait_ge(pe_s[par], b + 1)
                masked(lt, 1, before).then_inc(dve_s[par], 1)
                v.wait_ge(dve_s[par], base(u, DVN) + 1)
                masked(mt, 2, before)
                masked(x, 0, K["level1"][0:m, 0:m])
                D(v, v.tensor_tensor(tl(xt[0:m, 0:w]), tl(lt[0:m, 0:w]), bc(K["levels"][0:m, 0:m]), ALU.mult))
                D(v, v.tensor_tensor(tl(x[0:m, 0:w]), bc(e.ident[0:m, 0:m]), tl(x[0:m, 0:w]), ALU.subtract))
                v.tensor_tensor(tl(xt[0:m, 0:w]), bc(e.ident[0:m, 0:m]), tl(xt[0:m, 0:w]), ALU.subtract).then_inc(dve_s[par], 1)
                yield
                for lev in range(levels(u)):
                    v.wait_ge(pe_s[par], b + 3 + 2 * lev)
                    v.wait_ge(dve_s[par], base(u, DVN) + 2 + lev)
                    D(v, v.tensor_tensor(x[0:m, 0:w], x[0:m, 0:w], ps[0:m, bk + 1, 0:w], ALU.subtract))
                    v.tensor_tensor(xt[0:m, 0:w], xt[0:m, 0:w], ps[0:m, bk + 2, 0:w], ALU.subtract).then_inc(dve_s[par], 1)
                    yield

            for u0 in range(0, 8, 2):
                for _ in zip(unit_steps(u0), unit_steps(u0 + 1)):
                    pass
            for _ in unit_steps(8):
                pass
    c2.close()
    _rwkv_sequence(nc, c, e, pa, b2, b3, T, pc)


def _rwkv_sequence(nc, c, e, pa, b2, b3, T, pc):
    ps, K = e.ps, e.K
    g2, beT, kaT, vT = T[1], T[2], T[3], T[4]
    g1, kap, rho, bonus = b3, pa[:, 4:8], pa[:, 0:4], pa[:, 8:12]
    ya = e.ya
    bd4 = K["bones"][:, :].unsqueeze(1).to_broadcast([P, 4, P])
    c2 = ExitStack()
    ST = e.sb("state", [P, 4, P], c=c2)
    U = e.sb("u", [P, 2, 512], c=c2)
    upd = e.sb("upd", [P, 512], c=c2)
    at = [e.sb(f"at{i}", [P, 8, P], c=c2) for i in range(2)]
    (u_mm, u_done, s_mm, s_done, at_mm, at_done, y_mm, y_done, f_mm, f_done) = [e.sem("seq_" + s) for s in
        ("u_mm", "u", "s_mm", "s", "at_mm", "at", "y_mm", "y", "f_mm", "f")]
    with nc.Block() as block:
        @block.sync
        def _(sp):
            sp.wait_ge(f_done, 1)
            fin = upd[:, :].rearrange("p (a j) -> p a j", a=4)
            for hh in range(2):
                R = slice(64 * hh, 64 * hh + 64)
                e.store(sp, e.O["a_wkv_prompt"][e.l, 0].rearrange("(p hh) i j -> hh i p j", hh=2)[hh], fin[R, :, 64 * hh:64 * hh + 64])
            e.stores_done(sp)

        @block.tensor
        def _(pe):
            for ck in range(NCHUNK):
                tile, q = ck // 2, ck % 2
                Rq = slice(64 * q, 64 * q + 64)
                t = slice(ck * CHUNK, (ck + 1) * CHUNK)
                pe.wait_ge(s_done, ck + 1)
                for p in range(4):
                    last = pe.matmul(ps[Rq, 0, p * P:(p + 1) * P], g1[:, p, t], ST[:, p, :], start=True, stop=True)
                last.then_inc(u_mm, 1)
                if q == 0 and tile >= 2:
                    pe.wait_ge(y_done, tile - 1)
                yb_ = 1 + tile % 2
                for p in range(4):
                    pe.matmul(ps[:, yb_, p * P + q * 64:p * P + q * 64 + 64], ST[:, p, :], rho[:, p, t],
                              start=(q == 0 and p == 0), stop=False, skip_group_check=True)
                if q == 0:
                    if tile:
                        pe.wait_ge(at_done, 4 * tile)
                    tt = slice(tile * P, (tile + 1) * P)
                    for n, src in enumerate((b2, kap)):
                        for h in range(8):
                            R = slice(64 * (h % 2), 64 * (h % 2) + 64)
                            last = pe.matmul(ps[:, 4 + 2 * n + h % 2, h // 2 * P:(h // 2 + 1) * P], src[R, h // 2, tt],
                                             rho[R, h // 2, tt], start=True, stop=True)
                    last.then_inc(at_mm, 1)
                pe.wait_ge(u_done, ck + 1)
                for p in range(4):
                    pp = slice(p * P, (p + 1) * P)
                    pe.matmul(ps[:, 3, pp], beT[Rq, tile, pp], U[Rq, tile % 2, pp], start=True, stop=False)
                    last = pe.matmul(ps[:, 3, pp], kaT[Rq, tile, pp], vT[Rq, tile, pp], start=False, stop=True)
                last.then_inc(s_mm, 1)
                if q == 1:
                    pe.wait_ge(at_done, 4 * (tile + 1))
                    for h in range(8):
                        R, p = slice(64 * (h % 2), 64 * (h % 2) + 64), h // 2
                        f = slice(h * HD, (h + 1) * HD)
                        o = ps[R, yb_, p * P:(p + 1) * P]
                        pe.matmul(o, U[:, tile % 2, f], at[0][:, h, :], start=False, stop=False, skip_group_check=True)
                        last = pe.matmul(o, vT[:, tile, f], at[1][:, h, :], start=False, stop=True, skip_group_check=True)
                    last.then_inc(y_mm, 1)
            pe.wait_ge(s_done, NCHUNK + 1)
            for p in range(4):
                last = pe.transpose(ps[:, 0, p * P:(p + 1) * P], ST[:, p, :], e.ident[:, :])
            last.then_inc(f_mm, 1)

        @block.scalar
        def _(a):
            for tile in range(TT):
                a.wait_ge(y_mm, tile + 1)
                a.copy(ya[:, :, tile * P:(tile + 1) * P], ps[:, 1 + tile % 2, :].rearrange("p (a t) -> p a t", a=4)).then_inc(y_done, 1)
            a.wait_ge(f_mm, 1)
            a.wait_ge(s_done, NCHUNK + 1)
            a.copy(upd[:, :], ps[:, 0, :]).then_inc(f_done, 1)

        @block.vector
        def _(v):
            D = e.cD
            v.memset(ST[:, :, :], 0.0).then_inc(s_done, 1)
            v.wait_ge(s_done, 1)
            for ck in range(NCHUNK):
                tile, q = ck // 2, ck % 2
                Rq = slice(64 * q, 64 * q + 64)
                v.wait_ge(u_mm, ck + 1)
                if q == 0 and tile >= 2:
                    v.wait_ge(y_mm, tile - 1)
                v.tensor_tensor(U[Rq, tile % 2, :], ps[Rq, 0, :], g2[Rq, tile, :], ALU.add).then_inc(u_done, 1)
                if q == 0:
                    v.wait_ge(at_mm, tile + 1)
                    if tile:
                        v.wait_ge(y_mm, tile)
                    for n in range(2):
                        for hh in range(2):
                            v.tensor_tensor(at[n][:, :, :].rearrange("p (a hh) t -> p hh a t", hh=2)[:, hh],
                                            ps[:, 4 + 2 * n + hh, :].rearrange("p (a t) -> p a t", a=4),
                                            K["upto"][:, :].unsqueeze(1).to_broadcast([P, 4, P]), ALU.mult).then_inc(at_done, 1)
                v.wait_ge(s_mm, ck + 1)
                up4 = upd[:, :].rearrange("p (a t) -> p a t", a=4)
                D(v, v.tensor_tensor(up4, ps[:, 3, :].rearrange("p (a t) -> p a t", a=4), bd4, ALU.mult))
                D(v, v.tensor_tensor(ST[:, :, :], ST[:, :, :], up4, ALU.add))
                v.tensor_tensor(ST[:, :, :], ST[:, :, :], pc[:, :, ck:ck + 1].to_broadcast([P, 4, P]), ALU.mult).then_inc(s_done, 1)
                v.wait_ge(s_done, ck + 2)
    c2.close()

    c2 = ExitStack()
    SN = e.sb("state_rows", [P, 2, 8, P], c=c2)
    SS = e.sb("state_s", [P, 8, P], c=c2)
    G1m = e.sb("g1m", [P, 8, NDEC], c=c2)
    Us = e.sb("us", [NDEC, P], c=c2)
    Um = e.sb("um", [NDEC, 2, 8, P], c=c2)
    ats = e.sb("ats", [NDEC, 4, NDEC], c=c2)
    (z_done, s_in, t_mm, t_done, m_done, u_mm, u_done, at_mm, at_done, y_mm, y_done, s_mm, s_done, b_mm, b_done) = [
        e.sem("dec_" + s) for s in ("zero", "s_in", "t_mm", "t", "masked", "u_mm", "u", "at_mm", "at", "y_mm", "y", "s_mm", "s",
                                    "b_mm", "b")]
    with nc.Block() as block:
        @block.sync
        def _(sp):
            sp.wait_ge(z_done, 1)
            src = e.L["state_a_wkv"]

            def load(p):
                if p >= 2:
                    sp.wait_ge(e.out_stored, 16 * n_before[p - 2])
                for hh in range(2):
                    R = slice(64 * hh, 64 * hh + 64)
                    sp.dma_start(SN[R, p % 2, :, 64 * hh:64 * hh + 64],
                                 src[:, 2 * p + hh].rearrange("b i j -> i b j")).then_inc(s_in, 16)

            n_before = []
            load(0)
            load(1)
            for p in range(4):
                sp.wait_ge(b_done, 2 * (p + 1))
                for hh in range(2):
                    R = slice(64 * hh, 64 * hh + 64)
                    e.store(sp, e.O["a_wkv_sample"][e.l][:, 2 * p + hh].rearrange("b i j -> i b j"),
                            SN[R, p % 2, :, 64 * hh:64 * hh + 64])
                n_before.append(e.stores[0])
                if p + 2 < 4:
                    load(p + 2)
            e.stores_done(sp)

        @block.tensor
        def _(pe):
            for p in range(4):
                pp = slice(p * P, (p + 1) * P)
                pe.wait_ge(s_in, 64 if p == 0 else 32 * (p + 1))
                if p:
                    pe.wait_ge(b_done, 2 * p)
                for b in range(8):
                    last = pe.transpose(ps[:, b // 4, b % 4 * P:(b % 4 + 1) * P], SN[:, p % 2, b, :], e.ident[:, :])
                last.then_inc(t_mm, 1)
                if p:
                    pe.wait_ge(at_done, 4 * p)
                for n, src in enumerate((b2, kap)):
                    for hh in range(2):
                        R = slice(64 * hh, 64 * hh + 64)
                        last = pe.matmul(ps[0:NDEC, 6 + hh, n * NDEC:(n + 1) * NDEC], src[R, p, SEQ:NT], rho[R, p, SEQ:NT],
                                         start=True, stop=True)
                last.then_inc(at_mm, 1)
                pe.wait_ge(t_done, 2 * (p + 1))
                pe.wait_ge(m_done, 3 * p + 1)
                for b in range(8):
                    last = pe.matmul(ps[0:NDEC, 2, 0:P], G1m[:, b, :], SS[:, b, :], start=(b == 0), stop=(b == 7))
                last.then_inc(u_mm, 1)
                if p:
                    pe.wait_ge(y_done, p)
                for b in range(8):
                    t = slice(SEQ + 4 * b, SEQ + 4 * b + 4)
                    pe.matmul(ps[:, 3, 4 * b:4 * b + 4], SS[:, b, :], rho[:, p, t], start=(b == 0), stop=False, skip_group_check=True)
                pe.wait_ge(u_done, p + 1)
                pe.wait_ge(at_done, 4 * (p + 1))
                for hh in range(2):
                    R = slice(64 * hh, 64 * hh + 64)
                    f = slice(p * P + hh * HD, p * P + (hh + 1) * HD)
                    pe.matmul(ps[R, 3, 0:NDEC], Us[:, hh * HD:(hh + 1) * HD], ats[:, hh, :], start=False, stop=False, skip_group_check=True)
                    last = pe.matmul(ps[R, 3, 0:NDEC], vT[0:NDEC, 4, f], ats[:, 2 + hh, :], start=False, stop=True, skip_group_check=True)
                last.then_inc(y_mm, 1)
                pe.wait_ge(m_done, 3 * p + 3)
                for b in range(8):
                    o = ps[:, 4 + b // 4, b % 4 * P:(b % 4 + 1) * P]
                    pe.matmul(o, beT[0:NDEC, 4, pp], Um[:, 0, b, :], start=True, stop=False)
                    last = pe.matmul(o, kaT[0:NDEC, 4, pp], Um[:, 1, b, :], start=False, stop=True)
                last.then_inc(s_mm, 1)
                pe.wait_ge(s_done, p + 1)
                for b in range(8):
                    last = pe.transpose(ps[:, b // 4, b % 4 * P:(b % 4 + 1) * P], SS[:, b, :], e.ident[:, :])
                last.then_inc(b_mm, 1)

        @block.scalar
        def _(a):
            for p in range(4):
                a.wait_ge(t_mm, p + 1)
                for half in range(2):
                    a.copy(SS[:, 4 * half:4 * half + 4, :], ps[:, half, :].rearrange("p (b t) -> p b t", b=4)).then_inc(t_done, 1)
                a.wait_ge(y_mm, p + 1)
                a.copy(ya[:, p, SEQ:NT], ps[:, 3, 0:NDEC]).then_inc(y_done, 1)
                a.wait_ge(b_mm, p + 1)
                for half in range(2):
                    a.copy(SN[:, p % 2, 4 * half:4 * half + 4, :], ps[:, half, :].rearrange("p (b t) -> p b t", b=4)).then_inc(b_done, 1)

        @block.vector
        def _(v):
            D = e.cD
            v.memset(SN[:, :, :, :], 0.0).then_inc(z_done, 1)
            rowb = K["rowb"][0:NDEC, :].unsqueeze(2).to_broadcast([NDEC, 8, P])
            for p in range(4):
                pp = slice(p * P, (p + 1) * P)
                if p:
                    v.wait_ge(s_mm, p)
                v.tensor_tensor(G1m[:, :, :], g1[:, p, SEQ:NT].unsqueeze(1).to_broadcast([P, 8, NDEC]),
                                K["colb"][:, :].rearrange("p (b t) -> p b t", b=8), ALU.mult).then_inc(m_done, 1)
                v.tensor_tensor(Um[:, 1], vT[0:NDEC, 4, pp].unsqueeze(1).to_broadcast([NDEC, 8, P]), rowb, ALU.mult).then_inc(m_done, 1)
                v.wait_ge(at_mm, p + 1)
                for n in range(2):
                    for hh in range(2):
                        v.tensor_tensor(ats[:, 2 * n + hh, :], ps[0:NDEC, 6 + hh, n * NDEC:(n + 1) * NDEC], K["upto4"][0:NDEC, 0:NDEC],
                                        ALU.mult).then_inc(at_done, 1)
                v.wait_ge(u_mm, p + 1)
                v.tensor_tensor(Us[:, :], ps[0:NDEC, 2, 0:P], g2[0:NDEC, 4, pp], ALU.add).then_inc(u_done, 1)
                v.wait_ge(u_done, p + 1)
                v.tensor_tensor(Um[:, 0], Us[:, :].unsqueeze(1).to_broadcast([NDEC, 8, P]), rowb, ALU.mult).then_inc(m_done, 1)
                v.wait_ge(s_mm, p + 1)
                x4 = ps[:, 4:6, :].rearrange("p a (b t) -> p (a b) t", t=P)
                D(v, v.tensor_tensor(x4, x4, K["bones"][:, :].unsqueeze(1).to_broadcast([P, 8, P]), ALU.mult))
                D(v, v.tensor_tensor(SS[:, :, :], SS[:, :, :], x4, ALU.add))
                v.tensor_tensor(SS[:, :, :], SS[:, :, :], pc[:, p, 8:16].unsqueeze(2).to_broadcast([P, 8, P]), ALU.mult).then_inc(s_done, 1)
    c2.close()

    B0 = T[0][:, :, :].rearrange("p a b -> p (a b)")[:, 0:4 * NT].rearrange("p (j t) -> p j t", j=4)
    mean_mm, sq_done, var_mm, var_done, root_done = [e.sem("gn_" + s) for s in ("mean_mm", "sq", "var_mm", "var", "root")]

    def group_sum(pe, src):
        for j in range(4):
            for h in range(2):
                last = pe.matmul(ps[:, 2 * j + h, 0:HALF], K["bones"][:, :], src[:, j, h * HALF:(h + 1) * HALF], start=True, stop=True)
        return last

    def param(name):
        a = PRM[name][0]
        return e.prm[:, a:a + 4].unsqueeze(2).to_broadcast([P, 4, NT])

    with nc.Block() as block:
        @block.sync
        def _(sp):
            pass

        @block.tensor
        def _(pe):
            group_sum(pe, ya).then_inc(mean_mm, 1)
            pe.wait_ge(sq_done, 1)
            group_sum(pe, B0).then_inc(var_mm, 1)

        @block.scalar
        def _(a):
            a.wait_ge(var_done, 1)
            a.activation(B0, B0, ACT.Sqrt).then_inc(root_done, 1)

        @block.vector
        def _(v):
            D = e.cD
            v.wait_ge(mean_mm, 1)
            for j in range(4):
                y2 = ya[:, j].rearrange("p (h t) -> p h t", h=2)
                D(v, v.scalar_tensor_tensor(y2, ps[:, 2 * j:2 * j + 2, 0:HALF], -1.0 / HD, y2, ALU.mult, ALU.add))
            v.tensor_tensor(B0, ya[:, :, :], ya[:, :, :], ALU.mult).then_inc(sq_done, 1)
            v.wait_ge(var_mm, 1)
            for j in range(4):
                D(v, v.tensor_scalar(B0[:, j].rearrange("p (h t) -> p h t", h=2), ps[:, 2 * j:2 * j + 2, 0:HALF], 1.0 / HD, A_GN_EPS,
                                ALU.mult, ALU.add))
            v.sem_inc(var_done, 1)
            v.wait_ge(root_done, 1)
            D(v, v.reciprocal(B0, B0))
            D(v, v.tensor_tensor(ya[:, :, :], ya[:, :, :], B0, ALU.mult))
            D(v, v.tensor_tensor(ya[:, :, :], ya[:, :, :], param("a_gn_w"), ALU.mult))
            D(v, v.tensor_tensor(ya[:, :, :], ya[:, :, :], param("a_gn_b"), ALU.add))
            D(v, v.tensor_tensor(ya[:, :, :], ya[:, :, :], bonus, ALU.add))



def stage_stick_breaking(nc, c, e):
    e.yb, e.yc = e.sb("yb", [P, 4, NT]), e.sb("yc", [P, 3, NT])
    ps, K, yb = e.ps, e.K, e.yb
    qbd = e.sb("bq_blocks", [P, 4, DEC_BATCH, 32], c=c)
    kTn, vn = e.sb("bk_new_t", [P, 4, NDEC], c=c), e.sb("bv_new", [NDEC, B_WIDTH], c=c)
    c1 = ExitStack()
    qT, kT = e.sb("bq", [P, 4, NT], c=c1), e.sb("bk", [P, 4, NT], c=c1)
    vt, kt = e.sb("bv_tok", [P, 5, B_WIDTH], c=c1), e.sb("bk_tok", [P, 5, B_WIDTH], c=c1)
    new_clear = e.sem("b_new_clear")
    k_mm, k_done, v_ready = e.sem("b_k_mm"), e.sem("b_k_done"), e.sem("b_v_ready")

    def store_tokens(sp, tok, prompt, sample):
        e.store(sp, prompt[e.l, 0].rearrange("(i p) h d -> p i (h d)", p=P), tok[:, 0:TT, :])
        e.store(sp, sample[e.l].rearrange("b t h d -> (b t) (h d)"), tok[0:NDEC, TT, :])

    with nc.Block() as block:
        @block.sync
        def _(sp):
            e.prefetch(sp, "proj_b")
            sp.wait_ge(v_ready, 1)
            store_tokens(sp, vt, e.O["b_v_prompt"], e.O["b_v_sample"])
            sp.wait_ge(k_done, 5)
            store_tokens(sp, kt, e.O["b_k_prompt"], e.O["b_k_sample"])

        @block.tensor
        def _(pe):
            n0, n1 = PLAN["proj_b"]
            for n in range(n0, n1):
                slot = e.weights(pe, n)
                if n < n0 + 4:
                    e.channel_products(pe, slot, CW, KT, e.xnT)
                else:
                    e.token_products(pe, slot, CW, e.xnT)
            for i, (t0, m) in enumerate(TOK_TILES):
                if i >= 2:
                    pe.wait_ge(k_done, i - 1)
                for j in range(4):
                    last = pe.transpose(ps[0:m, 4 + i % 2, j * P:(j + 1) * P], kT[:, j, t0:t0 + m], e.ident[:, :])
                last.then_inc(k_mm, 1)

        @block.scalar
        def _(a):
            for j in range(8):
                o = e.unit_wait(a)
                dst = (qT if j < 4 else kT)[:, j % 4].rearrange("p (h t) -> p h t", h=2)
                a.mul(dst, o[:, :, 0:HALF], QK_SCALE if j < 4 else 1.0).then_inc(e.taken(), 1)
            for half in range(2):
                for i, (t0, m) in enumerate(TOK_TILES):
                    o = e.unit_wait(a)
                    a.copy(vt[0:m, i, half * CW:(half + 1) * CW], o[0:m, 0, 0:CW]).then_inc(e.taken(), 1)
            e.wait_taken(a, e.unit["take"] - 1)
            a.sem_inc(v_ready, 1)
            for i, (t0, m) in enumerate(TOK_TILES):
                a.wait_ge(k_mm, i + 1)
                a.copy(kt[0:m, i, :], ps[0:m, 4 + i % 2, :]).then_inc(k_done, 1)

    NQ = 1280
    col = [0, 512, 1024, 896]
    wid = [512 - P * s for s in range(4)]
    c2 = ExitStack()
    bufs = [[e.sb(f"sb{s}_{n}", [P, NQ], c=c2) for n in range(2)] for s in range(2)]
    (z_mm, ln_done, re_done, sp_done, spm_done, cum_mm, w_done, wm_done, y_mm, y_done) = [e.sem("sb_" + s) for s in
        ("z_mm", "ln", "scores", "sp", "sp_masked", "cum_mm", "w", "w_masked", "y_mm", "y")]

    def bank(h):
        return ps[:, 3 * (h % 2):3 * (h % 2) + 3, :].rearrange("p a b -> p (a b)")[:, 0:NQ]

    with nc.Block() as block:
        @block.sync
        def _(sp):
            pass

        @block.tensor
        def _(pe):
            for i in range(B_HEADS + 2):
                if i < B_HEADS:
                    h = i
                    R, z = slice(64 * (h % 2), 64 * (h % 2) + 64), bank(h)
                    if h >= 2:
                        pe.wait_ge(w_done, h - 1)
                    for s in range(4):
                        last = pe.matmul(z[:, col[s]:col[s] + wid[s]], kT[R, h // 2, s * P:(s + 1) * P], qT[R, h // 2, s * P:SEQ],
                                         start=(s != 3), stop=False, skip_group_check=True)
                    last.then_inc(z_mm, 1)
                if 1 <= i <= B_HEADS:
                    h = i - 1
                    z, sp_ = bank(h), bufs[h % 2][0]
                    pe.wait_ge(spm_done, h + 1)
                    for s in range(4):
                        for j in range(s, 4):
                            o = col[s] + (j - s) * P
                            last = pe.matmul(z[:, o:col[s] + wid[s]], K["tri" if j == s else "allneg"][:, :],
                                             sp_[:, col[j]:col[j] + wid[j]], start=False, stop=(j == 3), skip_group_check=True)
                    last.then_inc(cum_mm, 1)
                if i >= 2:
                    h = i - 2
                    R, w = slice(64 * (h % 2), 64 * (h % 2) + 64), bufs[h % 2][1]
                    pe.wait_ge(wm_done, h + 1)
                    if h >= 4 and h % 2 == 0:
                        pe.wait_ge(y_done, h // 2 - 1)
                    for s in range(4):
                        last = pe.matmul(ps[R, 6 + h // 2 % 2, s * P:SEQ], vt[:, s, h * HD:(h + 1) * HD], w[:, col[s]:col[s] + wid[s]],
                                         start=(s == 0), stop=(s == 3), skip_group_check=True)
                    last.then_inc(y_mm, 1)

        @block.scalar
        def _(a):
            A = e.cA
            for i in range(B_HEADS + 2):
                if i < B_HEADS:
                    h = i
                    b0, b1 = bufs[h % 2]
                    a.wait_ge(re_done, h + 1)
                    if h >= 2:
                        a.wait_ge(cum_mm, h - 1)
                    A(a, a.activation(b0[:, :], b1[:, :], ACT.Abs))
                    A(a, a.activation(b0[:, :], b0[:, :], ACT.Exp, scale=-1.0))
                    a.activation(b0[:, :], b0[:, :], ACT.Ln, bias=1.0).then_inc(ln_done, 1)
                if 1 <= i <= B_HEADS:
                    h = i - 1
                    a.wait_ge(cum_mm, h + 1)
                    a.activation(bufs[h % 2][1][:, :], bank(h), ACT.Exp, bias=e.bias_b[:, h:h + 1]).then_inc(w_done, 1)
                if i >= 2 and i % 2 == 1:
                    a.wait_ge(y_mm, i - 1)
                    a.copy(yb[:, (i - 2) // 2, 0:SEQ], ps[:, 6 + (i - 2) // 2 % 2, :]).then_inc(y_done, 1)

        @block.vector
        def _(v):
            v.memset(qbd[:, :, :, :], 0.0).then_inc(new_clear, 1)
            v.tensor_copy(kTn[:, :, :], kT[:, :, SEQ:NT])
            v.tensor_copy(vn[:, :], vt[0:NDEC, 4, :])
            v.wait_ge(new_clear, 1)
            for h in range(B_HEADS):
                R = slice(64 * (h % 2), 64 * (h % 2) + 64)
                v.tensor_copy(qbd[R, h // 2, :, 4 * h:4 * h + 4], qT[R, h // 2, SEQ:NT].rearrange("p (b t) -> p b t", t=4))
            for h in range(B_HEADS):
                b0, b1 = bufs[h % 2]
                v.wait_ge(z_mm, h + 1)
                if h >= 2:
                    v.wait_ge(y_mm, h - 1)
                v.tensor_scalar(b1[:, :], bank(h), e.bias_b[:, h:h + 1], None, ALU.add).then_inc(re_done, 1)
                v.wait_ge(re_done, h + 1)
                v.wait_ge(ln_done, h + 1)
                v.scalar_tensor_tensor(b0[:, :], b1[:, :], 0.0, b0[:, :], ALU.max, ALU.add).then_inc(sp_done, 1)

        @block.gpsimd
        def _(g):
            for i in range(B_HEADS + 1):
                if i < B_HEADS:
                    b0 = bufs[i % 2][0]
                    g.wait_ge(sp_done, i + 1)
                    for s in range(4):
                        d = b0[:, col[s]:col[s] + P]
                        last = g.affine_select(out=d, in_=d, compare_op=ALU.is_gt, fill=0.0, base=0, pattern=[[1, P]], channel_multiplier=-1)
                    last.then_inc(spm_done, 1)
                if i >= 1:
                    h = i - 1
                    b1 = bufs[h % 2][1]
                    g.wait_ge(w_done, h + 1)
                    for s in range(4):
                        d = b1[:, col[s]:col[s] + P]
                        last = g.affine_select(out=d, in_=d, compare_op=ALU.is_gt, fill=0.0, base=0, pattern=[[1, P]], channel_multiplier=-1)
                    last.then_inc(wm_done, 1)
    c2.close()

    with nc.Block() as block:
        @block.sync
        def _(sp):
            e.stores_done(sp)
    c1.close()

    c2 = ExitStack()
    NK = PAST_LEN + NDEC
    NCH = 2 * DEC_BATCH
    pages = e.sb("pages", [1, DEC_BATCH * N_PAGES], I32, c=c2)
    kp = e.sb("k_pages", [P, 2, 4, B_WIDTH], c=c2)
    vp = e.sb("v_pages", [P, 2, N_PAGES, B_WIDTH], c=c2)
    kpT = e.sb("k_pages_t", [P, 2, 4, 4 * PAGE], c=c2)
    zb, sp_ = [[e.sb(f"d{n}{i}", [P, NK], c=c2) for i in range(2)] for n in ("zb", "sp")]
    ones = e.sb("ones", [P, NK], c=c2)
    wT = e.sb("d_weights_t", [P, 9, P], c=c2)
    own = e.sb("d_own_head", [P, B_WIDTH], c=c2)
    rowbias = e.sb("d_row_bias", [P, 1], c=c2)
    (pt_in, bias_done, k_mm, takeA, takeD, z_mm, z_done, ln_done, r_done, w_done, y_mm, own_done, f_mm, f_done) = [
        e.sem("sd_" + s) for s in ("pt_in", "bias", "k_mm", "take_a", "take_d", "z_mm", "z", "ln", "rest", "w", "y_mm", "own",
                                   "f_mm", "f")]
    k_in = [e.sem(f"sd_k_in{j}") for j in range(2)]
    v_in = [e.sem(f"sd_v_in{j}") for j in range(2)]
    NKR = 4 * NCH

    def take(eng, copy, i, sem):
        eng.wait_ge(k_mm, i + 1)
        bank = ps[:, 6 + i % 2, :]
        if i < NKR:
            ch, j = i // 4, i % 4
            if ch >= 2:
                eng.wait_ge(z_mm, ch - 1)
            copy(kpT[:, ch % 2, :, j * PAGE:(j + 1) * PAGE], bank.rearrange("p (a t) -> p a t", a=4)).then_inc(sem, 1)
        else:
            half, r = (i - NKR) // 3, (i - NKR) % 3
            if half:
                eng.wait_ge(y_mm, 4)
            if r < 2:
                copy(wT[:, 4 * r:4 * r + 4, :], bank.rearrange("p (a t) -> p a t", a=4)).then_inc(sem, 1)
            else:
                copy(wT[0:NDEC, 8, :], bank[0:NDEC, 0:P]).then_inc(sem, 1)

    with nc.Block() as block:
        @block.sync
        def _(sp):
            sp.dma_start(pages[0:1, :], e.I["page_table"].rearrange("b n -> (b n)").unsqueeze(0)).then_inc(pt_in, 16)
            sp.wait_ge(pt_in, 16)
            n_pool = e.I["cache_b_k"].shape[1]

            def load(cache, dst, n, arrived):
                page = sp.value_load(pages[0:1, n:n + 1], min_val=0, max_val=n_pool - 1)
                sp.dma_start(dst, e.L[cache][bass.ds(page, 1)].rearrange("a p h d -> p (a h d)")).then_inc(arrived, 16)

            def load_values(b):
                if b >= 2:
                    sp.wait_ge(y_mm, b - 1)
                for j in range(N_PAGES):
                    load("cache_b_v", vp[:, b % 2, j, :], b * N_PAGES + j, v_in[b % 2])

            for ch in range(NCH):
                if ch >= 2:
                    sp.wait_ge(k_mm, 4 * (ch - 1))
                for j in range(4):
                    load("cache_b_k", kp[:, ch % 2, j, :], 4 * ch + j, k_in[ch % 2])
                if ch in (5, 7):
                    load_values((ch - 5) // 2)
            for b in range(2, DEC_BATCH):
                load_values(b)

        @block.tensor
        def _(pe):
            def turn(i, blocks):
                if i >= 2:
                    pe.wait_ge((takeA, takeD)[i % 2], i // 2)
                for j, (src, m) in enumerate(blocks):
                    last = pe.transpose(ps[0:m, 6 + i % 2, j * P:(j + 1) * P], src, e.ident[:, :])
                last.then_inc(k_mm, 1)

            def wait_rounds(n):
                pe.wait_ge(takeA, (n + 1) // 2)
                pe.wait_ge(takeD, n // 2)

            def turn_keys(ch):
                pe.wait_ge(k_in[ch % 2], 64 * (ch // 2 + 1))
                for j in range(4):
                    turn(4 * ch + j, [(kp[:, ch % 2, j, p * P:(p + 1) * P], P) for p in range(4)])

            turn_keys(0)
            for ch in range(NCH):
                if ch + 1 < NCH:
                    turn_keys(ch + 1)
                b, part = ch // 2, ch % 2
                half, R = b // 4, slice(32 * (b % 4), 32 * (b % 4) + 32)
                wait_rounds(4 * (ch + 1))
                for p in range(4):
                    last = pe.matmul(ps[R, 2 * half + part, :], qbd[:, p, b, :], kpT[:, ch % 2, p, :], start=(p == 0), stop=(p == 3))
                if part == 1:
                    for p in range(4):
                        last = pe.matmul(ps[R, 4 + half, 0:NDEC], qbd[:, p, b, :], kTn[:, p, :], start=(p == 0), stop=(p == 3))
                last.then_inc(z_mm, 1)
            for half in range(2):
                pe.wait_ge(w_done, half + 1)
                i0 = NKR + 3 * half
                w = zb[half]
                for r in range(2):
                    turn(i0 + r, [(w[:, (4 * r + j) * P:(4 * r + j + 1) * P], P) for j in range(4)])
                turn(i0 + 2, [(w[:, PAST_LEN:NK], NDEC)])
                wait_rounds(i0 + 3)
                for b in range(4 * half, 4 * half + 4):
                    R = slice(32 * (b % 4), 32 * (b % 4) + 32)
                    pe.wait_ge(v_in[b % 2], 16 * N_PAGES * (b // 2 + 1))
                    for j in range(N_PAGES):
                        pe.matmul(ps[R, 2 * half, :], wT[:, j, R], vp[:, b % 2, j, :], start=(j == 0), stop=False)
                    last = pe.matmul(ps[R, 2 * half, :], wT[0:NDEC, 8, R], vn[:, :], start=False, stop=True)
                    last.then_inc(y_mm, 1)
                pe.wait_ge(own_done, half + 1)
                for p in range(4):
                    last = pe.matmul(ps[:, 4 + half, 64 + 16 * p:80 + 16 * p], own[:, p * P:(p + 1) * P], K["rowtoken"][:, :], start=True, stop=True)
                last.then_inc(f_mm, 1)

        @block.scalar
        def _(a):
            A = e.cA

            def logs_of(half):
                z, s = zb[half], sp_[half]
                a.wait_ge(z_done, half + 1)
                A(a, a.activation(s[:, :], z[:, :], ACT.Abs))
                A(a, a.activation(s[:, :], s[:, :], ACT.Exp, scale=-1.0))
                a.activation(s[:, :], s[:, :], ACT.Ln, bias=1.0).then_inc(ln_done, 1)

            def weights_of(half):
                a.wait_ge(r_done, half + 1)
                a.activation(zb[half][:, :], zb[half][:, :], ACT.Exp).then_inc(w_done, 1)

            for i in range(0, NKR, 2):
                take(a, a.copy, i, takeA)
                if i == 4 * 10:
                    logs_of(0)
                if i == 4 * 12 + 2:
                    weights_of(0)
            logs_of(1)
            weights_of(1)
            for half in range(2):
                for i in range(NKR + 3 * half, NKR + 3 * half + 3):
                    if i % 2 == 0:
                        take(a, a.copy, i, takeA)
                a.wait_ge(f_mm, half + 1)
                a.copy(yb[:, :, SEQ + 16 * half:SEQ + 16 * half + 16],
                       ps[:, 4 + half, 64:128].rearrange("p (a t) -> p a t", a=4)).then_inc(f_done, 1)

        @block.vector
        def _(v):
            D = e.cD
            D(v, v.tensor_tensor(own[:, 0:8], e.bias_b[:, :], K["rowhead"][:, :], ALU.mult))
            D(v, v.tensor_reduce(rowbias[:, :], own[:, 0:8], AX_X, ALU.add))
            D(v, v.memset(ones[:, :], 1.0))

            def scores_of(half):
                z = zb[half]
                v.wait_ge(z_mm, 8 * (half + 1))
                v.tensor_scalar(z[:, 0:PAST_LEN], ps[:, 2 * half:2 * half + 2, :].rearrange("p a b -> p (a b)"), rowbias[:, 0:1], None, ALU.add)
                D(v, v.tensor_scalar(z[:, PAST_LEN:NK], ps[:, 4 + half, 0:NDEC], rowbias[:, 0:1], None, ALU.add))
                v.sem_inc(z_done, 1)

            def rests_of(half):
                z, s = zb[half], sp_[half]
                new = slice(32 * half, 32 * half + 32)
                v.wait_ge(ln_done, half + 1)
                D(v, v.scalar_tensor_tensor(s[:, :], z[:, :], 0.0, s[:, :], ALU.max, ALU.add))
                D(v, v.tensor_tensor(s[:, PAST_LEN:NK], s[:, PAST_LEN:NK], K["bnew"][:, new], ALU.mult))
                D(v, v.tensor_tensor_scan(s[:, ::-1], ones[:, :], s[:, ::-1], 0.0, ALU.mult, ALU.add))
                D(v, v.tensor_tensor(z[:, :], z[:, :], s[:, :], ALU.subtract))
                v.tensor_tensor(z[:, PAST_LEN:NK], z[:, PAST_LEN:NK], K["bnewneg"][:, new], ALU.add).then_inc(r_done, 1)

            for i in range(1, NKR, 2):
                take(v, v.tensor_copy, i, takeD)
                if i == 4 * 9 + 1:
                    scores_of(0)
                if i == 4 * 11 + 1:
                    rests_of(0)
            scores_of(1)
            rests_of(1)
            for half in range(2):
                for i in range(NKR + 3 * half, NKR + 3 * half + 3):
                    if i % 2 == 1:
                        take(v, v.tensor_copy, i, takeD)
                v.wait_ge(y_mm, 4 * (half + 1))
                if half:
                    v.wait_ge(f_mm, 1)
                v.tensor_tensor(own[:, :].rearrange("p (h d) -> p h d", d=HD), ps[:, 2 * half, :].rearrange("p (h d) -> p h d", d=HD),
                                K["rowhead"][:, :].unsqueeze(2).to_broadcast([P, 8, HD]), ALU.mult).then_inc(own_done, 1)
    c2.close()


def stage_windows(nc, c, e):
    ps, K, yc = e.ps, e.K, e.yc
    G, CH = C_GROUPS, C_HEADS
    kTn = e.sb("ck_new_t", [P, G * 3, NDEC], c=c)
    vn = e.sb("cv_new", [NDEC, G, C_WIDTH], c=c)
    qcb = e.sb("cq_blocks", [P, G, 3, DEC_BATCH, 32], c=c)
    c1 = ExitStack()
    qT, kT = e.sb("cq", [P, G * 3, NT], c=c1), e.sb("ck", [P, G * 3, NT], c=c1)
    cv = e.sb("cv", [P, G, 5, C_WIDTH], c=c1)
    c2 = ExitStack()
    raw = e.sb("c_raw", [P, 5, C_WIDTH], c=c2)
    swp = e.sb("c_swapped", [P, 5, C_WIDTH], c=c2)
    rot = [e.sb(f"c_rot{i}", [P, 5, C_WIDTH], c=c2) for i in range(2)]
    nw = e.sb("c_norm_w", [P, 2, HD], c=c2)
    tab = e.sb("c_tables", [P, 2, 2, 5, HD], c=c2)
    ssq = e.sb("c_ssq", [P, 5 * CH], c=c2)
    nw_in, clr, raw_done, sq_done, ss_done, root, rot_done, rot_sum, t_mm, t_done, v_done, raw_free, k_stored = [
        e.sem("c_" + s) for s in ("norm_in", "clear", "raw", "square", "sumsq", "root", "rot", "rot_sum", "t_mm", "t", "v",
                                  "raw_free", "k_stored")]

    def store_new(sp, g, kv, prompt_src, sample_src):
        stored = None if kv else k_stored
        keep = min(WINDOWS[g], SEQ)
        tiles = keep // P
        d = e.O[f"c{g + 1}_kv_prompt"][e.l, 0][:, kv].rearrange("(i p) h d -> p i (h d)", p=P)
        e.store(sp, d, prompt_src[:, TT - tiles:TT, :], stored)
        rows = e.O[f"c{g + 1}_kv_sample"].shape[2]
        for b in range(DEC_BATCH):
            d = e.O[f"c{g + 1}_kv_sample"][e.l, b][rows - DEC_SEQ:rows, kv].rearrange("t h d -> t (h d)")
            e.store(sp, d, sample_src[4 * b:4 * b + 4, :], stored)

    with nc.Block() as block:
        @block.sync
        def _(sp):
            sp.dma_start(nw[:, 0, :], e.L["c_qnorm"].partition_broadcast(P)).then_inc(nw_in, 16)
            sp.dma_start(nw[:, 1, :], e.L["c_knorm"].partition_broadcast(P)).then_inc(nw_in, 16)
            for g in range(G):
                e.prefetch(sp, f"proj_c{g}")
                sp.wait_ge(rot_done, 2 * g + 2)
                store_new(sp, g, 0, rot[1], rot[1][:, 4, :])
                sp.wait_ge(v_done, g + 1)
                store_new(sp, g, 1, cv[:, g], cv[:, g, 4])
            sp.wait_ge(k_stored, 16 * (1 + DEC_BATCH) * G)
            e.stores_done(sp)

        @block.tensor
        def _(pe):
            def turn(n):
                pe.wait_ge(rot_done, n + 1)
                for i, (t0, m) in enumerate(TOK_TILES):
                    u = 5 * n + i
                    if u >= 2:
                        pe.wait_ge(t_done, u - 1)
                    for j in range(3):
                        last = pe.transpose(ps[:, 4 + u % 2, j * P:j * P + m], rot[n % 2][0:m, i, j * P:(j + 1) * P],
                                            e.ident[0:m, 0:m])
                    last.then_inc(t_mm, 1)

            for g in range(G):
                n0 = PLAN[f"proj_c{g}"][0]
                for which in range(3):
                    for n in (n0 + 2 * which, n0 + 2 * which + 1):
                        e.token_products(pe, e.weights(pe, n), CHUNKS[n][2], e.xnT)
                    if which:
                        turn(2 * g + which - 1)

        @block.scalar
        def _(a):
            a.wait_ge(clr, 1)

            def take_turned(n):
                g, dst = n // 2, (qT, kT)[n % 2]
                for i, (t0, m) in enumerate(TOK_TILES):
                    u = 5 * n + i
                    a.wait_ge(t_mm, u + 1)
                    src = ps[:, 4 + u % 2, 0:3 * P].rearrange("p (j t) -> p j t", j=3)[:, :, 0:m]
                    a.mul(dst[:, 3 * g:3 * g + 3, t0:t0 + m], src, QK_SCALE if n % 2 == 0 else 1.0).then_inc(t_done, 1)

            for g in range(G):
                for which in range(3):
                    n = 2 * g + which
                    if which < 2 and n:
                        a.wait_ge(raw_free, n)
                    for c0, w in ((0, CW), (CW, C_WIDTH - CW)):
                        for i, (t0, m) in enumerate(TOK_TILES):
                            o = e.unit_wait(a)
                            dst = (raw if which < 2 else cv[:, g])[0:m, i, c0:c0 + w]
                            a.copy(dst, o[0:m, 0, 0:w]).then_inc(e.taken(), 1)
                    e.wait_taken(a, e.unit["take"] - 1)
                    if which < 2:
                        a.sem_inc(raw_done, 1)
                        if n:
                            a.wait_ge(rot_sum, n)
                        a.activation(swp[:, :, :], raw[:, :, :], ACT.Square).then_inc(sq_done, 1)
                        a.wait_ge(ss_done, n + 1)
                        a.activation(ssq[:, :], ssq[:, :], ACT.Sqrt).then_inc(root, 1)
                    else:
                        a.sem_inc(v_done, 1)
                    if which:
                        take_turned(2 * g + which - 1)

        @block.vector
        def _(v):
            D = e.cD
            v.memset(raw[:, 4, :], 0.0).then_inc(clr, 1)
            v.wait_ge(nw_in, 32)
            for w in range(2):
                for i in range(5):
                    same = K["rot_same"][:, i * HD:(i + 1) * HD]
                    swap = K["rot_swap"][:, i * HD:(i + 1) * HD]
                    v.tensor_tensor(tab[:, w, 0, i], same, nw[:, w, :], ALU.mult)
                    v.tensor_tensor(tab[:, w, 1, i, 0:32], swap[:, 0:32], nw[:, w, 32:64], ALU.mult)
                    D(v, v.tensor_tensor(tab[:, w, 1, i, 32:64], swap[:, 32:64], nw[:, w, 0:32], ALU.mult))
            for n in range(2 * G):
                w, r = n % 2, rot[n % 2]
                heads = lambda x: x.rearrange("p i (h d) -> p i h d", d=HD)
                v.wait_ge(sq_done, n + 1)
                D(v, v.tensor_reduce(ssq[:, :], swp[:, :, :].rearrange("p i (h d) -> p (i h) d", d=HD), AX_X, ALU.add))
                v.tensor_scalar(ssq[:, :], ssq[:, :], 1.0 / HD, NORM_EPS, ALU.mult, ALU.add).then_inc(ss_done, 1)
                if n >= 2:
                    v.wait_ge(t_mm, 5 * (n - 1))
                    if w == 1:
                        v.wait_ge(k_stored, 16 * (1 + DEC_BATCH) * (n // 2))
                tb = lambda k, lo, hi: tab[:, w, k, :, lo:hi].unsqueeze(2).to_broadcast([P, 5, CH, hi - lo])
                v.tensor_tensor(heads(r[:, :, :]), heads(raw[:, :, :]), tb(0, 0, HD), ALU.mult)
                v.tensor_tensor(heads(swp[:, :, :])[:, :, :, 0:32], heads(raw[:, :, :])[:, :, :, 32:64], tb(1, 0, 32), ALU.mult)
                v.tensor_tensor(heads(swp[:, :, :])[:, :, :, 32:64], heads(raw[:, :, :])[:, :, :, 0:32], tb(1, 32, 64),
                                ALU.mult).then_inc(raw_free, 1)
                v.wait_ge(raw_free, n + 1)
                v.tensor_tensor(r[:, :, :], r[:, :, :], swp[:, :, :], ALU.add).then_inc(rot_sum, 1)
                v.wait_ge(rot_sum, n + 1)
                v.wait_ge(root, n + 1)
                D(v, v.reciprocal(ssq[:, :], ssq[:, :]))
                r3 = r[:, :, :].rearrange("p i (h d) -> p (i h) d", d=HD)
                v.tensor_tensor(r3, r3, ssq[:, :].unsqueeze(2).to_broadcast([P, 5 * CH, HD]), ALU.mult).then_inc(rot_done, 1)
                v.wait_ge(rot_done, n + 1)
    c2.close()

    c2 = ExitStack()
    S = [e.sb(f"cs{i}", [P, 10, P], c=c2) for i in range(2)]
    PT = e.sb("c_pt", [P, 10, P], c=c2)
    yt = e.sb("c_ytok", [P, 2, C_WIDTH], c=c2)
    nmax, den, rden = [e.sb("c_" + n, [P, 2], c=c2) for n in ("nmax", "den", "rden")]
    (s_mm, s_take, mx_done, p_done, rd_done, p_mm, takeA, takeD, y_mm, y_take, new_done) = [e.sem("cp_" + s) for s in
        ("s_mm", "s_take", "max", "p", "rden", "p_mm", "take_a", "take_d", "y_mm", "y_take", "new")]
    units = [(qt, h) for qt in range(TT) for h in range(CH)]

    def keys(qt):
        return [(1, k) for k in range(qt + 1)] + [(2, k) for k in range(qt + 1)] + [(0, k) for k in range(max(qt - 1, 0), qt + 1)]

    rounds = []
    for n, (qt, h) in enumerate(units):
        nb = len(keys(qt))
        rounds += [("p", n, b, min(4, nb - b)) for b in range(0, nb, 4)]
        if h == CH - 1:
            rounds.append(("y", n, 0, 3))
    first_round, last_round, y_round = {}, {}, {}
    for i, (kind, n, b, k) in enumerate(rounds):
        if kind == "p":
            first_round.setdefault(n, i)
            last_round[n] = i
        else:
            y_round[units[n][0]] = i

    def take_round(eng, copy, i, sem):
        kind, n, b, k = rounds[i]
        eng.wait_ge(p_mm, i + 1)
        if kind == "p":
            if n:
                eng.wait_ge(y_mm, n)
            dst = PT[:, b:b + k, :]
        else:
            dst = yc[:, :, units[n][0] * P:(units[n][0] + 1) * P]
        copy(dst, ps[:, 6 + i % 2, 0:k * P].rearrange("p (k t) -> p k t", k=k)).then_inc(sem, 1)

    with nc.Block() as block:
        @block.sync
        def _(sp):
            pass

        @block.tensor
        def _(pe):
            def scores(n):
                qt, h = units[n]
                R, b0 = slice(64 * (h % 2), 64 * (h % 2) + 64), 3 * (n % 2)
                if n >= 2:
                    pe.wait_ge(s_take, n - 1)
                    pe.wait_ge(y_take, n - 1)
                for bank, g in enumerate((1, 2, 0)):
                    k0 = max(qt - 1, 0) if g == 0 else 0
                    last = pe.matmul(ps[:, b0 + bank, 0:(qt + 1 - k0) * P], qT[R, 3 * g + h // 2, qt * P:(qt + 1) * P],
                                     kT[R, 3 * g + h // 2, k0 * P:(qt + 1) * P], start=True, stop=True)
                last.then_inc(s_mm, 1)

            def turn(i):
                kind, n, b, k = rounds[i]
                if i >= 2:
                    pe.wait_ge((takeA, takeD)[i % 2], i // 2)
                for j in range(k):
                    src = S[n % 2][:, b + j, :] if kind == "p" else yt[:, units[n][0] % 2, j * P:(j + 1) * P]
                    last = pe.transpose(ps[:, 6 + i % 2, j * P:(j + 1) * P], src, e.ident[:, :])
                last.then_inc(p_mm, 1)

            scores(0)
            for n, (qt, h) in enumerate(units):
                if n + 1 < len(units):
                    scores(n + 1)
                pe.wait_ge(p_done, n + 1)
                for i in range(first_round[n], last_round[n] + 1):
                    turn(i)
                for s, count in ((takeA, last_round[n] // 2 + 1), (takeD, (last_round[n] + 1) // 2)):
                    if count:
                        pe.wait_ge(s, count)
                kb = keys(qt)
                for j, (g, k) in enumerate(kb):
                    last = pe.matmul(ps[:, 3 * (n % 2) + 2, 256:256 + HD], PT[:, j, :], cv[:, g, k, h * HD:(h + 1) * HD],
                                     start=(j == 0), stop=(j == len(kb) - 1))
                last.then_inc(y_mm, 1)
                if h == CH - 1:
                    pe.wait_ge(y_take, n + 1)
                    turn(y_round[qt])

        @block.scalar
        def _(a):
            for n, (qt, h) in enumerate(units):
                nb = len(keys(qt))
                a.wait_ge(mx_done, n + 1)
                a.activation(S[n % 2][:, 0:nb, :], S[n % 2][:, 0:nb, :], ACT.Exp, bias=nmax[:, n % 2:n % 2 + 1],
                             accum_out=den[:, n % 2:n % 2 + 1]).then_inc(p_done, 1)
                for i in range(first_round[n], last_round[n] + 1):
                    if i % 2 == 0:
                        take_round(a, a.copy, i, takeA)
                a.wait_ge(y_mm, n + 1)
                a.wait_ge(rd_done, n + 1)
                if h == 0 and qt >= 2:
                    a.wait_ge(p_mm, y_round[qt - 2] + 1)
                a.activation(yt[:, qt % 2, h * HD:(h + 1) * HD], ps[:, 3 * (n % 2) + 2, 256:256 + HD], ACT.Copy,
                             scale=rden[:, n % 2:n % 2 + 1]).then_inc(y_take, 1)
                if h == CH - 1 and y_round[qt] % 2 == 0:
                    take_round(a, a.copy, y_round[qt], takeA)

        @block.vector
        def _(v):
            v.memset(qcb[:, :, :, :, :], 0.0).then_inc(new_done, 1)
            v.tensor_copy(kTn[:, :, :], kT[:, :, SEQ:NT])
            v.tensor_copy(vn[:, :, :], cv[0:NDEC, :, 4, :])
            v.wait_ge(new_done, 1)
            for g in range(G):
                for p in range(3):
                    for hh in range(2):
                        R = slice(64 * hh, 64 * hh + 64)
                        o = (2 * p + hh) * 4
                        v.tensor_copy(qcb[R, g, p, :, o:o + 4], qT[R, 3 * g + p, SEQ:NT].rearrange("p (b t) -> p b t", t=4))

            def maxima(n):
                qt, h = units[n]
                s, b0, nq = S[n % 2], 3 * (n % 2), qt + 1
                v.wait_ge(s_mm, n + 1)
                if n >= 2:
                    v.wait_ge(p_mm, last_round[n - 2] + 1)
                cm = K["cmask"][:, :].rearrange("p (k t) -> p k t", t=P)
                blk = lambda bank, k: ps[:, b0 + bank, 0:k * P].rearrange("p (k t) -> p k t", t=P)
                v.tensor_tensor(s[:, 0:nq, :], blk(0, nq), cm[:, 4 - nq:4, :], ALU.add)
                v.tensor_tensor(s[:, nq:2 * nq, :], blk(1, nq), cm[:, 8 - nq:8, :], ALU.add)
                n1 = min(nq, 2)
                v.tensor_tensor(s[:, 2 * nq:2 * nq + n1, :], blk(2, n1), cm[:, 10 - n1:10, :], ALU.add).then_inc(s_take, 1)
                v.wait_ge(s_take, n + 1)
                v.tensor_reduce(nmax[:, n % 2:n % 2 + 1], s[:, 0:2 * nq + n1, :].rearrange("p k t -> p (k t)"), AX_X, ALU.max,
                                negate=True).then_inc(mx_done, 1)

            maxima(0)
            for n, (qt, h) in enumerate(units):
                if n + 1 < len(units):
                    maxima(n + 1)
                v.wait_ge(p_done, n + 1)
                v.reciprocal(rden[:, n % 2:n % 2 + 1], den[:, n % 2:n % 2 + 1]).then_inc(rd_done, 1)
                for i in range(first_round[n], last_round[n] + 1):
                    if i % 2 == 1:
                        take_round(v, v.tensor_copy, i, takeD)
                if h == CH - 1 and y_round[qt] % 2 == 1:
                    take_round(v, v.tensor_copy, y_round[qt], takeD)
    c2.close()
    c1.close()

    NSLOT = 4
    NK = 896
    c2 = ExitStack()
    slots = [e.sb(f"c_rows{i}", [P, 9, C_WIDTH], c=c2) for i in range(NSLOT)]
    keysT = e.sb("c_keys_t", [P, 3, NK], c=c2)
    Sd = [e.sb(f"c_scores{i}", [P, 992], c=c2) for i in range(2)]
    PTd = e.sb("c_weights_t", [P, 12, P], c=c2)
    st = e.sb("c_stats", [P, 2, 3], c=c2)
    own = e.sb("c_own_head", [P, C_WIDTH], c=c2)
    (k_mm, takeA, takeD, s_mm, mx_done, p_done, n_done, y_mm, own_done, f_mm, f_done) = [e.sem("cd_" + s) for s in
        ("k_mm", "take_a", "take_d", "s_mm", "max", "p", "norm", "y_mm", "own", "f_mm", "f")]
    rows_in = [e.sem(f"cd_rows_in{i}") for i in range(NSLOT)]
    items = [(kv, b) for kv in range(2) for b in range(DEC_BATCH)]
    KR = [("k", 0, None)] + [("k", 1, p) for p in range(3)] + [("k", 2, p) for p in range(3)]
    PR = [("w", 0, (0, 1, P, 0)), ("w", 1, (1, 4, 64, 128)), ("w", 2, (5, 3, NDEC, 384)), ("w", 3, (8, 4, P, 480))]
    drounds = [(r, b) for b in range(DEC_BATCH) for r in KR] + [(r, half) for half in range(2) for r in PR]
    NKR = len(KR)

    def take(eng, copy, i, sem):
        (kind, which, arg), x = drounds[i]
        bank = ps[:, 6 + i % 2, :]
        eng.wait_ge(k_mm, i + 1)
        if kind == "k":
            if x:
                eng.wait_ge(s_mm, x)
            if which == 0:
                copy(keysT[:, :, 0:P], bank[:, 0:3 * P].rearrange("p (j t) -> p j t", j=3)).then_inc(sem, 1)
            elif which == 1:
                copy(keysT[:, arg, 128:640], bank).then_inc(sem, 1)
            else:
                copy(keysT[:, arg, 640:896], bank[:, 0:256]).then_inc(sem, 1)
        else:
            b0, k, m, _ = arg
            if x:
                eng.wait_ge(y_mm, 4)
            copy(PTd[0:m, b0:b0 + k, :], bank[0:m, 0:k * P].rearrange("p (k t) -> p k t", k=k)).then_inc(sem, 1)

    with nc.Block() as block:
        @block.sync
        def _(sp):
            for i, (kv, b) in enumerate(items):
                if i >= NSLOT:
                    last_kv, last_b = items[i - NSLOT]
                    if last_kv:
                        sp.wait_ge(y_mm, last_b + 1)
                    else:
                        sp.wait_ge(k_mm, NKR * (last_b + 1))
                s, sm = slots[i % NSLOT], rows_in[i % NSLOT]
                sp.dma_start(s[:, 0, :], e.L["cache_c1_kv"][b, :, kv].rearrange("r h d -> r (h d)")).then_inc(sm, 16)
                sp.dma_start(s[:, 1:5, :], e.L["cache_c2_kv"][b, :, kv].rearrange("(j r) h d -> j r (h d)", r=4)).then_inc(sm, 16)
                sp.dma_start(s[0:64, 5:9, :], e.L["cache_c3_kv"][b, :, kv].rearrange("(j r) h d -> j r (h d)", r=16)[:, 0:4]).then_inc(sm, 16)

        @block.tensor
        def _(pe):
            def wait_bank(i):
                if i >= 2:
                    pe.wait_ge((takeA, takeD)[i % 2], i // 2)

            def wait_rounds(n):
                pe.wait_ge(takeA, (n + 1) // 2)
                pe.wait_ge(takeD, n // 2)

            for b in range(DEC_BATCH):
                s = slots[b % NSLOT]
                pe.wait_ge(rows_in[b % NSLOT], 48 * (b // NSLOT + 1))
                for r, (_, which, p) in enumerate(KR):
                    i = NKR * b + r
                    wait_bank(i)
                    o = ps[:, 6 + i % 2, :]
                    if which == 0:
                        for j in range(3):
                            last = pe.transpose(o[:, j * P:(j + 1) * P], s[:, 0, j * P:(j + 1) * P], e.ident[:, :])
                    elif which == 1:
                        for j in range(4):
                            last = pe.transpose(o[:, j * P:(j + 1) * P], s[:, 1 + j, p * P:(p + 1) * P], e.ident[:, :])
                    else:
                        for j in range(4):
                            last = pe.transpose(o[:, j * 64:(j + 1) * 64], s[0:64, 5 + j, p * P:(p + 1) * P], e.ident[0:64, 0:64])
                    last.then_inc(k_mm, 1)
                wait_rounds(NKR * (b + 1))
                R, half = slice(32 * (b % 4), 32 * (b % 4) + 32), b // 4
                for bank, c0, w, g, k0 in [(0, 0, P, 0, 0), (0, 128, 256, 2, 640), (1, 0, 512, 1, 128)] + [
                        (0, 384 + 32 * g, 32, g, None) for g in range(3)]:
                    for p in range(3):
                        x = keysT[:, p, k0:k0 + w] if k0 is not None else kTn[:, 3 * g + p, :]
                        last = pe.matmul(ps[R, 2 * half + bank, c0:c0 + w], qcb[:, g, p, b, :], x, start=(p == 0), stop=(p == 2))
                last.then_inc(s_mm, 1)
            for half in range(2):
                pe.wait_ge(n_done, half + 1)
                for r, (_, _, (b0, k, m, c0)) in enumerate(PR):
                    i = NKR * DEC_BATCH + 4 * half + r
                    wait_bank(i)
                    for j in range(k):
                        last = pe.transpose(ps[0:m, 6 + i % 2, j * P:(j + 1) * P], Sd[half][:, c0 + j * m:c0 + (j + 1) * m], e.ident[:, :])
                    last.then_inc(k_mm, 1)
                wait_rounds(NKR * DEC_BATCH + 4 * (half + 1))
                for b in range(4 * half, 4 * half + 4):
                    i = DEC_BATCH + b
                    s = slots[i % NSLOT]
                    pe.wait_ge(rows_in[i % NSLOT], 48 * (i // NSLOT + 1))
                    R = slice(32 * (b % 4), 32 * (b % 4) + 32)
                    o = ps[R, 4 + half, 0:C_WIDTH]
                    pe.matmul(o, PTd[:, 0, R], s[:, 0, :], start=True, stop=False)
                    for j in range(4):
                        pe.matmul(o, PTd[:, 8 + j, R], s[:, 1 + j, :], start=False, stop=False)
                    for j in range(4):
                        pe.matmul(o, PTd[0:64, 1 + j, R], s[0:64, 5 + j, :], start=False, stop=False)
                    for g in range(3):
                        last = pe.matmul(o, PTd[0:NDEC, 5 + g, R], vn[:, g, :], start=False, stop=(g == 2))
                    last.then_inc(y_mm, 1)
                pe.wait_ge(own_done, half + 1)
                for p in range(3):
                    last = pe.matmul(ps[:, 2 * half, 16 * p:16 * p + 16], own[:, p * P:(p + 1) * P], K["rowtoken"][:, :], start=True, stop=True)
                last.then_inc(f_mm, 1)

        K0 = NKR * DEC_BATCH

        @block.scalar
        def _(a):
            for i in range(0, K0, 2):
                take(a, a.copy, i, takeA)
                if i == 42 or i == 54:
                    half = 0 if i == 42 else 1
                    a.wait_ge(mx_done, half + 1)
                    a.activation(Sd[half][:, :], Sd[half][:, :], ACT.Exp, bias=st[:, half, 0:1], accum_out=st[:, half, 1:2]).then_inc(p_done, 1)
            for half in range(2):
                for i in range(K0 + 4 * half, K0 + 4 * half + 4, 2):
                    take(a, a.copy, i, takeA)
                a.wait_ge(f_mm, half + 1)
                a.copy(yc[:, :, SEQ + 16 * half:SEQ + 16 * half + 16],
                       ps[:, 2 * half, 0:48].rearrange("p (a t) -> p a t", a=3)).then_inc(f_done, 1)

        @block.vector
        def _(v):
            D = e.cD

            def maxima(half):
                s = Sd[half]
                v.wait_ge(s_mm, 4 * (half + 1))
                v.tensor_tensor(s[:, 0:384], ps[:, 2 * half, 0:384], K["dmask"][:, :], ALU.add)
                v.tensor_tensor(s[:, 384:480], ps[:, 2 * half, 384:480], K["dnew"][:, 96 * half:96 * half + 96], ALU.add)
                D(v, v.tensor_tensor(s[:, 480:992], ps[:, 2 * half + 1, :], K["dmask2"][:, :], ALU.add))
                v.tensor_reduce(st[:, half, 0:1], s[:, :], AX_X, ALU.max, negate=True).then_inc(mx_done, 1)

            def normalise(half):
                v.wait_ge(p_done, half + 1)
                D(v, v.reciprocal(st[:, half, 2:3], st[:, half, 1:2]))
                v.tensor_scalar(Sd[half][:, :], Sd[half][:, :], st[:, half, 2:3], None, ALU.mult).then_inc(n_done, 1)

            for i in range(1, K0, 2):
                if i == 31:
                    maxima(0)
                take(v, v.tensor_copy, i, takeD)
            maxima(1)
            for half in range(2):
                normalise(half)
                for i in range(K0 + 4 * half + 1, K0 + 4 * half + 4, 2):
                    take(v, v.tensor_copy, i, takeD)
                v.wait_ge(y_mm, 4 * (half + 1))
                if half:
                    v.wait_ge(f_mm, 1)
                v.tensor_tensor(own[:, :].rearrange("p (h d) -> p h d", d=HD), ps[:, 4 + half, 0:C_WIDTH].rearrange("p (h d) -> p h d", d=HD),
                                K["rowhead"][:, 0:CH].unsqueeze(2).to_broadcast([P, CH, HD]), ALU.mult).then_inc(own_done, 1)
    c2.close()


def stage_output(nc, c, e):
    ps = e.ps
    branches = [(e.ya, 4), (e.yb, 4), (e.yc, 3)]
    merged = e.sb("merged", [P, KT, NT], c=c)
    xres = e.sb("x_res", [P, 5, D_MODEL], c=c)
    gate = e.sb("gate", [P, 2, NT], c=c)
    tmp = e.sb("tmp", [P, 2, NT], c=c)
    x_in, gated, merge_done = [e.sem("o_" + s) for s in ("x_in", "gated", "merged")]
    halves = lambda x: x.rearrange("p (h t) -> p h t", h=2)
    unit = e.unit
    u0 = unit["take"]
    with nc.Block() as block:
        @block.sync
        def _(sp):
            for i, (t0, m) in enumerate(TOK_TILES):
                sp.dma_start(xres[0:m, i, :], e.y_rows[i]).then_inc(x_in, 16)
            for s in ("gate", "merge", "out"):
                e.prefetch(sp, s)
            for i, (t0, m) in enumerate(TOK_TILES):
                e.wait_taken(sp, u0 + 11 + 48 + 15 + i)
                e.store(sp, e.y_rows[i], xres[0:m, i, :])
            e.stores_done(sp)

        @block.tensor
        def _(pe):
            for n in range(*PLAN["gate"]):
                e.channel_products(pe, e.weights(pe, n), CHUNKS[n][2], KT, e.xnT)
            pe.wait_ge(gated, 11)
            a0, a1 = PLAN["merge"]
            for n in range(a0, a1):
                i = (n - a0) % 6
                rhs = branches[i // 2][0] if i % 2 else e.xnT
                e.channel_products(pe, e.weights(pe, n), CW, CHUNKS[n][3], rhs)
            pe.wait_ge(merge_done, 8)
            for n in range(*PLAN["out"]):
                e.token_products(pe, e.weights(pe, n), CW, merged)

        @block.scalar
        def _(a):
            def take(u, func):
                a.wait_ge(e.products_done, u + 1)
                a.activation(halves(gate[:, u % 2]), e.pair(u)[:, :, 0:HALF], func).then_inc(e.products_taken[u % 2], 1)

            for j in range(11):
                if j >= 2:
                    a.wait_ge(gated, j - 1)
                take(u0 + j, ACT.Silu)
            a.wait_ge(gated, 11)
            for u in range(u0 + 11, u0 + 11 + 48, 4):
                take(u, ACT.Sigmoid)
                take(u + 1, ACT.Sigmoid)

        @block.vector
        def _(v):
            D = e.cD
            for j in range(11):
                u = u0 + j
                y = (e.ya[:, j] if j < 4 else e.yb[:, j - 4] if j < 8 else e.yc[:, j - 8])
                v.wait_ge(e.products_taken[u % 2], u // 2 + 1)
                v.tensor_tensor(y, y, gate[:, u % 2], ALU.mult).then_inc(gated, 1)
            u = u0 + 11
            for jj in range(4):
                for i in range(3):
                    for s in range(2):
                        m = merged[:, 2 * jj + s]
                        b = u + 2 + s
                        v.wait_ge(e.products_taken[(u + s) % 2], (u + s) // 2 + 1)
                        v.wait_ge(e.products_done, b + 1)
                        dst = m if i == 0 else tmp[:, s]
                        v.tensor_tensor(halves(dst), e.pair(b)[:, :, 0:HALF], halves(gate[:, b % 2]), ALU.mult).then_inc(e.products_taken[b % 2], 1)
                        if i:
                            v.wait_ge(e.products_taken[b % 2], b // 2 + 1)
                            ins = v.tensor_tensor(m, m, tmp[:, s], ALU.add)
                            if i == 2:
                                ins.then_inc(merge_done, 1)
                            else:
                                D(v, ins)
                    u += 4
            v.wait_ge(x_in, 16 * 5)
            for q in range(D_MODEL // CW):
                for i, (t0, m) in enumerate(TOK_TILES):
                    v.wait_ge(e.products_done, u + 1)
                    xr = xres[0:m, i, q * CW:(q + 1) * CW]
                    v.tensor_tensor(xr, xr, e.pair(u)[0:m, 0, 0:CW], ALU.add).then_inc(e.products_taken[u % 2], 1)
                    u += 1
            unit["take"] = u


STAGES = [stage_norm, stage_rwkv, stage_stick_breaking, stage_windows, stage_output]


_INS = ['x_prompt', 'x_sample', 'state_a_wkv', 'state_a_shift', 'cache_b_k', 'cache_b_v', 'cache_c1_kv', 'cache_c2_kv',
        'cache_c3_kv', 'page_table', 'norm_w', 'w_in', 'a_mu', 'a_w0', 'a_w2', 'a_a0', 'a_a2', 'a_kk', 'a_ka', 'a_rk',
        'a_gn_w', 'a_gn_b', 'b_bias', 'c_qnorm', 'c_knorm', 'w_br_a', 'w_br_b', 'w_br_c', 'w_out']
_OUTS = [('y_prompt', (1, 512, 1024)), ('y_sample', (8, 4, 1024)), ('a_wkv_prompt', (2, 1, 8, 64, 64)),
         ('a_wkv_sample', (2, 8, 8, 64, 64)), ('a_shift_prompt', (2, 1, 1664)), ('a_shift_sample', (2, 8, 1664)),
         ('b_k_prompt', (2, 1, 512, 8, 64)), ('b_v_prompt', (2, 1, 512, 8, 64)), ('b_k_sample', (2, 8, 4, 8, 64)),
         ('b_v_sample', (2, 8, 4, 8, 64)), ('c1_kv_prompt', (2, 1, 128, 2, 6, 64)), ('c1_kv_sample', (2, 8, 128, 2, 6, 64)),
         ('c2_kv_prompt', (2, 1, 512, 2, 6, 64)), ('c2_kv_sample', (2, 8, 512, 2, 6, 64)),
         ('c3_kv_prompt', (2, 1, 512, 2, 6, 64)), ('c3_kv_sample', (2, 8, 1028, 2, 6, 64))]


def kernel(**inputs):
    import numpy as _np
    import concourse.bacc as _bacc
    from concourse import mybir as _mybir
    from concourse.bass_utils import run_bass_kernel_spmd as _run

    nc = _bacc.Bacc("TRN2", target_bir_lowering=False, num_devices=1)
    arrays, ins, outs = {}, {}, {}
    for name in _INS:
        a = _np.ascontiguousarray(inputs[name])
        arrays[f"in_{name}_dram"] = a
        ins[name] = nc.dram_tensor(f"in_{name}_dram", a.shape, _mybir.dt.from_np(a.dtype), kind="ExternalInput").ap()
    for name, a in host_constants().items():
        arrays[f"const_{name}_dram"] = a
        ins[name] = nc.dram_tensor(f"const_{name}_dram", a.shape, _mybir.dt.from_np(a.dtype), kind="ExternalInput").ap()
    for name, shape in _OUTS:
        outs[name] = nc.dram_tensor(f"out_{name}_dram", shape, F32, kind="ExternalOutput").ap()
    build(nc, ins, outs)
    r = _run(nc, [arrays], core_ids=[0])
    return tuple(r.results[0][f"out_{name}_dram"] for name, _ in _OUTS)
```

```python
from contextlib import ExitStack

import numpy as np

import concourse.bass as bass
from concourse import mybir

F32 = mybir.dt.float32
F32R = mybir.dt.float32r
I32 = mybir.dt.int32
ALU = mybir.AluOpType
ACT = mybir.ActivationFunctionType
AX_X = mybir.AxisListType.X

P = 128
D_MODEL, SEQ, DEPTH = 1024, 512, 2
DEC_BATCH, DEC_SEQ, PAST_LEN, PAGE = 8, 4, 1024, 128
HD = 64
A_HEADS, B_HEADS, C_HEADS, C_GROUPS = 8, 8, 6, 3
A_WIDTH, B_WIDTH, C_WIDTH = 512, 512, 384
C_QKV = C_GROUPS * C_WIDTH
A_SHIFT = 3 * A_WIDTH + 128
WINDOWS, DILATIONS = (128, 512, 2048), (1, 4, 16)
NORM_EPS, A_GN_EPS = 1e-6, 64e-5
QK_SCALE = HD ** -0.5
NDEC = DEC_BATCH * DEC_SEQ
NT = SEQ + NDEC
HALF = NT // 2
KT = D_MODEL // P
TT = SEQ // P
TOK_TILES = [(i * P, P) for i in range(TT)] + [(SEQ, NDEC)]
N_PAGES = PAST_LEN // PAGE
CHUNK = 64
NCHUNK = SEQ // CHUNK
DECAY_RATE = float(np.exp(-0.5))
NEG = -1.0e30

_SIZES = (A_SHIFT, A_WIDTH, 3 * B_WIDTH, B_WIDTH, 3 * C_QKV, C_WIDTH, 3 * D_MODEL)
PA0, ZA0, BQ0, ZB0, CQ0, ZC0, M0 = [sum(_SIZES[:i]) for i in range(7)]
BK0, BV0 = BQ0 + B_WIDTH, BQ0 + 2 * B_WIDTH
CK0, CV0 = CQ0 + C_QKV, CQ0 + 2 * C_QKV

PRM = {}
_row = 0
for _name, _n in (("norm_w", 8), ("a_mu", 13), ("a_w0", 4), ("a_a0", 4), ("a_kk", 4), ("a_ka", 4), ("a_rk", 4),
                  ("a_gn_w", 4), ("a_gn_b", 4)):
    PRM[_name] = (_row, _row + _n)
    _row += _n
N_PRM = _row

CW = 256
RING = 4


def cut(source, col0, width, ktiles=KT):
    return [(source, col0 + c, min(CW, width - c), ktiles) for c in range(0, width, CW)]


PLAN = {}
CHUNKS = []


def plan(stage, chunks):
    PLAN[stage] = (len(CHUNKS), len(CHUNKS) + len(chunks))
    CHUNKS.extend(chunks)


plan("norm", [])
plan("proj_a", cut("w_in", PA0, A_SHIFT))
plan("proj_b", cut("w_in", BQ0, 3 * B_WIDTH))
for _g in range(C_GROUPS):
    plan(f"proj_c{_g}", cut("w_in", CQ0 + _g * C_WIDTH, C_WIDTH) + cut("w_in", CK0 + _g * C_WIDTH, C_WIDTH)
         + cut("w_in", CV0 + _g * C_WIDTH, C_WIDTH))
plan("gate", cut("w_in", ZA0, A_WIDTH) + cut("w_in", ZB0, B_WIDTH) + cut("w_in", ZC0, C_WIDTH))
_out = []
for _j in range(D_MODEL // CW):
    for _i, (_w, _k) in enumerate((("w_br_a", 4), ("w_br_b", 4), ("w_br_c", 3))):
        _out += [("w_in", M0 + _i * D_MODEL + _j * CW, CW, KT), (_w, _j * CW, CW, _k)]
plan("merge", _out)
plan("out", cut("w_out", 0, D_MODEL))


def chunk_units(source, c0, width):
    token_major = source == "w_out" or (source == "w_in" and (BV0 <= c0 < ZB0 or CQ0 <= c0 < ZC0))
    return len(TOK_TILES) if token_major else width // P


UNITS_AFTER = [int(x) for x in np.cumsum([chunk_units(s, c0, w) for s, c0, w, _ in CHUNKS])]


def host_constants():
    t = np.arange(P)
    same = (t[:, None] // CHUNK) == (t[None, :] // CHUNK)
    c = {}
    c["ident"] = np.eye(P)
    c["bones"] = (t[:, None] // HD == t[None, :] // HD)
    c["before"] = same & (t[:, None] < t[None, :])
    c["upto"] = same & (t[:, None] <= t[None, :])
    lv = []
    for b in (1, 2, 4, 8, 16, 32):
        lv.append((t[:, None] // (2 * b) == t[None, :] // (2 * b)) & (t[:, None] // b % 2 == 0) & (t[None, :] // b % 2 == 1))
    c["levels"] = np.stack(lv, 1).reshape(P, -1)
    c["level1"] = lv[0].T
    q = np.arange(NDEC)
    sameb = (q[:, None] // DEC_SEQ) == (q[None, :] // DEC_SEQ)
    pad = lambda m: np.concatenate([m, np.zeros((P - m.shape[0],) + m.shape[1:])])
    c["before4"] = pad(sameb & (q[:, None] < q[None, :]))
    c["upto4"] = pad(sameb & (q[:, None] <= q[None, :]))
    c["rowb"] = pad(q[:, None] // DEC_SEQ == np.arange(DEC_BATCH)[None, :])
    reset = np.ones(NT)
    reset[0:SEQ:CHUNK] = 0
    reset[SEQ::DEC_SEQ] = 0
    c["reset"] = np.broadcast_to(reset, (P, NT))
    colb = np.zeros((DEC_BATCH, NDEC))
    for b in range(DEC_BATCH):
        colb[b, b * DEC_SEQ:(b + 1) * DEC_SEQ] = 1
    c["colb"] = np.broadcast_to(colb.reshape(-1), (P, DEC_BATCH * NDEC))
    c["tri"] = -(t[:, None] >= t[None, :]).astype(np.float32)
    c["allneg"] = -np.ones((P, P))
    r = np.arange(P)
    c["rowhead"] = (r[:, None] % 32) // DEC_SEQ == np.arange(8)[None, :]
    c["rowtoken"] = (r[:, None] // 32 * DEC_SEQ + r[:, None] % DEC_SEQ) == np.arange(4 * DEC_SEQ)[None, :]
    seen = [(r[:, None] // 32 + 4 * half == q[None, :] // DEC_SEQ) & (q[None, :] % DEC_SEQ < r[:, None] % DEC_SEQ) for half in range(2)]
    c["bnew"] = np.concatenate(seen, 1)
    c["bnewneg"] = np.where(c["bnew"], 0.0, NEG)
    dist = t[:, None] - t[None, :]
    neg = lambda ok: np.where(ok, 0.0, NEG)
    g = [[neg(dist % d == 0)] * 3 + [neg((dist % d == 0) & (dist >= 0))] for d in (4, 16)]
    c["cmask"] = np.concatenate(g[0] + g[1] + [neg(dist <= 0), neg(dist >= 0)], 1)
    r = np.arange(P) % 32
    qt = r % DEC_SEQ
    m1 = neg(np.arange(P)[None, :] >= qt[:, None])
    m2 = neg(np.repeat(np.arange(4), 128)[None, :] == qt[:, None])
    m3 = neg(np.repeat(np.arange(4), 64)[None, :] == qt[:, None])
    c["dmask"] = np.concatenate([m1, m3], 1)
    c["dmask2"] = m2
    new = []
    for half in range(2):
        b = half * 4 + np.arange(P) // 32
        for g_ in range(3):
            own = b[:, None] == q[None, :] // DEC_SEQ
            s = q[None, :] % DEC_SEQ
            new.append(neg(own & ((s <= qt[:, None]) if g_ == 0 else (s == qt[:, None]))))
    c["dnew"] = np.concatenate(new, 1)
    inv = (1.0 / (np.float32(10000.0) ** (np.arange(0, HD, 2, dtype=np.float32) / np.float32(HD)))).astype(np.float32)
    pos = np.zeros((5, P), np.float32)
    pos[:4] = np.arange(SEQ).reshape(4, P)
    pos[4, :NDEC] = PAST_LEN + np.arange(NDEC) % DEC_SEQ
    ang = (pos[:, :, None] * inv).astype(np.float32).transpose(1, 0, 2)
    cos, sin = np.cos(ang.astype(np.float64)), np.sin(ang.astype(np.float64))
    c["rot_same"] = np.concatenate([cos, cos], -1).reshape(P, -1)
    c["rot_swap"] = np.concatenate([-sin, sin], -1).reshape(P, -1)
    return {k: np.ascontiguousarray(v, dtype=np.float32) for k, v in c.items()}


CONST_W = {k: v.shape[1] for k, v in host_constants().items()}


class Chain:

    def __init__(self, sem):
        self.sem, self.n = sem, 0

    def __call__(self, eng, ins):
        self.n += 1
        ins.then_inc(self.sem, 1)
        eng.wait_ge(self.sem, self.n)


class Shared:
    pass


def build(nc, I, O):
    ctx = ExitStack()
    with ctx:
        uid = [0]

        def sb(name, shape, dt=F32, c=ctx):
            uid[0] += 1
            return c.enter_context(nc.sbuf_tensor(f"{name}_{uid[0]}", shape, dt))

        scopes = [(ctx, [])]

        def sem(name):
            scope, sems = scopes[-1]
            s = scope.enter_context(nc.semaphore(name))
            sems.append(s)
            return s

        def clear(sems):
            nc.all_engine_barrier()
            nums = sorted(s.num for s in sems)
            while nums:
                n = 1
                while n < len(nums) and nums[n] == nums[0] + n:
                    n += 1
                nc.sync.sem_clear(range(nums[0], nums[0] + n))
                nums = nums[n:]
            nc.all_engine_barrier()

        K = {k: sb(k, [P, w]) for k, w in CONST_W.items()}
        epsn = sb("epsn", [P, 2])
        xnT = sb("xnT", [P, KT, NT])
        ring = sb("ring", [P, RING, KT, CW])
        ya = sb("ya", [P, 4, NT])
        prm = sb("prm", [P, N_PRM])
        bias_b = sb("bias_b", [P, B_HEADS])
        ps = ctx.enter_context(nc.psum_tensor("ps", [P, 8, 512], F32))
        ident = K["ident"]

        const_in = ctx.enter_context(nc.semaphore("const_in"))
        weights_in = [sem(f"weights_in{i}") for i in range(RING)]
        products_done = sem("products_done")
        products_taken = [sem(f"products_taken{i}") for i in range(2)]
        out_stored = sem("out_stored")
        cD, cA, cG = Chain(sem("vector_step")), Chain(sem("scalar_step")), Chain(sem("gpsimd_step"))
        stores = [0]

        def store(eng, dst, src, stored=None):
            stores[0] += stored is None
            eng.dma_start(dst, src).then_inc(out_stored if stored is None else stored, 16)

        def stores_done(eng):
            eng.wait_ge(out_stored, 16 * stores[0])

        with nc.Block() as block:
            @block.sync
            def _(sp):
                for k in CONST_W:
                    sp.dma_start(K[k][:, :], I[k]).then_inc(const_in, 16)
                sp.dma_start(O["y_prompt"][0], I["x_prompt"][0]).then_inc(const_in, 16)
                sp.dma_start(O["y_sample"].rearrange("b t d -> (b t) d"),
                             I["x_sample"].rearrange("b t d -> (b t) d")).then_inc(const_in, 16)
                sp.wait_ge(const_in, 16 * (len(CONST_W) + 2))

        y_rows = [O["y_prompt"][0][i * P:(i + 1) * P, :] for i in range(TT)] + [O["y_sample"].rearrange("b t d -> (b t) d")]

        loop = ctx.enter_context(nc.Fori(0, DEPTH))
        l = loop
        L = {k: v[l] for k, v in I.items() if len(v.shape) > 1 and v.shape[0] == DEPTH and k not in CONST_W}
        W = {n: L[n].rearrange("(k p) n -> p k n", p=P) for n in ("w_in", "w_br_a", "w_br_b", "w_br_c", "w_out")}

        def load_chunks(sp, first, last):
            for n in range(first, min(last, len(CHUNKS))):
                source, c0, w, kts = CHUNKS[n]
                if n >= RING:
                    sp.wait_ge(products_done, UNITS_AFTER[n - RING])
                sp.dma_start(ring[:, n % RING, 0:kts, 0:w], W[source][:, :, c0:c0 + w]).then_inc(weights_in[n % RING], 16)

        def prefetch(sp, stage):
            a, b = PLAN[stage]
            load_chunks(sp, a + RING, b + RING)

        def weights(pe, n):
            pe.wait_ge(weights_in[n % RING], 16 * (n // RING + 1))
            return ring[:, n % RING]

        unit = {"pe": 0, "take": 0}

        def pair(u):
            return ps[:, 2 * (u % 2):2 * (u % 2) + 2]

        def unit_begin(pe):
            u = unit["pe"]
            unit["pe"] += 1
            if u >= 2:
                pe.wait_ge(products_taken[u % 2], u // 2)
            return pair(u)

        def unit_wait(eng):
            u = unit["take"]
            unit["take"] += 1
            eng.wait_ge(products_done, u + 1)
            return pair(u)

        def taken():
            return products_taken[(unit["take"] - 1) % 2]

        def wait_taken(eng, u):
            for v in (u - 1, u):
                eng.wait_ge(products_taken[v % 2], v // 2 + 1)

        def channel_products(pe, slot, w, kts, rhs):
            for c in range(w // P):
                o = unit_begin(pe)
                for half in range(2):
                    for k in range(kts):
                        last = pe.matmul(o[:, half, 0:HALF], slot[:, k, c * P:(c + 1) * P],
                                         rhs[:, k, half * HALF:(half + 1) * HALF], start=(k == 0), stop=(k == kts - 1))
                last.then_inc(products_done, 1)

        def token_products(pe, slot, w, lhs):
            for t0, m in TOK_TILES:
                o = unit_begin(pe)
                for k in range(KT):
                    last = pe.matmul(o[0:m, 0, 0:w], lhs[:, k, t0:t0 + m], slot[:, k, 0:w], start=(k == 0), stop=(k == KT - 1))
                last.then_inc(products_done, 1)

        class Split:

            def __init__(self, chunks, c):
                self.chunks = chunks
                self.x = [sb(n, [P, KT, NT], F32R, c=c) for n in ("x_hi", "x_lo")]
                self.w = [sb(n, [P, 2, KT, CW], F32R, c=c) for n in ("w_hi", "w_lo")]
                self.x_hi, self.x_lo, self.w_hi, self.w_lo = [sem("split_" + n) for n in ("x_hi", "x_lo", "w_hi", "w_lo")]
                self.x_seen, self.x_times = 0, 1

            def tokens_hi(self, a, src):
                for k in range(KT):
                    a.copy(self.x[0][:, k, :], src[:, k, :]).then_inc(self.x_hi, 1)

            def tokens_lo(self, v, src, times=0):
                for k in range(KT):
                    v.wait_ge(self.x_hi, KT * times + k + 1)
                    v.tensor_tensor(self.x[1][:, k, :], src[:, k, :], self.x[0][:, k, :].bitcast(F32), ALU.subtract).then_inc(self.x_lo, 1)

            def free(self, eng, i):
                if 2 <= i < len(self.chunks):
                    eng.wait_ge(products_done, UNITS_AFTER[self.chunks[i - 2]])

            def weights_hi(self, a, i):
                if i < len(self.chunks):
                    n = self.chunks[i]
                    _, _, w, kts = CHUNKS[n]
                    self.free(a, i)
                    a.copy(self.w[0][:, i % 2, 0:kts, 0:w], weights(a, n)[:, 0:kts, 0:w]).then_inc(self.w_hi, 1)

            def weights_lo(self, v, i):
                if i < len(self.chunks):
                    n = self.chunks[i]
                    _, _, w, kts = CHUNKS[n]
                    self.free(v, i)
                    v.wait_ge(self.w_hi, i + 1)
                    hi = self.w[0][:, i % 2, 0:kts, 0:w].bitcast(F32)
                    v.tensor_tensor(self.w[1][:, i % 2, 0:kts, 0:w], weights(v, n)[:, 0:kts, 0:w], hi, ALU.subtract).then_inc(self.w_lo, 1)

            def terms(self, pe, k):
                if self.x_seen < self.x_times * KT and self.x_seen % KT == k:
                    self.x_seen += 1
                    pe.wait_ge(self.x_lo, self.x_seen)
                return ((0, 0), (1, 0), (0, 1))

            def channel_products(self, pe, n):
                i = self.chunks.index(n)
                pe.wait_ge(self.w_lo, i + 1)
                for c in range(CHUNKS[n][2] // P):
                    o = unit_begin(pe)
                    for half in range(2):
                        for k in range(KT):
                            for j, (x, w) in enumerate(self.terms(pe, k)):
                                last = pe.matmul(o[:, half, 0:HALF], self.w[w][:, i % 2, k, c * P:(c + 1) * P],
                                                 self.x[x][:, k, half * HALF:(half + 1) * HALF],
                                                 start=(k == 0 and j == 0), stop=(k == KT - 1 and j == 2))
                    last.then_inc(products_done, 1)

            def token_products(self, pe, n):
                i = self.chunks.index(n)
                pe.wait_ge(self.w_lo, i + 1)
                for t0, m in TOK_TILES:
                    o = unit_begin(pe)
                    for k in range(KT):
                        for j, (x, w) in enumerate(self.terms(pe, k)):
                            last = pe.matmul(o[0:m, 0, 0:CHUNKS[n][2]], self.x[x][:, k, t0:t0 + m], self.w[w][:, i % 2, k, 0:CHUNKS[n][2]],
                                             start=(k == 0 and j == 0), stop=(k == KT - 1 and j == 2))
                    last.then_inc(products_done, 1)

        copies_done = sem("copies_done")
        e = Shared()
        e.Split = Split
        e.I, e.O, e.L, e.l, e.K = I, O, L, l, K
        e.sb, e.sem, e.ps, e.ident, e.xnT = sb, sem, ps, ident, xnT
        e.ya, e.prm, e.bias_b, e.y_rows, e.cD = ya, prm, bias_b, y_rows, cD
        e.cA, e.cG, e.store, e.stores, e.stores_done = cA, cG, store, stores, stores_done
        e.out_stored, e.copies_done, e.load_chunks, e.prefetch, e.weights = out_stored, copies_done, load_chunks, prefetch, weights
        e.unit, e.pair, e.unit_wait, e.taken, e.wait_taken = unit, pair, unit_wait, taken, wait_taken
        e.products_done, e.products_taken, e.channel_products, e.token_products = products_done, products_taken, channel_products, token_products
        for f in STAGES:
            with ExitStack() as c2:
                scopes.append((c2, []))
                f(nc, c2, e)
                clear(scopes.pop()[1])
        nc.sync.wait_ge(out_stored, 16 * stores[0])
        nc.sync.wait_ge(copies_done, 16 * 3 * DEC_BATCH)
        clear(scopes[0][1])


def stage_norm(nc, c, e):
    x = e.sb("x", [P, 5, D_MODEL], c=c)
    sq = e.sb("sq", [P, D_MODEL], c=c)
    ss = e.sb("ss", [P, 5], c=c)
    rows = e.sb("prm_rows", [N_PRM, P], c=c)
    x_in, prm_in, rstd_in, normed, turned, evacd, prm_t, cleared = [e.sem("n_" + s) for s in
        ("x_in", "prm_in", "sqrt", "normed", "turned", "evacd", "prm_t", "cleared")]
    with nc.Block() as block:
        @block.sync
        def _(sp):
            for i, (t0, m) in enumerate(TOK_TILES):
                if m < P:
                    sp.wait_ge(cleared, 1)
                sp.dma_start(x[0:m, i, :], e.y_rows[i]).then_inc(x_in, 16)
            for name, (a, b) in PRM.items():
                src = e.L[name]
                src = src.rearrange("h d -> (h d)") if len(src.shape) == 2 else src
                sp.dma_start(rows[a:b, :], src.rearrange("(r c) -> r c", c=P)).then_inc(prm_in, 16)
            sp.dma_start(e.bias_b[:, :], e.L["b_bias"].partition_broadcast(P)).then_inc(prm_in, 16)
            e.load_chunks(sp, 0, RING)

        @block.vector
        def _(v):
            v.memset(x[:, 4, :], 0.0).then_inc(cleared, 1)
            v.wait_ge(x_in, 16 * 5)
            for i in range(5):
                e.cD(v, v.tensor_tensor_reduce(sq[:, :], x[:, i, :], x[:, i, :], 1.0, 0.0, ALU.mult, ALU.add, ss[:, i:i + 1]))
            v.tensor_scalar(ss[:, :], ss[:, :], 1.0 / D_MODEL, NORM_EPS, ALU.mult, ALU.add).then_inc(normed, 1)
            v.wait_ge(rstd_in, 1)
            e.cD(v, v.reciprocal(ss[:, :], ss[:, :]))
            for i in range(5):
                v.tensor_scalar(x[:, i, :], x[:, i, :], ss[:, i:i + 1], None, ALU.mult).then_inc(normed, 1)
            v.wait_ge(prm_t, 1)
            e.cD(v, v.tensor_copy(e.prm[:, :], e.ps[:, 4, 0:N_PRM]))
            for i, (t0, m) in enumerate(TOK_TILES):
                v.wait_ge(turned, i + 1)
                pp = e.ps[:, 2 * (i % 2):2 * (i % 2) + 2].rearrange("p a (k t) -> p (a k) t", t=P)
                nw = e.prm[:, 0:KT].unsqueeze(2).to_broadcast([P, KT, m])
                v.tensor_tensor(e.xnT[:, :, t0:t0 + m], pp[:, :, 0:m], nw, ALU.mult).then_inc(evacd, 1)

        @block.scalar
        def _(a):
            a.wait_ge(normed, 1)
            a.activation(ss[:, :], ss[:, :], ACT.Sqrt).then_inc(rstd_in, 1)

        @block.tensor
        def _(pe):
            pe.wait_ge(prm_in, 16 * (len(PRM) + 1))
            pe.transpose(e.ps[:, 4, 0:N_PRM], rows[:, :], e.ident[0:N_PRM, 0:N_PRM]).then_inc(prm_t, 1)
            for i, (t0, m) in enumerate(TOK_TILES):
                pe.wait_ge(normed, 2 + i)
                if i >= 2:
                    pe.wait_ge(evacd, i - 1)
                for k in range(KT):
                    last = pe.transpose(e.ps[:, 2 * (i % 2) + k // 4, k % 4 * P:k % 4 * P + m], x[0:m, i, k * P:(k + 1) * P],
                                        e.ident[0:m, 0:m])
                last.then_inc(turned, 1)


def stage_rwkv(nc, c, e):
    ps, K, prm = e.ps, e.K, e.prm
    pa = e.sb("pa", [P, 13, NT], c=c)
    r_, k_, v_ = pa[:, 0:4], pa[:, 4:8], pa[:, 8:12]

    def param(name, j0, n, w=NT):
        a = PRM[name][0] + j0
        return prm[:, a:a + n].unsqueeze(2).to_broadcast([P, n, w])

    w2 = e.sb("w2", [P, A_WIDTH], c=c)
    prev = e.sb("prev", [P, 13, DEC_BATCH], c=c)
    last = e.sb("last", [P, 13, 9], c=c)
    omka_done, k_scaled = e.sem("a_omka"), e.sem("a_k_scaled")
    (prev_in, lora_in, prev_t, last_copied, last_t, last_rows_copied, mixed, th_done, lora_mm, sig_done, kk_sq, kk_mm,
     kk_rt, rk_done, rk_mm, vt_mm, vt_done, bonus_done, cum_done, e1, e2, e3, al_done, be_done, tr_mm, tr_taken) = [
        e.sem("a_" + s) for s in (
            "prev_in", "lora_in", "prev_t", "last_copied", "last_t", "last_rows_copied", "mixed", "tanh", "lora_mm", "sig",
            "kk_sq", "kk_mm", "kk_root", "rk", "rk_mm", "vt_mm", "vt_done", "bonus", "cum", "exp1", "exp2", "exp3",
            "alpha", "beta", "tr_mm", "tr_taken")]
    c2 = ExitStack()
    prev_rows = e.sb("prev_rows", [DEC_BATCH, 13 * P], c=c2)
    split = e.Split(list(range(*PLAN["proj_a"])), c2)
    with nc.Block() as block:
        @block.sync
        def _(sp):
            sp.dma_start(prev_rows[:, :], e.L["state_a_shift"]).then_inc(prev_in, 16)
            sp.dma_start(w2[0:64, :], e.L["a_w2"]).then_inc(lora_in, 16)
            sp.dma_start(w2[64:P, :], e.L["a_a2"]).then_inc(lora_in, 16)
            e.prefetch(sp, "proj_a")

        @block.tensor
        def _(pe):
            for n in split.chunks:
                split.channel_products(pe, n)
            pe.wait_ge(prev_in, 16)
            for j in range(13):
                i = pe.transpose(ps[:, 4, j * 8:(j + 1) * 8], prev_rows[:, j * P:(j + 1) * P], e.ident[0:8, 0:8])
            i.then_inc(prev_t, 1)

        @block.scalar
        def _(a):
            split.weights_hi(a, 0)
            split.tokens_hi(a, e.xnT)
            split.weights_hi(a, 1)
            for j in range(13):
                o = e.unit_wait(a)
                a.copy(pa[:, j].rearrange("p (h t) -> p h t", h=2), o[:, :, 0:HALF]).then_inc(e.taken(), 1)
                if j % 2:
                    split.weights_hi(a, j // 2 + 2)
            e.wait_taken(a, e.unit["take"] - 1)
            e.cA(a, a.copy(last[:, :, 0], pa[:, :, SEQ - 1]))
            a.copy(last[:, :, 1:9], pa[:, :, SEQ:NT].rearrange("p j (b t) -> p j b t", t=4)[:, :, :, 3]).then_inc(last_copied, 1)

        @block.vector
        def _(v):
            split.weights_lo(v, 0)
            split.tokens_lo(v, e.xnT)
            for i in range(1, len(split.chunks)):
                split.weights_lo(v, i)
            v.wait_ge(prev_t, 1)
            v.tensor_copy(prev[:, :, :], ps[:, 4, 0:104].rearrange("p (j b) -> p j b", b=8))
    c2.close()
    b2 = e.sb("b2", [P, 4, NT], c=c)
    b3 = e.sb("b3", [P, 4, NT], c=c)
    T = [e.sb(f"t{i}", [P, 5, A_WIDTH], c=c) for i in range(5)]
    B0, B1, B4, B5 = [T[i][:, :, :].rearrange("p a b -> p (a b)")[:, 0:4 * NT].rearrange("p (j t) -> p j t", j=4)
                      for i in range(4)]
    pc = e.sb("chunk_decay", [P, 4, 16], c=c)

    c2 = ExitStack()
    last_rows = e.sb("last_rows", [9, 13, P], c=c2)
    omka = e.sb("one_minus_ka", [P, 4], c=c2)
    alT, beT, kaT, vT = T[1], T[2], T[3], T[4]

    def bank_pairs_544(j):
        return ps[:, 2 * j:2 * j + 2, 0:HALF]

    def halves(x):
        return x.rearrange("p (h t) -> p h t", h=2)

    with nc.Block() as block:
        @block.sync
        def _(sp):
            sp.wait_ge(last_rows_copied, 1)
            rows = last_rows[:, :, :].rearrange("r j c -> r (j c)")
            e.store(sp, e.O["a_shift_prompt"][e.l], rows[0:1, :])
            e.store(sp, e.O["a_shift_sample"][e.l], rows[1:9, :])
            e.stores_done(sp)

        @block.tensor
        def _(pe):
            pe.wait_ge(last_copied, 1)
            for j in range(13):
                i = pe.transpose(ps[0:9, 4 + j // 4, j % 4 * P:(j % 4 + 1) * P], last[:, j, :], e.ident[:, :])
            i.then_inc(last_t, 1)
            pe.wait_ge(lora_in, 32)
            pe.wait_ge(th_done, 1)
            pe.wait_ge(mixed, 2)
            for j in range(4):
                for which in range(2):
                    u = 2 * j + which
                    if u >= 2:
                        pe.wait_ge(sig_done, u - 1)
                    else:
                        pe.wait_ge(last_rows_copied, 1)
                    s = slice(0, 64) if which == 0 else slice(64, P)
                    for h in range(2):
                        i = pe.matmul(ps[:, 2 * (u % 2) + h, 0:HALF], w2[s, j * P:(j + 1) * P],
                                      pa[s, 12, h * HALF:(h + 1) * HALF], start=True, stop=True)
                    i.then_inc(lora_mm, 1)
            pe.wait_ge(kk_sq, 1)
            pe.wait_ge(sig_done, 8)
            for j in range(4):
                for h in range(2):
                    i = pe.matmul(ps[:, 2 * j + h, 0:HALF], K["bones"][:, :], B0[:, j, h * HALF:(h + 1) * HALF], start=True, stop=True)
            i.then_inc(kk_mm, 1)
            pe.wait_ge(kk_rt, 1)
            for i5, (t0, m) in enumerate(TOK_TILES):
                if i5 >= 2:
                    pe.wait_ge(vt_done, i5 - 1)
                for j in range(4):
                    i = pe.transpose(ps[0:m, i5 % 2, j * P:(j + 1) * P], v_[:, j, t0:t0 + m], e.ident[:, :])
                i.then_inc(vt_mm, 1)
            pe.wait_ge(rk_done, 1)
            pe.wait_ge(vt_done, 5)
            for j in range(4):
                for h in range(2):
                    i = pe.matmul(ps[:, 2 * j + h, 0:HALF], K["bones"][:, :], B0[:, j, h * HALF:(h + 1) * HALF], start=True, stop=True)
            i.then_inc(rk_mm, 1)
            for n, (src, sig) in enumerate(((b3, al_done), (b2, be_done), (k_, be_done))):
                pe.wait_ge(sig, 1)
                if n == 0:
                    pe.wait_ge(bonus_done, 1)
                    pe.wait_ge(al_done, 3)
                for i5, (t0, m) in enumerate(TOK_TILES):
                    u = n * 5 + i5
                    if u >= 2:
                        pe.wait_ge(tr_taken, u - 1)
                    for j in range(4):
                        i = pe.transpose(ps[0:m, u % 2, j * P:(j + 1) * P], src[:, j, t0:t0 + m], e.ident[:, :])
                    i.then_inc(tr_mm, 1)

        @block.scalar
        def _(a):
            a.wait_ge(last_t, 1)
            for g in range(4):
                n = 4 if g < 3 else 1
                e.cA(a, a.copy(last_rows[:, 4 * g:4 * g + n, :], ps[0:9, 4 + g, 0:n * P].rearrange("r (j c) -> r j c", c=P)))
            a.sem_inc(last_rows_copied, 1)
            a.wait_ge(mixed, 1)
            a.activation(pa[0:64, 12, :], pa[0:64, 12, :], ACT.Tanh).then_inc(th_done, 1)
            for j in range(4):
                for which, (dst, pn) in enumerate(((B1, "a_w0"), (b2, "a_a0"))):
                    u = 2 * j + which
                    a.wait_ge(lora_mm, u + 1)
                    a.activation(halves(dst[:, j]), ps[:, 2 * (u % 2):2 * (u % 2) + 2, 0:HALF], ACT.Sigmoid,
                                 bias=prm[:, PRM[pn][0] + j:PRM[pn][0] + j + 1]).then_inc(sig_done, 1)
            a.wait_ge(kk_mm, 1)
            for j in range(4):
                e.cA(a, a.activation(halves(B0[:, j]), bank_pairs_544(j), ACT.Sqrt))
            a.sem_inc(kk_rt, 1)
            a.wait_ge(cum_done, 1)
            a.wait_ge(k_scaled, 1)
            a.activation(B5, B1, ACT.Exp, scale=-DECAY_RATE).then_inc(e1, 1)
            a.wait_ge(al_done, 1)
            a.activation(B5, B4, ACT.Exp, scale=DECAY_RATE).then_inc(e2, 1)
            a.wait_ge(be_done, 1)
            a.activation(B5, B4, ACT.Exp, scale=-DECAY_RATE).then_inc(e3, 1)
            for n, dst in enumerate((alT, beT, kaT)):
                for i5, (t0, m) in enumerate(TOK_TILES):
                    u = n * 5 + i5
                    a.wait_ge(tr_mm, u + 1)
                    a.copy(dst[0:m, i5, :], ps[0:m, u % 2, :]).then_inc(tr_taken, 1)

        @block.vector
        def _(v):
            D = e.cD
            v.tensor_scalar(omka[:, :], prm[:, PRM["a_ka"][0]:PRM["a_ka"][1]], -1.0, 1.0, ALU.mult, ALU.add).then_inc(omka_done, 1)
            for j0 in (12, 0, 4, 8):
                n = 1 if j0 == 12 else 4
                x, d = pa[:, j0:j0 + n], B0[:, 0:n]
                xs, ds = [y[:, :, SEQ:NT].rearrange("p j (b t) -> p j b t", t=4) for y in (x, d)]
                v.tensor_tensor(d[:, :, 1:SEQ], x[:, :, 0:SEQ - 1], x[:, :, 1:SEQ], ALU.subtract)
                v.tensor_scalar(d[:, :, 0:1], x[:, :, 0:1], -1.0, None, ALU.mult)
                v.tensor_tensor(ds[:, :, :, 1:4], xs[:, :, :, 0:3], xs[:, :, :, 1:4], ALU.subtract)
                D(v, v.tensor_tensor(ds[:, :, :, 0], prev[:, j0:j0 + n, :], xs[:, :, :, 0], ALU.subtract))
                D(v, v.tensor_tensor(d, d, param("a_mu", j0, n), ALU.mult))
                if j0 == 12:
                    v.tensor_tensor(x, x, d, ALU.add).then_inc(mixed, 1)
                    v.wait_ge(mixed, 1)
                    v.sem_inc(mixed, 1)
                else:
                    D(v, v.tensor_tensor(x, x, d, ALU.add))
            D(v, v.tensor_tensor(b3[:, :, :], k_, param("a_kk", 0, 4), ALU.mult))
            v.tensor_tensor(B0, b3[:, :, :], b3[:, :, :], ALU.mult).then_inc(kk_sq, 1)
            v.wait_ge(sig_done, 8)
            for j in range(4):
                v.tensor_tensor_scan(B4[:, j], K["reset"][:, :], B1[:, j], 0.0, ALU.mult, ALU.add)
            v.wait_ge(kk_rt, 1)
            D(v, v.tensor_scalar(B0, B0, 1e-12, None, ALU.max))
            D(v, v.reciprocal(B0, B0))
            D(v, v.tensor_tensor(b3[:, :, :], b3[:, :, :], B0, ALU.mult))
            v.tensor_tensor(B1, B4, B1, ALU.subtract).then_inc(cum_done, 1)
            v.wait_ge(k_scaled, 1)
            D(v, v.tensor_tensor(b2[:, :, :], b2[:, :, :], b3[:, :, :], ALU.mult))
            D(v, v.tensor_tensor(B0, r_, k_, ALU.mult))
            v.tensor_tensor(B0, B0, param("a_rk", 0, 4), ALU.mult).then_inc(rk_done, 1)
            for i5, (t0, m) in enumerate(TOK_TILES):
                v.wait_ge(vt_mm, i5 + 1)
                v.tensor_copy(vT[0:m, i5, :], ps[0:m, i5 % 2, :]).then_inc(vt_done, 1)
            v.wait_ge(rk_mm, 1)
            for j in range(4):
                D(v, v.tensor_tensor(halves(v_[:, j]), bank_pairs_544(j), halves(v_[:, j]), ALU.mult))
            v.sem_inc(bonus_done, 1)
            v.wait_ge(e1, 1)
            v.tensor_tensor(b3[:, :, :], b3[:, :, :], B5, ALU.mult).then_inc(al_done, 1)
            v.wait_ge(e2, 1)
            D(v, v.tensor_tensor(b2[:, :, :], b2[:, :, :], B5, ALU.mult))
            v.tensor_tensor(k_, k_, B5, ALU.mult).then_inc(be_done, 1)
            v.wait_ge(e3, 1)
            v.tensor_tensor(r_, r_, B5, ALU.mult).then_inc(al_done, 1)
            v.tensor_copy(pc[:, :, 0:8], B5[:, :, 0:SEQ].rearrange("p j (c t) -> p j c t", t=CHUNK)[:, :, :, CHUNK - 1])
            D(v, v.tensor_copy(pc[:, :, 8:16], B5[:, :, SEQ:NT].rearrange("p j (c t) -> p j c t", t=4)[:, :, :, 3]))
            v.sem_inc(al_done, 1)

        @block.gpsimd
        def _(g):
            g.wait_ge(omka_done, 1)
            g.wait_ge(sig_done, 8)
            g.tensor_tensor(B5, b2[:, :, :], param("a_ka", 0, 4), ALU.mult).then_inc(omka_done, 1)
            g.wait_ge(omka_done, 2)
            g.tensor_tensor(B5, B5, omka[:, :].unsqueeze(2).to_broadcast([P, 4, NT]), ALU.add).then_inc(omka_done, 1)
            g.wait_ge(omka_done, 3)
            g.wait_ge(kk_sq, 1)
            g.tensor_tensor(k_, k_, B5, ALU.mult).then_inc(k_scaled, 1)
    c2.close()
    _rwkv_inverse(nc, c, e, pa, b2, b3, T, pc)


def _rwkv_inverse(nc, c, e, pa, b2, b3, T, pc):
    ps, K = e.ps, e.K
    alT, beT, kaT, vT = T[1], T[2], T[3], T[4]
    kap, rho = pa[:, 4:8], pa[:, 0:4]
    c2 = ExitStack()
    S = [[e.sb(f"inv{par}_{n}", [P, 512], c=c2) for n in ("x", "xt", "lt", "mt", "y", "lm")] for par in range(2)]
    pe_s, x_s, dve_s, act_s, pool_s = [[e.sem(f"inv_{n}{par}") for par in range(2)] for n in ("pe", "x", "dve", "act", "pool")]
    NLEV = 5

    def levels(u):
        return NLEV if u < 8 else 1

    def base(u, per_head):
        return per_head * (u // 2)

    PEN, DVN, ACN, PON = 3 + 2 * NLEV, 2 + NLEV, NLEV + 3, NLEV

    def blocks(u):
        if u < 8:
            j, R = u // 2, slice(64 * (u % 2), 64 * (u % 2) + 64)
            return [(i, P, slice(i * P, (i + 1) * P), (R, j, slice(i * P, (i + 1) * P))) for i in range(4)]
        return [(h, NDEC, slice(h * NDEC, (h + 1) * NDEC),
                 (slice(64 * (h % 2), 64 * (h % 2) + 64), h // 2, slice(SEQ, NT))) for h in range(8)]

    with nc.Block() as block:
        @block.sync
        def _(sp):
            for b in range(DEC_BATCH):
                for i in range(C_GROUPS):
                    src, dst = e.L[f"cache_c{i + 1}_kv"][b], e.O[f"c{i + 1}_kv_sample"][e.l][b]
                    stay = dst.shape[0] - DEC_SEQ
                    flat = lambda x: x.rearrange("r k h d -> (r k h d)").rearrange("(s x) -> s x", s=16)
                    sp.dma_start(flat(dst[0:stay]), flat(src[src.shape[0] - stay:])).then_inc(e.copies_done, 16)

        @block.tensor
        def _(pe):
            def unit_steps(u):
                par, bk = u % 2, 4 * (u % 2)
                x, xt, lt, mt, y, lm = S[par]
                b = base(u, PEN)
                m = P if u < 8 else NDEC
                if u >= 2:
                    pe.wait_ge(act_s[par], base(u, ACN))
                    pe.wait_ge(dve_s[par], base(u, DVN))
                if u == 8:
                    pe.wait_ge(act_s[1], base(9, ACN))
                    pe.wait_ge(dve_s[1], base(9, DVN))
                for bank, (L_, R_) in enumerate(((b3, b2), (b2, b3), (kap, b3))):
                    for i, _, f, (R, j, t) in blocks(u):
                        o = ps[0:m, bk + bank, f] if u < 8 else ps[0:m, bank + 4 * (i % 2), j * NDEC:(j + 1) * NDEC]
                        last = pe.matmul(o, L_[R, j, t], R_[R, j, t], start=True, stop=True)
                last.then_inc(pe_s[par], 1)
                yield
                for lev in range(levels(u)):
                    pe.wait_ge(pool_s[par], base(u, PON) + lev + 1)
                    pe.wait_ge(x_s[par], base(u, NLEV) + lev + 1)
                    for i, _, f, _x in blocks(u):
                        last = pe.matmul(ps[0:m, bk, f], lm[0:m, f], x[0:m, f], start=True, stop=True)
                    last.then_inc(pe_s[par], 1)
                    yield
                    pe.wait_ge(act_s[par], base(u, ACN) + lev + 1)
                    pe.wait_ge(dve_s[par], base(u, DVN) + 2 + lev)
                    for i, _, f, _x in blocks(u):
                        last = pe.matmul(ps[0:m, bk + 2, f], y[0:m, f], xt[0:m, f], start=True, stop=True)
                    if lev < levels(u) - 1:
                        for i, _, f, _x in blocks(u):
                            last = pe.matmul(ps[0:m, bk + 1, f], xt[0:m, f], y[0:m, f], start=True, stop=True)
                    last.then_inc(pe_s[par], 1)
                    yield
                nl = levels(u)
                pe.wait_ge(dve_s[par], base(u, DVN) + 2 + nl)
                for i, _, f, (R, j, t) in blocks(u):
                    h, tile = (u, i) if u < 8 else (i, 4)
                    pe.matmul(ps[0:m, bk + 3, i * HD:(i + 1) * HD],
                              mt[0:m, f], vT[0:m, tile, h * HD:(h + 1) * HD], start=True, stop=True)
                for i, _, f, (R, j, t) in blocks(u):
                    h, tile = (u, i) if u < 8 else (i, 4)
                    o = ps[R, bk, f] if u < 8 else ps[R, bk + h % 2, j * NDEC:(j + 1) * NDEC]
                    last = pe.matmul(o, alT[0:m, tile, h * HD:(h + 1) * HD], xt[0:m, f], start=True, stop=True)
                last.then_inc(pe_s[par], 1)
                yield
                pe.wait_ge(act_s[par], base(u, ACN) + nl + 1)
                for i, _, f, (R, j, t) in blocks(u):
                    last = pe.matmul(ps[0:m, bk + 2, i * HD:(i + 1) * HD], xt[0:m, f], y[0:m, i * HD:(i + 1) * HD],
                                     start=True, stop=True)
                last.then_inc(pe_s[par], 1)
                yield

            for u0 in range(0, 8, 2):
                for _ in zip(unit_steps(u0), unit_steps(u0 + 1)):
                    pass
            for _ in unit_steps(8):
                pass

        @block.gpsimd
        def _(g):
            def unit_steps(u):
                par = u % 2
                x, xt, lt, mt, y, lm = S[par]
                m = P if u < 8 else NDEC
                w = 512 if u < 8 else 8 * NDEC
                g.wait_ge(dve_s[par], base(u, DVN) + 1)
                for lev in range(levels(u)):
                    if lev:
                        g.wait_ge(pe_s[par], base(u, PEN) + 2 * lev)
                    mk = K["levels"][0:m, (lev + 1) * P:(lev + 1) * P + m].unsqueeze(1).to_broadcast([m, w // m, m])
                    g.tensor_tensor(lm[0:m, 0:w].rearrange("p (i t) -> p i t", t=m), lt[0:m, 0:w].rearrange("p (i t) -> p i t", t=m),
                                    mk, ALU.mult).then_inc(pool_s[par], 1)
                    yield

            for u0 in range(0, 8, 2):
                for _ in zip(unit_steps(u0), unit_steps(u0 + 1)):
                    pass
            for _ in unit_steps(8):
                pass

        @block.scalar
        def _(a):
            def unit_steps(u):
                par, bk = u % 2, 4 * (u % 2)
                x, xt, lt, mt, y, lm = S[par]
                b, m = base(u, PEN), (P if u < 8 else NDEC)
                w = 512 if u < 8 else 8 * NDEC
                for lev in range(levels(u)):
                    a.wait_ge(pe_s[par], b + 2 + 2 * lev)
                    a.copy(y[0:m, 0:w], ps[0:m, bk, 0:w]).then_inc(act_s[par], 1)
                    yield
                nl = levels(u)
                a.wait_ge(pe_s[par], b + 2 + 2 * nl)
                vw = 256 if u < 8 else 512
                a.copy(y[0:m, 0:vw], ps[0:m, bk + 3, 0:vw]).then_inc(act_s[par], 1)
                if u < 8:
                    R, j = slice(64 * (u % 2), 64 * (u % 2) + 64), u // 2
                    a.mul(b3[R, j, 0:SEQ], ps[R, bk, :], -1.0).then_inc(act_s[par], 1)
                else:
                    for hh in range(2):
                        R = slice(64 * hh, 64 * hh + 64)
                        i = a.mul(b3[R, :, SEQ:NT], ps[R, bk + hh, 0:4 * NDEC].rearrange("p (j t) -> p j t", t=NDEC), -1.0)
                        e.cA(a, i)
                    a.sem_inc(act_s[par], 1)
                yield
                a.wait_ge(pe_s[par], b + 3 + 2 * nl)
                if u < 8:
                    a.mul(alT[:, 0:4, u * HD:(u + 1) * HD], ps[:, bk + 2, 0:256].rearrange("p (i d) -> p i d", d=HD),
                          -1.0).then_inc(act_s[par], 1)
                else:
                    a.mul(alT[0:m, 4, :], ps[0:m, bk + 2, :], -1.0).then_inc(act_s[par], 1)
                yield

            for u0 in range(0, 8, 2):
                for _ in zip(unit_steps(u0), unit_steps(u0 + 1)):
                    pass
            for _ in unit_steps(8):
                pass

        @block.vector
        def _(v):
            D = e.cD

            def unit_steps(u):
                par, bk = u % 2, 4 * (u % 2)
                x, xt, lt, mt, y, lm = S[par]
                b, m = base(u, PEN), (P if u < 8 else NDEC)
                w = 512 if u < 8 else 8 * NDEC
                tl = lambda ap: ap.rearrange("p (i t) -> p i t", t=m)
                bc = lambda mk: mk.unsqueeze(1).to_broadcast([m, w // m, m])
                before = K["before"][0:m, 0:m] if u < 8 else K["before4"][0:m, 0:m]

                def masked(dst, bank, mask):
                    if u < 8:
                        return v.tensor_tensor(tl(dst[0:m, 0:w]), tl(ps[0:m, bk + bank, 0:w]), bc(mask), ALU.mult)
                    return v.tensor_tensor(dst[0:m, 0:w].rearrange("p (a z t) -> p z a t", z=2, t=m),
                                           ps[0:m, bank:bank + 5:4, 0:w // 2].rearrange("p z (a t) -> p z a t", t=m),
                                           mask.unsqueeze(1).unsqueeze(1).to_broadcast([m, 2, w // (2 * m), m]), ALU.mult)

                v.wait_ge(pe_s[par], b + 1)
                masked(lt, 1, before).then_inc(dve_s[par], 1)
                v.wait_ge(dve_s[par], base(u, DVN) + 1)
                masked(mt, 2, before)
                masked(x, 0, K["level1"][0:m, 0:m])
                D(v, v.tensor_tensor(tl(xt[0:m, 0:w]), tl(lt[0:m, 0:w]), bc(K["levels"][0:m, 0:m]), ALU.mult))
                v.tensor_tensor(tl(x[0:m, 0:w]), bc(e.ident[0:m, 0:m]), tl(x[0:m, 0:w]), ALU.subtract).then_inc(x_s[par], 1)
                v.tensor_tensor(tl(xt[0:m, 0:w]), bc(e.ident[0:m, 0:m]), tl(xt[0:m, 0:w]), ALU.subtract).then_inc(dve_s[par], 1)
                yield
                for lev in range(levels(u)):
                    v.wait_ge(pe_s[par], b + 3 + 2 * lev)
                    v.wait_ge(dve_s[par], base(u, DVN) + 2 + lev)
                    if lev < levels(u) - 1:
                        v.wait_ge(x_s[par], base(u, NLEV) + lev + 1)
                        v.tensor_tensor(x[0:m, 0:w], x[0:m, 0:w], ps[0:m, bk + 1, 0:w], ALU.subtract).then_inc(x_s[par], 1)
                    v.tensor_tensor(xt[0:m, 0:w], xt[0:m, 0:w], ps[0:m, bk + 2, 0:w], ALU.subtract).then_inc(dve_s[par], 1)
                    yield

            for u0 in range(0, 8, 2):
                for _ in zip(unit_steps(u0), unit_steps(u0 + 1)):
                    pass
            for _ in unit_steps(8):
                pass
    c2.close()
    _rwkv_sequence(nc, c, e, pa, b2, b3, T, pc)


def _rwkv_sequence(nc, c, e, pa, b2, b3, T, pc):
    ps, K = e.ps, e.K
    g2, beT, kaT, vT = T[1], T[2], T[3], T[4]
    g1, kap, rho, bonus = b3, pa[:, 4:8], pa[:, 0:4], pa[:, 8:12]
    ya = e.ya
    bd4 = K["bones"][:, :].unsqueeze(1).to_broadcast([P, 4, P])
    c2 = ExitStack()
    ST = e.sb("state", [P, 4, P], c=c2)
    U = e.sb("u", [P, 2, 512], c=c2)
    upd = e.sb("upd", [P, 512], c=c2)
    at = [e.sb(f"at{i}", [P, 8, P], c=c2) for i in range(2)]
    (u_mm, u_done, s_mm, s_done, at_mm, at_done, y_mm, y_done, f_mm, f_done) = [e.sem("seq_" + s) for s in
        ("u_mm", "u", "s_mm", "s", "at_mm", "at", "y_mm", "y", "f_mm", "f")]
    with nc.Block() as block:
        @block.sync
        def _(sp):
            sp.wait_ge(f_done, 1)
            fin = upd[:, :].rearrange("p (a j) -> p a j", a=4)
            for hh in range(2):
                R = slice(64 * hh, 64 * hh + 64)
                e.store(sp, e.O["a_wkv_prompt"][e.l, 0].rearrange("(p hh) i j -> hh i p j", hh=2)[hh], fin[R, :, 64 * hh:64 * hh + 64])
            e.stores_done(sp)

        @block.tensor
        def _(pe):
            for ck in range(NCHUNK):
                tile, q = ck // 2, ck % 2
                Rq = slice(64 * q, 64 * q + 64)
                t = slice(ck * CHUNK, (ck + 1) * CHUNK)
                pe.wait_ge(s_done, ck + 1)
                for p in range(4):
                    last = pe.matmul(ps[Rq, 0, p * P:(p + 1) * P], g1[:, p, t], ST[:, p, :], start=True, stop=True)
                last.then_inc(u_mm, 1)
                if q == 0 and tile >= 2:
                    pe.wait_ge(y_done, tile - 1)
                yb_ = 1 + tile % 2
                for p in range(4):
                    pe.matmul(ps[:, yb_, p * P + q * 64:p * P + q * 64 + 64], ST[:, p, :], rho[:, p, t],
                              start=(q == 0 and p == 0), stop=False, skip_group_check=True)
                pe.wait_ge(u_done, ck + 1)
                for p in range(4):
                    pp = slice(p * P, (p + 1) * P)
                    pe.matmul(ps[:, 3, pp], beT[Rq, tile, pp], U[Rq, tile % 2, pp], start=True, stop=False)
                    last = pe.matmul(ps[:, 3, pp], kaT[Rq, tile, pp], vT[Rq, tile, pp], start=False, stop=True)
                last.then_inc(s_mm, 1)
                if q == 0:
                    if tile:
                        pe.wait_ge(at_done, 4 * tile)
                    tt = slice(tile * P, (tile + 1) * P)
                    for n, src in enumerate((b2, kap)):
                        for h in range(8):
                            R = slice(64 * (h % 2), 64 * (h % 2) + 64)
                            last = pe.matmul(ps[:, 4 + 2 * n + h % 2, h // 2 * P:(h // 2 + 1) * P], src[R, h // 2, tt],
                                             rho[R, h // 2, tt], start=True, stop=True)
                    last.then_inc(at_mm, 1)
                if q == 1:
                    pe.wait_ge(at_done, 4 * (tile + 1))
                    for h in range(8):
                        R, p = slice(64 * (h % 2), 64 * (h % 2) + 64), h // 2
                        f = slice(h * HD, (h + 1) * HD)
                        o = ps[R, yb_, p * P:(p + 1) * P]
                        pe.matmul(o, U[:, tile % 2, f], at[0][:, h, :], start=False, stop=False, skip_group_check=True)
                        last = pe.matmul(o, vT[:, tile, f], at[1][:, h, :], start=False, stop=True, skip_group_check=True)
                    last.then_inc(y_mm, 1)
            pe.wait_ge(s_done, NCHUNK + 1)
            for p in range(4):
                last = pe.transpose(ps[:, 0, p * P:(p + 1) * P], ST[:, p, :], e.ident[:, :])
            last.then_inc(f_mm, 1)

        @block.scalar
        def _(a):
            for tile in range(TT):
                a.wait_ge(y_mm, tile + 1)
                a.copy(ya[:, :, tile * P:(tile + 1) * P], ps[:, 1 + tile % 2, :].rearrange("p (a t) -> p a t", a=4)).then_inc(y_done, 1)
            a.wait_ge(f_mm, 1)
            a.wait_ge(s_done, NCHUNK + 1)
            a.copy(upd[:, :], ps[:, 0, :]).then_inc(f_done, 1)

        @block.vector
        def _(v):
            D = e.cD
            v.memset(ST[:, :, :], 0.0).then_inc(s_done, 1)
            v.wait_ge(s_done, 1)
            for ck in range(NCHUNK):
                tile, q = ck // 2, ck % 2
                Rq = slice(64 * q, 64 * q + 64)
                v.wait_ge(u_mm, ck + 1)
                if q == 0 and tile >= 2:
                    v.wait_ge(y_mm, tile - 1)
                v.tensor_tensor(U[Rq, tile % 2, :], ps[Rq, 0, :], g2[Rq, tile, :], ALU.add).then_inc(u_done, 1)
                if q == 1:
                    v.wait_ge(at_mm, tile + 1)
                    if tile:
                        v.wait_ge(y_mm, tile)
                    for n in range(2):
                        for hh in range(2):
                            v.tensor_tensor(at[n][:, :, :].rearrange("p (a hh) t -> p hh a t", hh=2)[:, hh],
                                            ps[:, 4 + 2 * n + hh, :].rearrange("p (a t) -> p a t", a=4),
                                            K["upto"][:, :].unsqueeze(1).to_broadcast([P, 4, P]), ALU.mult).then_inc(at_done, 1)
                v.wait_ge(s_mm, ck + 1)
                up4 = upd[:, :].rearrange("p (a t) -> p a t", a=4)
                D(v, v.tensor_tensor(up4, ps[:, 3, :].rearrange("p (a t) -> p a t", a=4), bd4, ALU.mult))
                D(v, v.tensor_tensor(ST[:, :, :], ST[:, :, :], up4, ALU.add))
                v.tensor_tensor(ST[:, :, :], ST[:, :, :], pc[:, :, ck:ck + 1].to_broadcast([P, 4, P]), ALU.mult).then_inc(s_done, 1)
                v.wait_ge(s_done, ck + 2)
    c2.close()

    c2 = ExitStack()
    SN = e.sb("state_rows", [P, 2, 8, P], c=c2)
    SO = T[0][:, 0:4, :].rearrange("p a (b t) -> p (a b) t", t=P).rearrange("p (two b) t -> p two b t", two=2)
    SS = e.sb("state_s", [P, 2, 8, P], c=c2)
    G1m = e.sb("g1m", [P, 8, NDEC], c=c2)
    Us = e.sb("us", [NDEC, P], c=c2)
    Um = e.sb("um", [NDEC, 8, P], c=c2)
    Vm = e.sb("vm", [NDEC, 2, 8, P], c=c2)
    ats = T[0][0:NDEC, 4, 0:8 * NDEC].rearrange("p (two n t) -> p two n t", two=2, n=4)
    (z_done, t_mm, t_done, gm_done, vm_done, um_done, u_mm, u_done, at_mm, at_done, y_mm, y_done, s_mm, s_done, b_mm, b_done) = [
        e.sem("dec_" + s) for s in ("zero", "t_mm", "t", "g1m", "vm", "um", "u_mm", "u", "at_mm", "at", "y_mm", "y", "s_mm", "s",
                                    "b_mm", "b")]
    s_in = [e.sem(f"dec_s_in{j}") for j in range(2)]
    s_stored = [e.sem(f"dec_s_stored{j}") for j in range(2)]
    with nc.Block() as block:
        @block.sync
        def _(sp):
            sp.wait_ge(z_done, 1)
            src = e.L["state_a_wkv"]

            def load(p):
                if p >= 2:
                    sp.wait_ge(t_mm, p - 1)
                for hh in range(2):
                    R = slice(64 * hh, 64 * hh + 64)
                    sp.dma_start(SN[R, p % 2, :, 64 * hh:64 * hh + 64],
                                 src[:, 2 * p + hh].rearrange("b i j -> i b j")).then_inc(s_in[p % 2], 16)

            load(0)
            load(1)
            load(2)
            for p in range(4):
                sp.wait_ge(b_done, 2 * (p + 1))
                for hh in range(2):
                    R = slice(64 * hh, 64 * hh + 64)
                    e.store(sp, e.O["a_wkv_sample"][e.l][:, 2 * p + hh].rearrange("b i j -> i b j"),
                            SO[R, p % 2, :, 64 * hh:64 * hh + 64], s_stored[p % 2])
                if p == 0:
                    load(3)
            for j in range(2):
                sp.wait_ge(s_stored[j], 64)

        @block.tensor
        def _(pe):
            def turn_in(p):
                pe.wait_ge(s_in[p % 2], 32 * (p // 2 + 1))
                if p >= 2:
                    pe.wait_ge(b_done, 2 * (p - 1))
                for b in range(8):
                    last = pe.transpose(ps[:, b // 4, b % 4 * P:(b % 4 + 1) * P], SN[:, p % 2, b, :], e.ident[:, :])
                last.then_inc(t_mm, 1)

            def attention(p):
                if p:
                    pe.wait_ge(at_done, 4 * p)
                for n, src in enumerate((b2, kap)):
                    for hh in range(2):
                        R = slice(64 * hh, 64 * hh + 64)
                        last = pe.matmul(ps[0:NDEC, 6 + hh, n * NDEC:(n + 1) * NDEC], src[R, p, SEQ:NT], rho[R, p, SEQ:NT],
                                         start=True, stop=True)
                last.then_inc(at_mm, 1)

            def turn_out(p):
                pe.wait_ge(s_done, p + 1)
                for b in range(8):
                    last = pe.transpose(ps[:, b // 4, b % 4 * P:(b % 4 + 1) * P], SS[:, p % 2, b, :], e.ident[:, :])
                last.then_inc(b_mm, 1)

            turn_in(0)
            attention(0)
            for p in range(4):
                pp = slice(p * P, (p + 1) * P)
                pe.wait_ge(t_done, 2 * (p + 1))
                pe.wait_ge(gm_done, p + 1)
                for b in range(8):
                    last = pe.matmul(ps[0:NDEC, 2, 0:P], G1m[:, b, :], SS[:, p % 2, b, :], start=(b == 0), stop=(b == 7))
                last.then_inc(u_mm, 1)
                if p:
                    pe.wait_ge(y_done, p)
                for b in range(8):
                    t = slice(SEQ + 4 * b, SEQ + 4 * b + 4)
                    pe.matmul(ps[:, 3, 4 * b:4 * b + 4], SS[:, p % 2, b, :], rho[:, p, t], start=(b == 0), stop=False, skip_group_check=True)
                if p:
                    turn_out(p - 1)
                if p < 3:
                    attention(p + 1)
                pe.wait_ge(u_done, p + 1)
                pe.wait_ge(at_done, 4 * (p + 1))
                for hh in range(2):
                    R = slice(64 * hh, 64 * hh + 64)
                    f = slice(p * P + hh * HD, p * P + (hh + 1) * HD)
                    pe.matmul(ps[R, 3, 0:NDEC], Us[:, hh * HD:(hh + 1) * HD], ats[:, p % 2, hh, :], start=False, stop=False, skip_group_check=True)
                    last = pe.matmul(ps[R, 3, 0:NDEC], vT[0:NDEC, 4, f], ats[:, p % 2, 2 + hh, :], start=False, stop=True, skip_group_check=True)
                last.then_inc(y_mm, 1)
                if p < 3:
                    turn_in(p + 1)
                pe.wait_ge(um_done, p + 1)
                pe.wait_ge(vm_done, p + 1)
                for b in range(8):
                    o = ps[:, 4 + b // 4, b % 4 * P:(b % 4 + 1) * P]
                    pe.matmul(o, beT[0:NDEC, 4, pp], Um[:, b, :], start=True, stop=False)
                    last = pe.matmul(o, kaT[0:NDEC, 4, pp], Vm[:, p % 2, b, :], start=False, stop=True)
                last.then_inc(s_mm, 1)
            pe.wait_ge(b_done, 6)
            turn_out(3)

        @block.scalar
        def _(a):
            def take_in(p):
                a.wait_ge(t_mm, p + 1)
                for half in range(2):
                    a.copy(SS[:, p % 2, 4 * half:4 * half + 4, :], ps[:, half, :].rearrange("p (b t) -> p b t", b=4)).then_inc(t_done, 1)

            def take_out(p):
                a.wait_ge(b_mm, p + 1)
                if p >= 2:
                    a.wait_ge(s_stored[p % 2], 32 * (p // 2))
                for half in range(2):
                    a.copy(SO[:, p % 2, 4 * half:4 * half + 4, :], ps[:, half, :].rearrange("p (b t) -> p b t", b=4)).then_inc(b_done, 1)

            take_in(0)
            for p in range(4):
                if p:
                    take_out(p - 1)
                a.wait_ge(y_mm, p + 1)
                a.copy(ya[:, p, SEQ:NT], ps[:, 3, 0:NDEC]).then_inc(y_done, 1)
                if p < 3:
                    take_in(p + 1)
            take_out(3)

        @block.vector
        def _(v):
            D = e.cD
            v.memset(SN[:, :, :, :], 0.0).then_inc(z_done, 1)
            rowb = K["rowb"][0:NDEC, :].unsqueeze(2).to_broadcast([NDEC, 8, P])

            def masked(p):
                if p:
                    v.wait_ge(u_mm, p)
                v.tensor_tensor(G1m[:, :, :], g1[:, p, SEQ:NT].unsqueeze(1).to_broadcast([P, 8, NDEC]),
                                K["colb"][:, :].rearrange("p (b t) -> p b t", b=8), ALU.mult).then_inc(gm_done, 1)
                if p >= 2:
                    v.wait_ge(s_mm, p - 1)
                v.tensor_tensor(Vm[:, p % 2], vT[0:NDEC, 4, p * P:(p + 1) * P].unsqueeze(1).to_broadcast([NDEC, 8, P]), rowb,
                                ALU.mult).then_inc(vm_done, 1)
                v.wait_ge(at_mm, p + 1)
                if p >= 2:
                    v.wait_ge(y_mm, p - 1)
                for n in range(2):
                    for hh in range(2):
                        v.tensor_tensor(ats[:, p % 2, 2 * n + hh, :], ps[0:NDEC, 6 + hh, n * NDEC:(n + 1) * NDEC], K["upto4"][0:NDEC, 0:NDEC],
                                        ALU.mult).then_inc(at_done, 1)

            masked(0)
            for p in range(4):
                v.wait_ge(u_mm, p + 1)
                if p:
                    v.wait_ge(y_mm, p)
                v.tensor_tensor(Us[:, :], ps[0:NDEC, 2, 0:P], g2[0:NDEC, 4, p * P:(p + 1) * P], ALU.add).then_inc(u_done, 1)
                v.wait_ge(u_done, p + 1)
                if p:
                    v.wait_ge(s_mm, p)
                v.tensor_tensor(Um[:, :, :], Us[:, :].unsqueeze(1).to_broadcast([NDEC, 8, P]), rowb, ALU.mult).then_inc(um_done, 1)
                if p < 3:
                    masked(p + 1)
                v.wait_ge(s_mm, p + 1)
                x4 = ps[:, 4:6, :].rearrange("p a (b t) -> p (a b) t", t=P)
                D(v, v.tensor_tensor(x4, x4, K["bones"][:, :].unsqueeze(1).to_broadcast([P, 8, P]), ALU.mult))
                D(v, v.tensor_tensor(SS[:, p % 2], SS[:, p % 2], x4, ALU.add))
                v.tensor_tensor(SS[:, p % 2], SS[:, p % 2], pc[:, p, 8:16].unsqueeze(2).to_broadcast([P, 8, P]), ALU.mult).then_inc(s_done, 1)
    c2.close()

    B0 = T[0][:, :, :].rearrange("p a b -> p (a b)")[:, 0:4 * NT].rearrange("p (j t) -> p j t", j=4)
    mean_mm, sq_done, var_mm, var_done, root_done, bonus_done = [e.sem("gn_" + s) for s in
        ("mean_mm", "sq", "var_mm", "var", "root", "bonus")]

    def group_sum(pe, src):
        for j in range(4):
            for h in range(2):
                last = pe.matmul(ps[:, 2 * j + h, 0:HALF], K["bones"][:, :], src[:, j, h * HALF:(h + 1) * HALF], start=True, stop=True)
        return last

    def param(name):
        a = PRM[name][0]
        return e.prm[:, a:a + 4].unsqueeze(2).to_broadcast([P, 4, NT])

    with nc.Block() as block:
        @block.sync
        def _(sp):
            pass

        @block.tensor
        def _(pe):
            group_sum(pe, ya).then_inc(mean_mm, 1)
            pe.wait_ge(sq_done, 1)
            group_sum(pe, B0).then_inc(var_mm, 1)

        @block.scalar
        def _(a):
            a.wait_ge(var_done, 1)
            a.activation(B0, B0, ACT.Sqrt).then_inc(root_done, 1)

        @block.vector
        def _(v):
            D = e.cD
            v.wait_ge(mean_mm, 1)
            for j in range(4):
                y2 = ya[:, j].rearrange("p (h t) -> p h t", h=2)
                D(v, v.scalar_tensor_tensor(y2, ps[:, 2 * j:2 * j + 2, 0:HALF], -1.0 / HD, y2, ALU.mult, ALU.add))
            v.tensor_tensor(B0, ya[:, :, :], ya[:, :, :], ALU.mult).then_inc(sq_done, 1)
            v.wait_ge(var_mm, 1)
            for j in range(4):
                D(v, v.tensor_scalar(B0[:, j].rearrange("p (h t) -> p h t", h=2), ps[:, 2 * j:2 * j + 2, 0:HALF], 1.0 / HD, A_GN_EPS,
                                ALU.mult, ALU.add))
            v.sem_inc(var_done, 1)
            v.wait_ge(root_done, 1)
            D(v, v.reciprocal(B0, B0))
            D(v, v.tensor_tensor(ya[:, :, :], ya[:, :, :], B0, ALU.mult))
            D(v, v.tensor_tensor(ya[:, :, :], ya[:, :, :], param("a_gn_w"), ALU.mult))
            v.wait_ge(bonus_done, 1)
            D(v, v.tensor_tensor(ya[:, :, :], ya[:, :, :], bonus, ALU.add))

        @block.gpsimd
        def _(g):
            g.tensor_tensor(bonus, bonus, param("a_gn_b"), ALU.add).then_inc(bonus_done, 1)



def stage_stick_breaking(nc, c, e):
    e.yb = e.sb("yb", [P, 4, NT])
    ps, K, yb = e.ps, e.K, e.yb
    qbd = e.sb("bq_blocks", [P, 4, DEC_BATCH, 32], c=c)
    kTn, vn = e.sb("bk_new_t", [P, 4, NDEC], c=c), e.sb("bv_new", [NDEC, B_WIDTH], c=c)
    pages = e.sb("pages", [1, DEC_BATCH * N_PAGES], I32, c=c)
    kp = e.sb("k_pages", [P, 2, 4, B_WIDTH], c=c)
    c1 = ExitStack()
    qT, kT = e.sb("bq", [P, 4, NT], c=c1), e.sb("bk", [P, 4, NT], c=c1)
    vt = e.sb("bv_tok", [P, 5, B_WIDTH], c=c1)
    new_clear = e.sem("b_new_clear")
    k_mm, k_done, v_ready = e.sem("b_k_mm"), e.sem("b_k_done"), e.sem("b_v_ready")

    def store_tokens(sp, tok, prompt, sample):
        e.store(sp, prompt[e.l, 0].rearrange("(i p) h d -> p i (h d)", p=P), tok[:, 0:TT, :])
        e.store(sp, sample[e.l].rearrange("b t h d -> (b t) (h d)"), tok[0:NDEC, TT, :])

    c2 = ExitStack()
    n0, n1 = PLAN["proj_b"]
    split = e.Split(list(range(n0, n1)), c2)
    with nc.Block() as block:
        @block.sync
        def _(sp):
            e.prefetch(sp, "proj_b")
            sp.wait_ge(v_ready, 1)
            store_tokens(sp, vt, e.O["b_v_prompt"], e.O["b_v_sample"])

        @block.tensor
        def _(pe):
            for n in split.chunks:
                (split.channel_products if n < n0 + 4 else split.token_products)(pe, n)

        @block.scalar
        def _(a):
            split.weights_hi(a, 0)
            split.tokens_hi(a, e.xnT)
            split.weights_hi(a, 1)
            for j in range(8):
                o = e.unit_wait(a)
                dst = (qT if j < 4 else kT)[:, j % 4].rearrange("p (h t) -> p h t", h=2)
                a.mul(dst, o[:, :, 0:HALF], QK_SCALE if j < 4 else 1.0).then_inc(e.taken(), 1)
                if j % 2:
                    split.weights_hi(a, j // 2 + 2)
            for half in range(2):
                for i, (t0, m) in enumerate(TOK_TILES):
                    o = e.unit_wait(a)
                    a.copy(vt[0:m, i, half * CW:(half + 1) * CW], o[0:m, 0, 0:CW]).then_inc(e.taken(), 1)
            e.wait_taken(a, e.unit["take"] - 1)
            a.sem_inc(v_ready, 1)

        @block.vector
        def _(v):
            split.weights_lo(v, 0)
            split.tokens_lo(v, e.xnT)
            for i in range(1, len(split.chunks)):
                split.weights_lo(v, i)
    c2.close()

    NCH, NV = 2 * DEC_BATCH, 3
    pt_in = e.sem("b_table_in")
    k_in = [e.sem(f"b_k_in{j}") for j in range(2)]
    v_in = [e.sem(f"b_v_in{j}") for j in range(NV)]

    def load_pages(sp, cache, dst, n0, n, arrived):
        _, found = nc.values_load_multi_w_load_instructions(pages[0:1, n0:n0 + n], engines=[mybir.EngineType.SP], min_val=0,
                                                            max_val=e.I[cache].shape[1] - 1)
        for j, page in enumerate(found):
            sp.dma_start(dst[:, j, :], e.L[cache][bass.ds(page, 1)].rearrange("a p h d -> p (a h d)")).then_inc(arrived, 16)

    def load_keys(sp, ch):
        load_pages(sp, "cache_b_k", kp[:, ch % 2], 4 * ch, 4, k_in[ch % 2])

    def load_values(sp, b):
        load_pages(sp, "cache_b_v", vp[:, b % NV], b * N_PAGES, N_PAGES, v_in[b % NV])

    NQ = 1280
    col = [0, 512, 1024, 896]
    wid = [512 - P * s for s in range(4)]
    c2 = ExitStack()
    kt = e.sb("bk_tok", [P, 5, B_WIDTH], c=c2)
    bufs = [[e.sb(f"sb{s}_{n}", [P, NQ], c=c2) for n in range(2)] for s in range(2)]
    kz = e.sb("k_alone", [P, 2, SEQ], c=c2)
    (kz_done, z_mm, abs_done, ln_done, re_done, sp_done, spm_done, cum_mm, w_done, wm_done, y_mm, y_done) = [e.sem("sb_" + s) for s in
        ("k_alone", "z_mm", "abs", "ln", "scores", "sp", "sp_masked", "cum_mm", "w", "w_masked", "y_mm", "y")]

    def bank(h):
        return ps[:, 3 * (h % 2):3 * (h % 2) + 3, :].rearrange("p a b -> p (a b)")[:, 0:NQ]

    with nc.Block() as block:
        @block.sync
        def _(sp):
            sp.dma_start(pages[0:1, :], e.I["page_table"].rearrange("b n -> (b n)").unsqueeze(0)).then_inc(pt_in, 16)
            sp.wait_ge(pt_in, 16)
            load_keys(sp, 0)
            load_keys(sp, 1)
            sp.wait_ge(k_done, 5)
            store_tokens(sp, kt, e.O["b_k_prompt"], e.O["b_k_sample"])
            e.stores_done(sp)

        @block.tensor
        def _(pe):
            for i, (t0, m) in enumerate(TOK_TILES):
                if i >= 2:
                    pe.wait_ge(k_done, i - 1)
                for j in range(4):
                    last = pe.transpose(ps[0:m, 4 + i % 2, j * P:(j + 1) * P], kT[:, j, t0:t0 + m], e.ident[:, :])
                last.then_inc(k_mm, 1)
            pe.wait_ge(k_done, 5)
            for i in range(B_HEADS + 2):
                if i < B_HEADS:
                    h = i
                    z = bank(h)
                    pe.wait_ge(kz_done, h + 1)
                    if h >= 2:
                        pe.wait_ge(w_done, h - 1)
                    for s in range(4):
                        last = pe.matmul(z[:, col[s]:col[s] + wid[s]], kz[:, h % 2, s * P:(s + 1) * P], qT[:, h // 2, s * P:SEQ],
                                         start=(s != 3), stop=False, skip_group_check=True)
                    last.then_inc(z_mm, 1)
                if i >= 2:
                    h = i - 2
                    R, w = slice(64 * (h % 2), 64 * (h % 2) + 64), bufs[h % 2][0]
                    pe.wait_ge(wm_done, h + 1)
                    if h >= 4 and h % 2 == 0:
                        pe.wait_ge(y_done, h // 2 - 1)
                    for s in range(4):
                        last = pe.matmul(ps[R, 6 + h // 2 % 2, s * P:SEQ], vt[:, s, h * HD:(h + 1) * HD], w[:, col[s]:col[s] + wid[s]],
                                         start=(s == 0), stop=(s == 3), skip_group_check=True)
                    last.then_inc(y_mm, 1)
                if 1 <= i <= B_HEADS:
                    h = i - 1
                    z, sp_ = bank(h), bufs[h % 2][0]
                    pe.wait_ge(spm_done, h + 1)
                    for s in range(4):
                        for j in range(s, 4):
                            o = col[s] + (j - s) * P
                            last = pe.matmul(z[:, o:col[s] + wid[s]], K["tri" if j == s else "allneg"][:, :],
                                             sp_[:, col[j]:col[j] + wid[j]], start=False, stop=(j == 3), skip_group_check=True)
                    last.then_inc(cum_mm, 1)

        @block.scalar
        def _(a):
            A = e.cA
            for i, (t0, m) in enumerate(TOK_TILES):
                a.wait_ge(k_mm, i + 1)
                a.copy(kt[0:m, i, :], ps[0:m, 4 + i % 2, :]).then_inc(k_done, 1)
            for i in range(B_HEADS + 2):
                if i < B_HEADS:
                    h = i
                    b0 = bufs[h % 2][0]
                    a.wait_ge(z_mm, h + 1)
                    if h >= 2:
                        a.wait_ge(y_mm, h - 1)
                    a.activation(b0[:, :], bank(h), ACT.Abs, bias=e.bias_b[:, h:h + 1]).then_inc(abs_done, 1)
                    a.wait_ge(abs_done, h + 1)
                    A(a, a.activation(b0[:, :], b0[:, :], ACT.Exp, scale=-1.0))
                    a.activation(b0[:, :], b0[:, :], ACT.Ln, bias=1.0).then_inc(ln_done, 1)
                if 1 <= i <= B_HEADS:
                    h = i - 1
                    a.wait_ge(cum_mm, h + 1)
                    a.activation(bufs[h % 2][0][:, :], bank(h), ACT.Exp, bias=e.bias_b[:, h:h + 1]).then_inc(w_done, 1)
                if i >= 2 and i % 2 == 1:
                    a.wait_ge(y_mm, i - 1)
                    a.copy(yb[:, (i - 2) // 2, 0:SEQ], ps[:, 6 + (i - 2) // 2 % 2, :]).then_inc(y_done, 1)

        @block.vector
        def _(v):
            v.memset(qbd[:, :, :, :], 0.0).then_inc(new_clear, 1)
            v.memset(kz[:, :, :], 0.0).then_inc(new_clear, 1)
            v.tensor_copy(kTn[:, :, :], kT[:, :, SEQ:NT])
            v.tensor_copy(vn[:, :], vt[0:NDEC, 4, :])
            v.wait_ge(new_clear, 2)

            def key_rows(h):
                R = slice(64 * (h % 2), 64 * (h % 2) + 64)
                if h >= 2:
                    v.wait_ge(z_mm, h - 1)
                v.tensor_copy(kz[R, h % 2, :], kT[R, h // 2, 0:SEQ]).then_inc(kz_done, 1)

            key_rows(0)
            key_rows(1)
            for h in range(B_HEADS):
                R = slice(64 * (h % 2), 64 * (h % 2) + 64)
                v.tensor_copy(qbd[R, h // 2, :, 4 * h:4 * h + 4], qT[R, h // 2, SEQ:NT].rearrange("p (b t) -> p b t", t=4))
            for h in range(B_HEADS):
                b0, b1 = bufs[h % 2]
                v.wait_ge(abs_done, h + 1)
                v.tensor_scalar(b1[:, :], bank(h), e.bias_b[:, h:h + 1], None, ALU.add).then_inc(re_done, 1)
                v.wait_ge(re_done, h + 1)
                v.wait_ge(ln_done, h + 1)
                v.scalar_tensor_tensor(b0[:, :], b1[:, :], 0.0, b0[:, :], ALU.max, ALU.add).then_inc(sp_done, 1)
                if h + 2 < B_HEADS:
                    key_rows(h + 2)

        @block.gpsimd
        def _(g):
            for i in range(B_HEADS + 1):
                if i < B_HEADS:
                    b0 = bufs[i % 2][0]
                    g.wait_ge(sp_done, i + 1)
                    for s in range(4):
                        d = b0[:, col[s]:col[s] + P]
                        last = g.affine_select(out=d, in_=d, compare_op=ALU.is_gt, fill=0.0, base=0, pattern=[[1, P]], channel_multiplier=-1)
                    last.then_inc(spm_done, 1)
                if i >= 1:
                    h = i - 1
                    b0 = bufs[h % 2][0]
                    g.wait_ge(w_done, h + 1)
                    for s in range(4):
                        d = b0[:, col[s]:col[s] + P]
                        last = g.affine_select(out=d, in_=d, compare_op=ALU.is_gt, fill=0.0, base=0, pattern=[[1, P]], channel_multiplier=-1)
                    last.then_inc(wm_done, 1)
    c2.close()

    c1.close()

    c2 = ExitStack()
    NK = PAST_LEN + NDEC
    vp = e.sb("v_pages", [P, NV, N_PAGES, B_WIDTH], c=c2)
    kpT = e.sb("k_pages_t", [P, 2, 4, 4 * PAGE], c=c2)
    zb, sp_ = [[e.sb(f"d{n}{i}", [P, NK], c=c2) for i in range(2)] for n in ("zb", "sp")]
    ones = e.sb("ones", [P, 1], c=c2)
    wT = e.sb("d_weights_t", [P, 9, P], c=c2)
    own = e.sb("d_own_head", [P, B_WIDTH], c=c2)
    rowbias = e.sb("d_row_bias", [P, 1], c=c2)
    (bias_done, k_mm, takeA, takeD, z_mm, z_done, ln_done, r_done, w_done, y_mm, own_done, f_mm, f_done) = [
        e.sem("sd_" + s) for s in ("bias", "k_mm", "take_a", "take_d", "z_mm", "z", "ln", "rest", "w", "y_mm", "own",
                                   "f_mm", "f")]
    NKR = 4 * NCH

    def take(eng, copy, i, sem):
        eng.wait_ge(k_mm, i + 1)
        bank = ps[:, 6 + i % 2, :]
        if i < NKR:
            ch, j = i // 4, i % 4
            if ch >= 2:
                eng.wait_ge(z_mm, ch - 1)
            copy(kpT[:, ch % 2, :, j * PAGE:(j + 1) * PAGE], bank.rearrange("p (a t) -> p a t", a=4)).then_inc(sem, 1)
        else:
            half, r = (i - NKR) // 3, (i - NKR) % 3
            if half:
                eng.wait_ge(y_mm, 4)
            if r < 2:
                copy(wT[:, 4 * r:4 * r + 4, :], bank.rearrange("p (a t) -> p a t", a=4)).then_inc(sem, 1)
            else:
                copy(wT[0:NDEC, 8, :], bank[0:NDEC, 0:P]).then_inc(sem, 1)

    with nc.Block() as block:
        @block.sync
        def _(sp):
            for ch in range(2, NCH):
                sp.wait_ge(k_mm, 4 * (ch - 1))
                load_keys(sp, ch)
                if ch in (6, 9, 12):
                    load_values(sp, (ch - 6) // 3)
            for b in range(3, DEC_BATCH):
                sp.wait_ge(y_mm, b - NV + 1)
                load_values(sp, b)

        @block.tensor
        def _(pe):
            def turn(i, blocks):
                if i >= 2:
                    pe.wait_ge((takeA, takeD)[i % 2], i // 2)
                for j, (src, m) in enumerate(blocks):
                    last = pe.transpose(ps[0:m, 6 + i % 2, j * P:(j + 1) * P], src, e.ident[:, :])
                last.then_inc(k_mm, 1)

            def wait_rounds(n):
                pe.wait_ge(takeA, (n + 1) // 2)
                pe.wait_ge(takeD, n // 2)

            def turn_keys(ch):
                pe.wait_ge(k_in[ch % 2], 64 * (ch // 2 + 1))
                for j in range(4):
                    turn(4 * ch + j, [(kp[:, ch % 2, j, p * P:(p + 1) * P], P) for p in range(4)])

            turn_keys(0)
            for ch in range(NCH):
                if ch + 1 < NCH:
                    turn_keys(ch + 1)
                b, part = ch // 2, ch % 2
                half, R = b // 4, slice(32 * (b % 4), 32 * (b % 4) + 32)
                wait_rounds(4 * (ch + 1))
                for p in range(4):
                    last = pe.matmul(ps[R, 2 * half + part, :], qbd[:, p, b, :], kpT[:, ch % 2, p, :], start=(p == 0), stop=(p == 3))
                if part == 1:
                    for p in range(4):
                        last = pe.matmul(ps[R, 4 + half, 0:NDEC], qbd[:, p, b, :], kTn[:, p, :], start=(p == 0), stop=(p == 3))
                last.then_inc(z_mm, 1)
            for half in range(2):
                pe.wait_ge(w_done, half + 1)
                i0 = NKR + 3 * half
                w = zb[half]
                for r in range(2):
                    turn(i0 + r, [(w[:, (4 * r + j) * P:(4 * r + j + 1) * P], P) for j in range(4)])
                turn(i0 + 2, [(w[:, PAST_LEN:NK], NDEC)])
                wait_rounds(i0 + 3)
                for b in range(4 * half, 4 * half + 4):
                    R = slice(32 * (b % 4), 32 * (b % 4) + 32)
                    pe.wait_ge(v_in[b % NV], 16 * N_PAGES * (b // NV + 1))
                    for j in range(N_PAGES):
                        pe.matmul(ps[R, 2 * half, :], wT[:, j, R], vp[:, b % NV, j, :], start=(j == 0), stop=False)
                    last = pe.matmul(ps[R, 2 * half, :], wT[0:NDEC, 8, R], vn[:, :], start=False, stop=True)
                    last.then_inc(y_mm, 1)
                pe.wait_ge(own_done, half + 1)
                for p in range(4):
                    last = pe.matmul(ps[:, 4 + half, 64 + 16 * p:80 + 16 * p], own[:, p * P:(p + 1) * P], K["rowtoken"][:, :], start=True, stop=True)
                last.then_inc(f_mm, 1)

        @block.scalar
        def _(a):
            A = e.cA

            def logs_of(half):
                z, s = zb[half], sp_[half]
                a.wait_ge(z_done, half + 1)
                A(a, a.activation(s[:, :], z[:, :], ACT.Abs))
                A(a, a.activation(s[:, :], s[:, :], ACT.Exp, scale=-1.0))
                a.activation(s[:, :], s[:, :], ACT.Ln, bias=1.0).then_inc(ln_done, 1)

            def weights_of(half):
                a.wait_ge(r_done, half + 1)
                a.activation(zb[half][:, :], zb[half][:, :], ACT.Exp).then_inc(w_done, 1)

            for i in range(0, NKR, 2):
                take(a, a.copy, i, takeA)
                if i == 4 * 10:
                    logs_of(0)
                if i == 4 * 12 + 2:
                    weights_of(0)
            logs_of(1)
            weights_of(1)
            for half in range(2):
                for i in range(NKR + 3 * half, NKR + 3 * half + 3):
                    if i % 2 == 0:
                        take(a, a.copy, i, takeA)
                a.wait_ge(f_mm, half + 1)
                a.copy(yb[:, :, SEQ + 16 * half:SEQ + 16 * half + 16],
                       ps[:, 4 + half, 64:128].rearrange("p (a t) -> p a t", a=4)).then_inc(f_done, 1)

        @block.vector
        def _(v):
            D = e.cD
            D(v, v.tensor_tensor(own[:, 0:8], e.bias_b[:, :], K["rowhead"][:, :], ALU.mult))
            D(v, v.tensor_reduce(rowbias[:, :], own[:, 0:8], AX_X, ALU.add))
            D(v, v.memset(ones[:, :], 1.0))

            def scores_of(half):
                z = zb[half]
                v.wait_ge(z_mm, 8 * (half + 1))
                v.tensor_scalar(z[:, 0:PAST_LEN], ps[:, 2 * half:2 * half + 2, :].rearrange("p a b -> p (a b)"), rowbias[:, 0:1], None, ALU.add)
                D(v, v.tensor_scalar(z[:, PAST_LEN:NK], ps[:, 4 + half, 0:NDEC], rowbias[:, 0:1], None, ALU.add))
                v.sem_inc(z_done, 1)

            def rests_of(half):
                z, s = zb[half], sp_[half]
                new = slice(32 * half, 32 * half + 32)
                v.wait_ge(ln_done, half + 1)
                D(v, v.scalar_tensor_tensor(s[:, :], z[:, :], 0.0, s[:, :], ALU.max, ALU.add))
                D(v, v.tensor_tensor(s[:, PAST_LEN:NK], s[:, PAST_LEN:NK], K["bnew"][:, new], ALU.mult))
                D(v, v.tensor_tensor_scan(s[:, ::-1], ones[:, :].to_broadcast([P, NK]), s[:, ::-1], 0.0, ALU.mult, ALU.add))
                D(v, v.tensor_tensor(z[:, :], z[:, :], s[:, :], ALU.subtract))
                v.tensor_tensor(z[:, PAST_LEN:NK], z[:, PAST_LEN:NK], K["bnewneg"][:, new], ALU.add).then_inc(r_done, 1)

            for i in range(1, NKR, 2):
                take(v, v.tensor_copy, i, takeD)
                if i == 4 * 9 + 1:
                    scores_of(0)
                if i == 4 * 11 + 1:
                    rests_of(0)
            scores_of(1)
            rests_of(1)
            for half in range(2):
                for i in range(NKR + 3 * half, NKR + 3 * half + 3):
                    if i % 2 == 1:
                        take(v, v.tensor_copy, i, takeD)
                v.wait_ge(y_mm, 4 * (half + 1))
                if half:
                    v.wait_ge(f_mm, 1)
                v.tensor_tensor(own[:, :].rearrange("p (h d) -> p h d", d=HD), ps[:, 2 * half, :].rearrange("p (h d) -> p h d", d=HD),
                                K["rowhead"][:, :].unsqueeze(2).to_broadcast([P, 8, HD]), ALU.mult).then_inc(own_done, 1)
    c2.close()


def stage_windows(nc, c, e):
    yc = e.yc = e.sb("yc", [P, 3, NT])
    ps, K = e.ps, e.K
    G, CH = C_GROUPS, C_HEADS
    kTn = e.sb("ck_new_t", [P, G * 3, NDEC], c=c)
    vn = e.sb("cv_new", [NDEC, G, C_WIDTH], c=c)
    qcb = e.sb("cq_blocks", [P, G, 3, DEC_BATCH, 32], c=c)
    c1 = ExitStack()
    qT, kT = e.sb("cq", [P, G * 3, NT], c=c1), e.sb("ck", [P, G * 3, NT], c=c1)
    cv = e.sb("cv", [P, G, 5, C_WIDTH], c=c1)
    c2 = ExitStack()
    raw = e.sb("c_raw", [P, 5, C_WIDTH], c=c2)
    swp = e.sb("c_swapped", [P, 5, C_WIDTH], c=c2)
    rot = [e.sb(f"c_rot{i}", [P, 5, C_WIDTH], c=c2) for i in range(2)]
    nw = e.sb("c_norm_w", [P, 2, HD], c=c2)
    tab = e.sb("c_tables", [P, 2, 2, 5, HD], c=c2)
    ssq = e.sb("c_ssq", [P, 5 * CH], c=c2)
    nw_in, clr, raw_done, sq_done, ss_done, root, rot_done, rot_sum, t_mm, t_done, v_done, raw_free, k_stored = [
        e.sem("c_" + s) for s in ("norm_in", "clear", "raw", "square", "sumsq", "root", "rot", "rot_sum", "t_mm", "t", "v",
                                  "raw_free", "k_stored")]

    def store_new(sp, g, kv, prompt_src, sample_src):
        stored = None if kv else k_stored
        keep = min(WINDOWS[g], SEQ)
        tiles = keep // P
        d = e.O[f"c{g + 1}_kv_prompt"][e.l, 0][:, kv].rearrange("(i p) h d -> p i (h d)", p=P)
        e.store(sp, d, prompt_src[:, TT - tiles:TT, :], stored)
        rows = e.O[f"c{g + 1}_kv_sample"].shape[2]
        for b in range(DEC_BATCH):
            d = e.O[f"c{g + 1}_kv_sample"][e.l, b][rows - DEC_SEQ:rows, kv].rearrange("t h d -> t (h d)")
            e.store(sp, d, sample_src[4 * b:4 * b + 4, :], stored)

    with nc.Block() as block:
        @block.sync
        def _(sp):
            sp.dma_start(nw[:, 0, :], e.L["c_qnorm"].partition_broadcast(P)).then_inc(nw_in, 16)
            sp.dma_start(nw[:, 1, :], e.L["c_knorm"].partition_broadcast(P)).then_inc(nw_in, 16)
            for g in range(G):
                e.prefetch(sp, f"proj_c{g}")
                sp.wait_ge(rot_done, 2 * g + 2)
                store_new(sp, g, 0, rot[1], rot[1][:, 4, :])
                if g < G - 1:
                    sp.wait_ge(v_done, g + 1)
                    store_new(sp, g, 1, cv[:, g], cv[:, g, 4])
            sp.wait_ge(k_stored, 16 * (1 + DEC_BATCH) * G)

        @block.tensor
        def _(pe):
            def turn(n):
                pe.wait_ge(rot_done, n + 1)
                for i, (t0, m) in enumerate(TOK_TILES):
                    u = 5 * n + i
                    if u >= 2:
                        pe.wait_ge(t_done, u - 1)
                    for j in range(3):
                        last = pe.transpose(ps[:, 4 + u % 2, j * P:j * P + m], rot[n % 2][0:m, i, j * P:(j + 1) * P],
                                            e.ident[0:m, 0:m])
                    last.then_inc(t_mm, 1)

            for g in range(G):
                n0 = PLAN[f"proj_c{g}"][0]
                for which in range(3):
                    for n in (n0 + 2 * which, n0 + 2 * which + 1):
                        e.token_products(pe, e.weights(pe, n), CHUNKS[n][2], e.xnT)
                    if which:
                        turn(2 * g + which - 1)

        @block.scalar
        def _(a):
            a.wait_ge(clr, 1)

            def take_turned(n):
                g, dst = n // 2, (qT, kT)[n % 2]
                for i, (t0, m) in enumerate(TOK_TILES):
                    u = 5 * n + i
                    a.wait_ge(t_mm, u + 1)
                    src = ps[:, 4 + u % 2, 0:3 * P].rearrange("p (j t) -> p j t", j=3)[:, :, 0:m]
                    a.mul(dst[:, 3 * g:3 * g + 3, t0:t0 + m], src, QK_SCALE if n % 2 == 0 else 1.0).then_inc(t_done, 1)

            for g in range(G):
                for which in range(3):
                    n = 2 * g + which
                    if which < 2 and n:
                        a.wait_ge(raw_free, n)
                    for c0, w in ((0, CW), (CW, C_WIDTH - CW)):
                        for i, (t0, m) in enumerate(TOK_TILES):
                            o = e.unit_wait(a)
                            dst = (raw if which < 2 else cv[:, g])[0:m, i, c0:c0 + w]
                            a.copy(dst, o[0:m, 0, 0:w]).then_inc(e.taken(), 1)
                    e.wait_taken(a, e.unit["take"] - 1)
                    if which < 2:
                        a.sem_inc(raw_done, 1)
                        if n:
                            a.wait_ge(rot_sum, n)
                        a.activation(swp[:, :, :], raw[:, :, :], ACT.Square).then_inc(sq_done, 1)
                        a.wait_ge(ss_done, n + 1)
                        a.activation(ssq[:, :], ssq[:, :], ACT.Sqrt).then_inc(root, 1)
                    else:
                        a.sem_inc(v_done, 1)
                    if which:
                        take_turned(2 * g + which - 1)

        @block.vector
        def _(v):
            D = e.cD
            v.memset(raw[:, 4, :], 0.0).then_inc(clr, 1)
            v.wait_ge(nw_in, 32)
            for w in range(2):
                for i in range(5):
                    same = K["rot_same"][:, i * HD:(i + 1) * HD]
                    swap = K["rot_swap"][:, i * HD:(i + 1) * HD]
                    v.tensor_tensor(tab[:, w, 0, i], same, nw[:, w, :], ALU.mult)
                    v.tensor_tensor(tab[:, w, 1, i, 0:32], swap[:, 0:32], nw[:, w, 32:64], ALU.mult)
                    D(v, v.tensor_tensor(tab[:, w, 1, i, 32:64], swap[:, 32:64], nw[:, w, 0:32], ALU.mult))
            for n in range(2 * G):
                w, r = n % 2, rot[n % 2]
                heads = lambda x: x.rearrange("p i (h d) -> p i h d", d=HD)
                v.wait_ge(sq_done, n + 1)
                D(v, v.tensor_reduce(ssq[:, :], swp[:, :, :].rearrange("p i (h d) -> p (i h) d", d=HD), AX_X, ALU.add))
                v.tensor_scalar(ssq[:, :], ssq[:, :], 1.0 / HD, NORM_EPS, ALU.mult, ALU.add).then_inc(ss_done, 1)
                if n >= 2:
                    v.wait_ge(t_mm, 5 * (n - 1))
                    if w == 1:
                        v.wait_ge(k_stored, 16 * (1 + DEC_BATCH) * (n // 2))
                tb = lambda k, lo, hi: tab[:, w, k, :, lo:hi].unsqueeze(2).to_broadcast([P, 5, CH, hi - lo])
                v.tensor_tensor(heads(r[:, :, :]), heads(raw[:, :, :]), tb(0, 0, HD), ALU.mult)
                v.tensor_tensor(heads(swp[:, :, :])[:, :, :, 0:32], heads(raw[:, :, :])[:, :, :, 32:64], tb(1, 0, 32), ALU.mult)
                v.tensor_tensor(heads(swp[:, :, :])[:, :, :, 32:64], heads(raw[:, :, :])[:, :, :, 0:32], tb(1, 32, 64),
                                ALU.mult).then_inc(raw_free, 1)
                v.wait_ge(raw_free, n + 1)
                v.tensor_tensor(r[:, :, :], r[:, :, :], swp[:, :, :], ALU.add).then_inc(rot_sum, 1)
                v.wait_ge(rot_sum, n + 1)
                v.wait_ge(root, n + 1)
                D(v, v.reciprocal(ssq[:, :], ssq[:, :]))
                r3 = r[:, :, :].rearrange("p i (h d) -> p (i h) d", d=HD)
                v.tensor_tensor(r3, r3, ssq[:, :].unsqueeze(2).to_broadcast([P, 5 * CH, HD]), ALU.mult).then_inc(rot_done, 1)
                v.wait_ge(rot_done, n + 1)
    c2.close()

    c2 = ExitStack()
    S = [e.sb(f"cs{i}", [P, 10, P], c=c2) for i in range(2)]
    PT = [e.sb(f"c_pt{i}", [P, 10, P], c=c2) for i in range(2)]
    qz = e.sb("c_q_alone", [P, 2, G, P], c=c2)
    diag = e.sb("c_diag", [P, 2, P], c=c2)
    ones = e.sb("c_ones", [P, HD], c=c2)
    scale = e.sb("c_scale", [P, P], c=c2)
    nmax, den, rden = [e.sb("c_" + n, [P, 2], c=c2) for n in ("nmax", "den", "rden")]
    (q_done, s_mm, s_take, mx_done, p_done, rd_done, dg_done, r_mm, p_take, sc_take, v_take, new_done) = [e.sem("cp_" + s) for s in
        ("q", "s_mm", "s_take", "max", "p", "rden", "diag", "round_mm", "p_take", "scale_take", "v_take", "new")]
    units = [(qt, h) for qt in range(TT) for h in range(CH)]

    def keys(qt):
        return [(1, k) for k in range(qt + 1)] + [(2, k) for k in range(qt + 1)] + [(0, k) for k in range(max(qt - 1, 0), qt + 1)]

    rounds = []
    p_rounds, v_round = {}, {}
    for n in range(len(units) + 1):
        if n < len(units):
            nb = len(keys(units[n][0]))
            p_rounds[n] = range(len(rounds), len(rounds) + (nb + 3) // 4)
            rounds += [("p", n, b, min(4, nb - b)) for b in range(0, nb, 4)]
        if n:
            v_round[n - 1] = len(rounds)
            rounds.append(("v", n - 1, 0, 0))

    def wait_taken(pe, i):
        kind = rounds[i][0]
        pe.wait_ge(p_take if kind == "p" else v_take, sum(x[0] == kind for x in rounds[:i + 1]))

    with nc.Block() as block:
        @block.sync
        def _(sp):
            store_new(sp, G - 1, 1, cv[:, G - 1], cv[:, G - 1, 4])
            e.stores_done(sp)

        @block.tensor
        def _(pe):
            def scores(n):
                qt, h = units[n]
                b0 = 3 * (n % 2)
                pe.wait_ge(q_done, n + 1)
                if n >= 2:
                    pe.wait_ge(s_take, n - 1)
                for bank, g in enumerate((1, 2, 0)):
                    k0 = max(qt - 1, 0) if g == 0 else 0
                    last = pe.matmul(ps[:, b0 + bank, 0:(qt + 1 - k0) * P], qz[:, n % 2, g, :],
                                     kT[:, 3 * g + h // 2, k0 * P:(qt + 1) * P], start=True, stop=True)
                last.then_inc(s_mm, 1)

            def do_round(i):
                kind, n, b, k = rounds[i]
                qt, h = units[n]
                bank = ps[:, 6 + i % 2, :]
                if i >= 2:
                    wait_taken(pe, i - 2)
                if kind == "v":
                    wait_taken(pe, p_rounds[n][-1])
                    kb = keys(qt)
                    R = slice(64 * (h % 2), 64 * (h % 2) + 64)
                    pe.wait_ge(dg_done, n + 1)
                    pe.matmul(bank[R, P:2 * P], ones[:, :], diag[:, n % 2, :], start=True, stop=True)
                    for j, (g, kt) in enumerate(kb):
                        last = pe.matmul(bank[R, 0:P], cv[:, g, kt, h * HD:(h + 1) * HD], PT[n % 2][:, j, :],
                                         start=(j == 0), stop=(j == len(kb) - 1))
                else:
                    for j in range(k):
                        last = pe.transpose(bank[:, j * P:(j + 1) * P], S[n % 2][:, b + j, :], e.ident[:, :])
                last.then_inc(r_mm, 1)

            scores(0)
            scores(1)
            for n in range(len(units) + 1):
                if n + 2 < len(units):
                    scores(n + 2)
                if n < len(units):
                    pe.wait_ge(p_done, n + 1)
                    for i in p_rounds[n]:
                        do_round(i)
                if n:
                    do_round(v_round[n - 1])

        @block.scalar
        def _(a):
            def exponentials(n):
                nb = len(keys(units[n][0]))
                a.wait_ge(mx_done, n + 1)
                if n >= 2:
                    a.wait_ge(rd_done, n - 1)
                a.activation(S[n % 2][:, 0:nb, :], S[n % 2][:, 0:nb, :], ACT.Exp, bias=nmax[:, n % 2:n % 2 + 1],
                             accum_out=den[:, n % 2:n % 2 + 1]).then_inc(p_done, 1)

            exponentials(0)
            for n in range(len(units)):
                for i in p_rounds[n]:
                    _, _, b, k = rounds[i]
                    a.wait_ge(r_mm, i + 1)
                    a.copy(PT[n % 2][:, b:b + k, :], ps[:, 6 + i % 2, 0:k * P].rearrange("p (k t) -> p k t", k=k)).then_inc(p_take, 1)
                if n + 1 < len(units):
                    exponentials(n + 1)

        @block.vector
        def _(v):
            v.memset(ones[:, :], 1.0)

            def for_sample(n):
                if n == 0:
                    v.tensor_copy(kTn[:, :, :], kT[:, :, SEQ:NT])
                    v.tensor_copy(vn[:, :, :], cv[0:NDEC, :, 4, :])
                    v.wait_ge(new_done, 2)
                elif n <= G * 3:
                    g, p = (n - 1) // 3, (n - 1) % 3
                    for hh in range(2):
                        R = slice(64 * hh, 64 * hh + 64)
                        o = (2 * p + hh) * 4
                        v.tensor_copy(qcb[R, g, p, :, o:o + 4], qT[R, 3 * g + p, SEQ:NT].rearrange("p (b t) -> p b t", t=4))

            def maxima(n):
                qt, h = units[n]
                s, b0, nq = S[n % 2], 3 * (n % 2), qt + 1
                v.wait_ge(s_mm, n + 1)
                if n >= 2:
                    v.wait_ge(r_mm, p_rounds[n - 2][-1] + 1)
                cm = K["cmask"][:, :].rearrange("p (k t) -> p k t", t=P)
                blk = lambda bank, k: ps[:, b0 + bank, 0:k * P].rearrange("p (k t) -> p k t", t=P)
                v.tensor_tensor(s[:, 0:nq, :], blk(0, nq), cm[:, 4 - nq:4, :], ALU.add)
                v.tensor_tensor(s[:, nq:2 * nq, :], blk(1, nq), cm[:, 8 - nq:8, :], ALU.add)
                n1 = min(nq, 2)
                v.tensor_tensor(s[:, 2 * nq:2 * nq + n1, :], blk(2, n1), cm[:, 10 - n1:10, :], ALU.add).then_inc(s_take, 1)
                v.wait_ge(s_take, n + 1)
                v.tensor_reduce(nmax[:, n % 2:n % 2 + 1], s[:, 0:2 * nq + n1, :].rearrange("p k t -> p (k t)"), AX_X, ALU.max,
                                negate=True).then_inc(mx_done, 1)

            def outputs(n):
                qt, h = units[n]
                R, bank = slice(64 * (h % 2), 64 * (h % 2) + 64), ps[:, 6 + v_round[n] % 2, :]
                v.wait_ge(r_mm, v_round[n] + 1)
                if n:
                    v.wait_ge(v_take, n)
                v.tensor_copy(scale[R, :], bank[R, P:2 * P]).then_inc(sc_take, 1)
                v.wait_ge(sc_take, n + 1)
                v.tensor_tensor(yc[R, h // 2, qt * P:(qt + 1) * P], bank[R, 0:P], scale[R, :], ALU.mult).then_inc(v_take, 1)

            maxima(0)
            for n in range(len(units)):
                if n + 1 < len(units):
                    maxima(n + 1)
                v.wait_ge(p_done, n + 1)
                v.reciprocal(rden[:, n % 2:n % 2 + 1], den[:, n % 2:n % 2 + 1]).then_inc(rd_done, 1)
                v.wait_ge(rd_done, n + 1)
                if n >= 2:
                    v.wait_ge(r_mm, v_round[n - 2] + 1)
                v.tensor_scalar(diag[:, n % 2, :], e.ident[:, :], rden[:, n % 2:n % 2 + 1], None, ALU.mult).then_inc(dg_done, 1)
                if n:
                    outputs(n - 1)
                for_sample(n)
            outputs(len(units) - 1)

        @block.gpsimd
        def _(g):
            g.memset(qz[:, :, :, :], 0.0).then_inc(new_done, 1)
            g.wait_ge(new_done, 1)
            g.memset(qcb[:, :, :, :, :], 0.0).then_inc(new_done, 1)
            g.wait_ge(new_done, 2)
            for n, (qt, h) in enumerate(units):
                R = slice(64 * (h % 2), 64 * (h % 2) + 64)
                if n >= 2:
                    g.wait_ge(s_mm, n - 1)
                g.tensor_copy(qz[R, n % 2, :, :], qT[R, h // 2:3 * G:3, qt * P:(qt + 1) * P]).then_inc(q_done, 1)
    c2.close()
    c1.close()

    NSLOT = 4
    NK = 896
    c2 = ExitStack()
    slots = [e.sb(f"c_rows{i}", [P, 9, C_WIDTH], c=c2) for i in range(NSLOT)]
    keysT = e.sb("c_keys_t", [P, 3, NK], c=c2)
    Sd = [e.sb(f"c_scores{i}", [P, 992], c=c2) for i in range(2)]
    PTd = e.sb("c_weights_t", [P, 12, P], c=c2)
    st = e.sb("c_stats", [P, 2, 3], c=c2)
    own = e.sb("c_own_head", [P, C_WIDTH], c=c2)
    (k_mm, takeA, takeD, s_mm, mx_done, p_done, n_done, y_mm, own_done, f_mm, f_done) = [e.sem("cd_" + s) for s in
        ("k_mm", "take_a", "take_d", "s_mm", "max", "p", "norm", "y_mm", "own", "f_mm", "f")]
    rows_in = [e.sem(f"cd_rows_in{i}") for i in range(NSLOT)]
    items = [(kv, b) for kv in range(2) for b in range(DEC_BATCH)]
    KR = [("k", 0, None)] + [("k", 1, p) for p in range(3)] + [("k", 2, p) for p in range(3)]
    PR = [("w", 0, (0, 1, P, 0)), ("w", 1, (1, 4, 64, 128)), ("w", 2, (5, 3, NDEC, 384)), ("w", 3, (8, 4, P, 480))]
    drounds = [(r, b) for b in range(DEC_BATCH) for r in KR] + [(r, half) for half in range(2) for r in PR]
    NKR = len(KR)

    def take(eng, copy, i, sem):
        (kind, which, arg), x = drounds[i]
        bank = ps[:, 6 + i % 2, :]
        eng.wait_ge(k_mm, i + 1)
        if kind == "k":
            if x:
                eng.wait_ge(s_mm, x)
            if which == 0:
                copy(keysT[:, :, 0:P], bank[:, 0:3 * P].rearrange("p (j t) -> p j t", j=3)).then_inc(sem, 1)
            elif which == 1:
                copy(keysT[:, arg, 128:640], bank).then_inc(sem, 1)
            else:
                copy(keysT[:, arg, 640:896], bank[:, 0:256]).then_inc(sem, 1)
        else:
            b0, k, m, _ = arg
            if x:
                eng.wait_ge(y_mm, 4)
            copy(PTd[0:m, b0:b0 + k, :], bank[0:m, 0:k * P].rearrange("p (k t) -> p k t", k=k)).then_inc(sem, 1)

    with nc.Block() as block:
        @block.sync
        def _(sp):
            for i, (kv, b) in enumerate(items):
                if i >= NSLOT:
                    last_kv, last_b = items[i - NSLOT]
                    if last_kv:
                        sp.wait_ge(y_mm, last_b + 1)
                    else:
                        sp.wait_ge(k_mm, NKR * (last_b + 1))
                s, sm = slots[i % NSLOT], rows_in[i % NSLOT]
                sp.dma_start(s[:, 0, :], e.L["cache_c1_kv"][b, :, kv].rearrange("r h d -> r (h d)")).then_inc(sm, 16)
                sp.dma_start(s[:, 1:5, :], e.L["cache_c2_kv"][b, :, kv].rearrange("(j r) h d -> j r (h d)", r=4)).then_inc(sm, 16)
                sp.dma_start(s[0:64, 5:9, :], e.L["cache_c3_kv"][b, :, kv].rearrange("(j r) h d -> j r (h d)", r=16)[:, 0:4]).then_inc(sm, 16)

        @block.tensor
        def _(pe):
            def wait_bank(i):
                if i >= 2:
                    pe.wait_ge((takeA, takeD)[i % 2], i // 2)

            def wait_rounds(n):
                pe.wait_ge(takeA, (n + 1) // 2)
                pe.wait_ge(takeD, n // 2)

            for b in range(DEC_BATCH):
                s = slots[b % NSLOT]
                pe.wait_ge(rows_in[b % NSLOT], 48 * (b // NSLOT + 1))
                for r, (_, which, p) in enumerate(KR):
                    i = NKR * b + r
                    wait_bank(i)
                    o = ps[:, 6 + i % 2, :]
                    if which == 0:
                        for j in range(3):
                            last = pe.transpose(o[:, j * P:(j + 1) * P], s[:, 0, j * P:(j + 1) * P], e.ident[:, :])
                    elif which == 1:
                        for j in range(4):
                            last = pe.transpose(o[:, j * P:(j + 1) * P], s[:, 1 + j, p * P:(p + 1) * P], e.ident[:, :])
                    else:
                        for j in range(4):
                            last = pe.transpose(o[:, j * 64:(j + 1) * 64], s[0:64, 5 + j, p * P:(p + 1) * P], e.ident[0:64, 0:64])
                    last.then_inc(k_mm, 1)
                wait_rounds(NKR * (b + 1))
                R, half = slice(32 * (b % 4), 32 * (b % 4) + 32), b // 4
                for bank, c0, w, g, k0 in [(0, 0, P, 0, 0), (0, 128, 256, 2, 640), (1, 0, 512, 1, 128)] + [
                        (0, 384 + 32 * g, 32, g, None) for g in range(3)]:
                    for p in range(3):
                        x = keysT[:, p, k0:k0 + w] if k0 is not None else kTn[:, 3 * g + p, :]
                        last = pe.matmul(ps[R, 2 * half + bank, c0:c0 + w], qcb[:, g, p, b, :], x, start=(p == 0), stop=(p == 2))
                last.then_inc(s_mm, 1)
            for half in range(2):
                pe.wait_ge(n_done, half + 1)
                for r, (_, _, (b0, k, m, c0)) in enumerate(PR):
                    i = NKR * DEC_BATCH + 4 * half + r
                    wait_bank(i)
                    for j in range(k):
                        last = pe.transpose(ps[0:m, 6 + i % 2, j * P:(j + 1) * P], Sd[half][:, c0 + j * m:c0 + (j + 1) * m], e.ident[:, :])
                    last.then_inc(k_mm, 1)
                wait_rounds(NKR * DEC_BATCH + 4 * (half + 1))
                for b in range(4 * half, 4 * half + 4):
                    i = DEC_BATCH + b
                    s = slots[i % NSLOT]
                    pe.wait_ge(rows_in[i % NSLOT], 48 * (i // NSLOT + 1))
                    R = slice(32 * (b % 4), 32 * (b % 4) + 32)
                    o = ps[R, 4 + half, 0:C_WIDTH]
                    pe.matmul(o, PTd[:, 0, R], s[:, 0, :], start=True, stop=False)
                    for j in range(4):
                        pe.matmul(o, PTd[:, 8 + j, R], s[:, 1 + j, :], start=False, stop=False)
                    for j in range(4):
                        pe.matmul(o, PTd[0:64, 1 + j, R], s[0:64, 5 + j, :], start=False, stop=False)
                    for g in range(3):
                        last = pe.matmul(o, PTd[0:NDEC, 5 + g, R], vn[:, g, :], start=False, stop=(g == 2))
                    last.then_inc(y_mm, 1)
                pe.wait_ge(own_done, half + 1)
                for p in range(3):
                    last = pe.matmul(ps[:, 2 * half, 16 * p:16 * p + 16], own[:, p * P:(p + 1) * P], K["rowtoken"][:, :], start=True, stop=True)
                last.then_inc(f_mm, 1)

        K0 = NKR * DEC_BATCH

        @block.scalar
        def _(a):
            for i in range(0, K0, 2):
                take(a, a.copy, i, takeA)
                if i == 42 or i == 54:
                    half = 0 if i == 42 else 1
                    a.wait_ge(mx_done, half + 1)
                    a.activation(Sd[half][:, :], Sd[half][:, :], ACT.Exp, bias=st[:, half, 0:1], accum_out=st[:, half, 1:2]).then_inc(p_done, 1)
            for half in range(2):
                for i in range(K0 + 4 * half, K0 + 4 * half + 4, 2):
                    take(a, a.copy, i, takeA)
                a.wait_ge(f_mm, half + 1)
                a.copy(yc[:, :, SEQ + 16 * half:SEQ + 16 * half + 16],
                       ps[:, 2 * half, 0:48].rearrange("p (a t) -> p a t", a=3)).then_inc(f_done, 1)

        @block.vector
        def _(v):
            D = e.cD

            def maxima(half):
                s = Sd[half]
                v.wait_ge(s_mm, 4 * (half + 1))
                v.tensor_tensor(s[:, 0:384], ps[:, 2 * half, 0:384], K["dmask"][:, :], ALU.add)
                v.tensor_tensor(s[:, 384:480], ps[:, 2 * half, 384:480], K["dnew"][:, 96 * half:96 * half + 96], ALU.add)
                D(v, v.tensor_tensor(s[:, 480:992], ps[:, 2 * half + 1, :], K["dmask2"][:, :], ALU.add))
                v.tensor_reduce(st[:, half, 0:1], s[:, :], AX_X, ALU.max, negate=True).then_inc(mx_done, 1)

            def normalise(half):
                v.wait_ge(p_done, half + 1)
                D(v, v.reciprocal(st[:, half, 2:3], st[:, half, 1:2]))
                v.tensor_scalar(Sd[half][:, :], Sd[half][:, :], st[:, half, 2:3], None, ALU.mult).then_inc(n_done, 1)

            for i in range(1, K0, 2):
                if i == 31:
                    maxima(0)
                take(v, v.tensor_copy, i, takeD)
            maxima(1)
            for half in range(2):
                normalise(half)
                for i in range(K0 + 4 * half + 1, K0 + 4 * half + 4, 2):
                    take(v, v.tensor_copy, i, takeD)
                v.wait_ge(y_mm, 4 * (half + 1))
                if half:
                    v.wait_ge(f_mm, 1)
                v.tensor_tensor(own[:, :].rearrange("p (h d) -> p h d", d=HD), ps[:, 4 + half, 0:C_WIDTH].rearrange("p (h d) -> p h d", d=HD),
                                K["rowhead"][:, 0:CH].unsqueeze(2).to_broadcast([P, CH, HD]), ALU.mult).then_inc(own_done, 1)
    c2.close()


def stage_output(nc, c, e):
    ps = e.ps
    branches = [(e.ya, 4), (e.yb, 4), (e.yc, 3)]
    merged = e.sb("merged", [P, KT, NT], c=c)
    xres = e.sb("x_res", [P, 5, D_MODEL], c=c)
    gate = e.sb("gate", [P, 2, NT], c=c)
    tmp = e.sb("tmp", [P, 2, NT], c=c)
    x_in, gated, merge_done = [e.sem("o_" + s) for s in ("x_in", "gated", "merged")]
    halves = lambda x: x.rearrange("p (h t) -> p h t", h=2)
    unit = e.unit
    u0 = unit["take"]
    a0, a1 = PLAN["merge"]
    split = e.Split(list(range(*PLAN["gate"])) + list(range(a0, a1, 2)) + list(range(*PLAN["out"])), c)
    with nc.Block() as block:
        @block.sync
        def _(sp):
            for i, (t0, m) in enumerate(TOK_TILES):
                sp.dma_start(xres[0:m, i, :], e.y_rows[i]).then_inc(x_in, 16)
            for s in ("gate", "merge", "out"):
                e.prefetch(sp, s)
            for i, (t0, m) in enumerate(TOK_TILES):
                e.wait_taken(sp, u0 + 11 + 48 + 15 + i)
                e.store(sp, e.y_rows[i], xres[0:m, i, :])
            e.stores_done(sp)

        @block.tensor
        def _(pe):
            for n in range(*PLAN["gate"]):
                split.channel_products(pe, n)
            pe.wait_ge(gated, 11)
            for n in range(a0, a1):
                i = (n - a0) % 6
                if i % 2:
                    e.channel_products(pe, e.weights(pe, n), CW, CHUNKS[n][3], branches[i // 2][0])
                else:
                    split.channel_products(pe, n)
            split.x_times = 2
            for n in range(*PLAN["out"]):
                split.token_products(pe, n)

        @block.scalar
        def _(a):
            def take(u, func):
                a.wait_ge(e.products_done, u + 1)
                a.activation(halves(gate[:, u % 2]), e.pair(u)[:, :, 0:HALF], func).then_inc(e.products_taken[u % 2], 1)

            split.weights_hi(a, 0)
            split.tokens_hi(a, e.xnT)
            split.weights_hi(a, 1)
            for j in range(11):
                if j >= 2:
                    a.wait_ge(gated, j - 1)
                take(u0 + j, ACT.Silu)
                if j % 2 or j == 10:
                    split.weights_hi(a, j // 2 + 2)
            a.wait_ge(gated, 11)
            for n in range(12):
                u = u0 + 11 + 4 * n
                take(u, ACT.Sigmoid)
                take(u + 1, ACT.Sigmoid)
                split.weights_hi(a, 6 + n + 2)
            a.wait_ge(e.products_done, UNITS_AFTER[a1 - 2])
            for k in range(KT):
                a.wait_ge(merge_done, k + 1)
                a.copy(split.x[0][:, k, :], merged[:, k, :]).then_inc(split.x_hi, 1)
            for i in range(20, 22):
                split.weights_hi(a, i)

        @block.vector
        def _(v):
            D = e.cD
            split.weights_lo(v, 0)
            split.tokens_lo(v, e.xnT)
            split.weights_lo(v, 1)
            for j in range(11):
                u = u0 + j
                y = (e.ya[:, j] if j < 4 else e.yb[:, j - 4] if j < 8 else e.yc[:, j - 8])
                v.wait_ge(e.products_taken[u % 2], u // 2 + 1)
                v.tensor_tensor(y, y, gate[:, u % 2], ALU.mult).then_inc(gated, 1)
                if j % 2 or j == 10:
                    split.weights_lo(v, j // 2 + 2)
            u = u0 + 11
            for jj in range(4):
                for i in range(3):
                    for s in range(2):
                        m = merged[:, 2 * jj + s]
                        b = u + 2 + s
                        v.wait_ge(e.products_taken[(u + s) % 2], (u + s) // 2 + 1)
                        v.wait_ge(e.products_done, b + 1)
                        dst = m if i == 0 else tmp[:, s]
                        v.tensor_tensor(halves(dst), e.pair(b)[:, :, 0:HALF], halves(gate[:, b % 2]), ALU.mult).then_inc(e.products_taken[b % 2], 1)
                        if i:
                            v.wait_ge(e.products_taken[b % 2], b // 2 + 1)
                            ins = v.tensor_tensor(m, m, tmp[:, s], ALU.add)
                            if i == 2:
                                ins.then_inc(merge_done, 1)
                            else:
                                D(v, ins)
                    u += 4
                    split.weights_lo(v, 6 + 3 * jj + i + 2)
            v.wait_ge(merge_done, 8)
            split.tokens_lo(v, merged, 1)
            v.wait_ge(x_in, 16 * 5)
            for q in range(D_MODEL // CW):
                for i, (t0, m) in enumerate(TOK_TILES):
                    v.wait_ge(e.products_done, u + 1)
                    xr = xres[0:m, i, q * CW:(q + 1) * CW]
                    v.tensor_tensor(xr, xr, e.pair(u)[0:m, 0, 0:CW], ALU.add).then_inc(e.products_taken[u % 2], 1)
                    u += 1
                split.weights_lo(v, 20 + q)
            unit["take"] = u


STAGES = [stage_norm, stage_rwkv, stage_stick_breaking, stage_windows, stage_output]


_INS = ['x_prompt', 'x_sample', 'state_a_wkv', 'state_a_shift', 'cache_b_k', 'cache_b_v', 'cache_c1_kv', 'cache_c2_kv',
        'cache_c3_kv', 'page_table', 'norm_w', 'w_in', 'a_mu', 'a_w0', 'a_w2', 'a_a0', 'a_a2', 'a_kk', 'a_ka', 'a_rk',
        'a_gn_w', 'a_gn_b', 'b_bias', 'c_qnorm', 'c_knorm', 'w_br_a', 'w_br_b', 'w_br_c', 'w_out']
_OUTS = [('y_prompt', (1, 512, 1024)), ('y_sample', (8, 4, 1024)), ('a_wkv_prompt', (2, 1, 8, 64, 64)),
         ('a_wkv_sample', (2, 8, 8, 64, 64)), ('a_shift_prompt', (2, 1, 1664)), ('a_shift_sample', (2, 8, 1664)),
         ('b_k_prompt', (2, 1, 512, 8, 64)), ('b_v_prompt', (2, 1, 512, 8, 64)), ('b_k_sample', (2, 8, 4, 8, 64)),
         ('b_v_sample', (2, 8, 4, 8, 64)), ('c1_kv_prompt', (2, 1, 128, 2, 6, 64)), ('c1_kv_sample', (2, 8, 128, 2, 6, 64)),
         ('c2_kv_prompt', (2, 1, 512, 2, 6, 64)), ('c2_kv_sample', (2, 8, 512, 2, 6, 64)),
         ('c3_kv_prompt', (2, 1, 512, 2, 6, 64)), ('c3_kv_sample', (2, 8, 1028, 2, 6, 64))]


def kernel(**inputs):
    import numpy as _np
    import concourse.bacc as _bacc
    from concourse import mybir as _mybir
    from concourse.bass_utils import run_bass_kernel_spmd as _run

    nc = _bacc.Bacc("TRN2", target_bir_lowering=False, num_devices=1)
    arrays, ins, outs = {}, {}, {}
    for name in _INS:
        a = _np.ascontiguousarray(inputs[name])
        arrays[f"in_{name}_dram"] = a
        ins[name] = nc.dram_tensor(f"in_{name}_dram", a.shape, _mybir.dt.from_np(a.dtype), kind="ExternalInput").ap()
    for name, a in host_constants().items():
        arrays[f"const_{name}_dram"] = a
        ins[name] = nc.dram_tensor(f"const_{name}_dram", a.shape, _mybir.dt.from_np(a.dtype), kind="ExternalInput").ap()
    for name, shape in _OUTS:
        outs[name] = nc.dram_tensor(f"out_{name}_dram", shape, F32, kind="ExternalOutput").ap()
    build(nc, ins, outs)
    r = _run(nc, [arrays], core_ids=[0])
    return tuple(r.results[0][f"out_{name}_dram"] for name, _ in _OUTS)
```
